# Optimizing a Trainium2 kernel written in Bass

```python
import math
import jax
import jax.numpy as jnp
from jax import lax
import numpy as np
import jax, jax.numpy as jnp

D_MODEL = 1024
BATCH = 1
SEQ = 512
DEPTH = 1

MEM_LEN = 256
MIX_W = 512
N_BRANCH = 3
CONV_K = 3
SB_HEADS = 8
SB_HEAD_DIM = MIX_W // SB_HEADS
SB_BLOCK = 128
RWKV_HEADS = 8
RWKV_HEAD = MIX_W // RWKV_HEADS
DECAY_LORA = 64
ICLR_LORA = 64
GATE_LORA = 128
VRES_LORA = 32
DECAY_SCALE = math.exp(-0.5)
CA_HEADS = 4
CA_HEAD_DIM = D_MODEL // CA_HEADS
FFN_DIM = 2816
FFN_CONV_K = 3
RMS_EPS = 1e-6
GN_EPS = 64e-5

CONV_COLS = 3 * MIX_W
SB_COLS = 3 * MIX_W
GATE_COLS = N_BRANCH * D_MODEL
RWKV_COLS = 3 * MIX_W + DECAY_LORA + ICLR_LORA + GATE_LORA
COMB_COLS = CONV_COLS + SB_COLS + GATE_COLS + RWKV_COLS
OFF_SB = CONV_COLS
OFF_GATE = OFF_SB + SB_COLS
OFF_RWKV = OFF_GATE + GATE_COLS


def rms_norm(x, g):
    xf = x.astype(jnp.float32)
    y = xf * lax.rsqrt(jnp.mean(xf * xf, axis=-1, keepdims=True) + RMS_EPS)
    return (y * g.astype(jnp.float32)).astype(x.dtype)

def causal_dwconv(x, w):
    c = x.shape[-1]
    return lax.conv_general_dilated(
        x, w[:, None, :].astype(x.dtype), window_strides=(1,),
        padding=[(w.shape[0] - 1, 0)], dimension_numbers=("NWC", "WIO", "NWC"),
        feature_group_count=c)

def stick_breaking_attention(q, k, v):
    s_len, dh = q.shape[2], q.shape[3]
    scale = dh ** -0.5
    outs = []
    for i in range(s_len // SB_BLOCK):
        start, end = i * SB_BLOCK, (i + 1) * SB_BLOCK
        q_blk = q[:, :, start:end]
        k_blk, v_blk = k[:, :, :end], v[:, :, :end]
        z = jnp.einsum("bhqd,bhkd->bhqk", q_blk, k_blk).astype(jnp.float32) * scale
        q_pos = start + jnp.arange(SB_BLOCK)
        k_pos = jnp.arange(end)
        mask = k_pos[None, :] < q_pos[:, None]
        log_not = jnp.where(mask, jax.nn.log_sigmoid(-z), 0.0)
        suffix = lax.cumsum(log_not, axis=3, reverse=True) - log_not
        log_w = jax.nn.log_sigmoid(z) + suffix
        att = jnp.where(mask, jnp.exp(log_w), 0.0)
        outs.append(jnp.einsum("bhqk,bhkd->bhqd", att.astype(v.dtype), v_blk))
    return jnp.concatenate(outs, axis=2)

def rwkv7_time_mix(p, mu, w0, w_lora, a0, a_lora, g_lora, k_k, k_a, r_k, lnx_w, lnx_b,
                   v_first, v0, v_lora):
    b, s, _ = p.shape
    f32 = jnp.float32
    p = p.astype(f32)
    prev = jnp.pad(p, ((0, 0), (1, 0), (0, 0)))[:, :-1]
    p = p + mu.astype(f32) * (prev - p)
    w_ = MIX_W
    r, k, v = p[..., :w_], p[..., w_:2 * w_], p[..., 2 * w_:3 * w_]
    o = 3 * w_
    xw = p[..., o:o + DECAY_LORA]; o += DECAY_LORA
    xa = p[..., o:o + ICLR_LORA]; o += ICLR_LORA
    xg = p[..., o:o + GATE_LORA]; o += GATE_LORA
    log_decay = -DECAY_SCALE * jax.nn.sigmoid(w0 + jnp.tanh(xw) @ w_lora)
    a = jax.nn.sigmoid(a0 + xa @ a_lora)
    if v0 is None:
        v_first = v
    else:
        xv = p[..., o:o + VRES_LORA]
        v = v + (v_first - v) * jax.nn.sigmoid(v0 + xv @ v_lora)
    g = jax.nn.sigmoid(xg) @ g_lora

    def heads(t):
        return t.reshape(b, s, RWKV_HEADS, RWKV_HEAD)

    kk = heads(k * k_k)
    kk = kk / jnp.maximum(jnp.linalg.norm(kk, axis=-1, keepdims=True), 1e-12)
    k = k * (1.0 + (a - 1.0) * k_a)
    rh, kh, vh, ah, wh = heads(r), heads(k), heads(v), heads(a), heads(jnp.exp(log_decay))

    def step(state, inp):
        r_t, w_t, k_t, v_t, kk_t, a_t = inp
        sa = jnp.einsum("bhvk,bhk->bhv", state, kk_t)
        state = (state * w_t[:, :, None, :]
                 - sa[..., None] * (kk_t * a_t)[:, :, None, :]
                 + v_t[..., None] * k_t[:, :, None, :])
        return state, jnp.einsum("bhvk,bhk->bhv", state, r_t)

    xs = tuple(jnp.moveaxis(t, 1, 0) for t in (rh, wh, kh, vh, kk, ah))
    state0 = jnp.zeros((b, RWKV_HEADS, RWKV_HEAD, RWKV_HEAD), f32)
    _, out = lax.scan(step, state0, xs)
    out = jnp.moveaxis(out, 0, 1)
    mean = jnp.mean(out, axis=-1, keepdims=True)
    var = jnp.mean(jnp.square(out - mean), axis=-1, keepdims=True)
    out = ((out - mean) * lax.rsqrt(var + GN_EPS)).reshape(b, s, w_) * lnx_w + lnx_b
    bonus = (jnp.sum(rh * kh * r_k, axis=-1, keepdims=True) * vh).reshape(b, s, w_)
    return (out + bonus) * g, v_first

def hybrid_token_mixer(xn, w_comb, conv_w, mu_rwkv, w0, w_lora, a0, a_lora, g_lora, k_k, k_a,
                       r_k, lnx_w, lnx_b, branch_proj, gate_b, w_mix_out, v_first, vres):
    b, s, _ = xn.shape
    mu = mu_rwkv
    v0 = v_lora = None
    if vres is not None:
        w_vres, mu_vres, v0, v_lora = vres
        w_comb = jnp.concatenate([w_comb, w_vres], axis=1)
        mu = jnp.concatenate([mu_rwkv, mu_vres], axis=0)
    proj = xn @ w_comb

    c_b, c_c, c_x = jnp.split(proj[..., :OFF_SB], 3, axis=-1)
    y_conv = c_b * causal_dwconv(c_c * c_x, conv_w)

    q, k, v = jnp.split(proj[..., OFF_SB:OFF_GATE], 3, axis=-1)

    def to_heads(t):
        return t.reshape(b, s, SB_HEADS, SB_HEAD_DIM).transpose(0, 2, 1, 3)

    y_sb = stick_breaking_attention(to_heads(q), to_heads(k), to_heads(v))
    y_sb = y_sb.transpose(0, 2, 1, 3).reshape(b, s, MIX_W)

    y_rwkv, v_first = rwkv7_time_mix(proj[..., OFF_RWKV:], mu, w0, w_lora, a0, a_lora, g_lora,
                                     k_k, k_a, r_k, lnx_w, lnx_b, v_first, v0, v_lora)

    gates = jax.nn.sigmoid(
        proj[..., OFF_GATE:OFF_RWKV].reshape(b, s, N_BRANCH, D_MODEL).astype(jnp.float32)
        + gate_b).astype(xn.dtype)
    ys = jnp.stack([y_conv.astype(xn.dtype), y_sb.astype(xn.dtype), y_rwkv.astype(xn.dtype)],
                   axis=2)
    branches = jnp.einsum("bsnc,ncd->bsnd", ys, branch_proj)
    merged = jnp.einsum("bsnd,bsnd->bsd", gates, branches)
    return merged @ w_mix_out, v_first

def memory_cross_attention(hn, mem_n, wq, wkv, wo):
    b, s, _ = hn.shape
    m = mem_n.shape[1]
    q = (hn @ wq).reshape(b, s, CA_HEADS, CA_HEAD_DIM)
    k, v = jnp.split(mem_n @ wkv, 2, axis=-1)
    k = k.reshape(b, m, CA_HEADS, CA_HEAD_DIM)
    v = v.reshape(b, m, CA_HEADS, CA_HEAD_DIM)
    scores = jnp.einsum("bshd,bmhd->bhsm", q, k).astype(jnp.float32) * (CA_HEAD_DIM ** -0.5)
    probs = jax.nn.softmax(scores, axis=-1).astype(v.dtype)
    out = jnp.einsum("bhsm,bmhd->bshd", probs, v).reshape(b, s, D_MODEL)
    return out @ wo

def conv_ffn(hn, w_up, conv_w, conv_b, w_down):
    u = causal_dwconv(hn @ w_up, conv_w) + conv_b
    gate, val = jnp.split(u, 2, axis=-1)
    return (jax.nn.silu(gate) * val) @ w_down

def first_inputs(seed: int = 0) -> dict:
    key = jax.random.key(seed)
    ks = iter(jax.random.split(key, 48))

    def nrm(shape, scale):
        return jax.random.normal(next(ks), shape, jnp.float32) * scale

    def gain(shape):
        return 1.0 + nrm(shape, 0.02)

    L, Lv, D, W, F = DEPTH, DEPTH - 1, D_MODEL, MIX_W, FFN_DIM
    return {
        "x": nrm((BATCH, SEQ, D), 1.0),
        "mem": nrm((BATCH, MEM_LEN, D), 1.0),
        "norm_mix": gain((L, D)),
        "w_comb": nrm((L, D, COMB_COLS), D ** -0.5),
        "conv_w": nrm((L, CONV_K, W), 0.5),
        "mu_rwkv": jax.random.uniform(next(ks), (L, RWKV_COLS), jnp.float32),
        "w0": 0.5 + nrm((L, W), 0.5),
        "w_lora": nrm((L, DECAY_LORA, W), 0.1),
        "a0": nrm((L, W), 0.3),
        "a_lora": nrm((L, ICLR_LORA, W), 0.1),
        "g_lora": nrm((L, GATE_LORA, W), GATE_LORA ** -0.5),
        "k_k": 1.0 + nrm((L, W), 0.1),
        "k_a": 1.0 + nrm((L, W), 0.1),
        "r_k": nrm((L, RWKV_HEADS, RWKV_HEAD), 0.1),
        "lnx_w": gain((L, W)),
        "lnx_b": nrm((L, W), 0.02),
        "w_vres": nrm((Lv, D, VRES_LORA), D ** -0.5),
        "mu_vres": jax.random.uniform(next(ks), (Lv, VRES_LORA), jnp.float32),
        "v0": nrm((Lv, W), 0.3),
        "v_lora": nrm((Lv, VRES_LORA, W), 0.1),
        "branch_proj": nrm((L, N_BRANCH, W, D), W ** -0.5),
        "gate_b": nrm((L, N_BRANCH, D), 0.01),
        "w_mix_out": nrm((L, D, D), D ** -0.5),
        "norm_ca": gain((L, D)),
        "norm_mem": gain((L, D)),
        "ca_wq": nrm((L, D, D), D ** -0.5),
        "ca_wkv": nrm((L, D, 2 * D), D ** -0.5),
        "ca_wo": nrm((L, D, D), D ** -0.5),
        "norm_ffn": gain((L, D)),
        "ffn_up": nrm((L, D, 2 * F), D ** -0.5),
        "ffn_conv_w": nrm((L, FFN_CONV_K, 2 * F), 0.5),
        "ffn_conv_b": nrm((L, 2 * F), 0.02),
        "ffn_down": nrm((L, F, D), F ** -0.5),
        "norm_final": gain((D,)),
    }

def first_block(x, mem, norm_mix, w_comb, conv_w, mu_rwkv, w0, w_lora, a0, a_lora, g_lora, k_k,
              k_a, r_k, lnx_w, lnx_b, w_vres, mu_vres, v0, v_lora, branch_proj, gate_b,
              w_mix_out, norm_ca, norm_mem, ca_wq, ca_wkv, ca_wo, norm_ffn, ffn_up, ffn_conv_w,
              ffn_conv_b, ffn_down, norm_final):
    h = x
    v_first = None
    for l in range(DEPTH):
        vres = None if l == 0 else (w_vres[l - 1], mu_vres[l - 1], v0[l - 1], v_lora[l - 1])
        mix, v_first = hybrid_token_mixer(
            rms_norm(h, norm_mix[l]), w_comb[l], conv_w[l], mu_rwkv[l], w0[l], w_lora[l], a0[l],
            a_lora[l], g_lora[l], k_k[l], k_a[l], r_k[l], lnx_w[l], lnx_b[l], branch_proj[l],
            gate_b[l], w_mix_out[l], v_first, vres)
        h = h + mix
        h = h + memory_cross_attention(rms_norm(h, norm_ca[l]), rms_norm(mem, norm_mem[l]),
                                       ca_wq[l], ca_wkv[l], ca_wo[l])
        h = h + conv_ffn(rms_norm(h, norm_ffn[l]), ffn_up[l], ffn_conv_w[l], ffn_conv_b[l],
                         ffn_down[l])
    return rms_norm(h, norm_final)


HEAD_DIM = 64
FOX_HEADS = 8
NSA_HEADS = 8
NSA_KV_GROUPS = 2
NSA_REP = NSA_HEADS // NSA_KV_GROUPS
CMP_BLOCK = 32
CMP_STRIDE = 16
CMP_HIDDEN = 256
SLC_BLOCK = 64
SLC_TOPK = 16
WINDOW = 512
Q_BLOCK = 128
REL_BUCKETS = 32
REL_MAX_DIST = 128
D_FF = 4 * D_MODEL
NEG_INF = -1e30
FORCED_SCORE = 1e4
SCALE = HEAD_DIM ** -0.5

FOX_W = FOX_HEADS * HEAD_DIM
NSA_W = NSA_HEADS * HEAD_DIM
KV_W = NSA_KV_GROUPS * HEAD_DIM
IN_SPLITS = (FOX_W, FOX_W, FOX_W, FOX_HEADS,
             NSA_W, KV_W, KV_W, KV_W, KV_W, KV_W, KV_W, 3 * NSA_HEADS,
             D_MODEL, D_MODEL)
IN_WIDTH = sum(IN_SPLITS)


def rms_norm_2(x, g):
    xf = x.astype(jnp.float32)
    y = xf * lax.rsqrt(jnp.mean(xf * xf, axis=-1, keepdims=True) + RMS_EPS)
    return (y * g.astype(jnp.float32)).astype(x.dtype)

def masked_softmax(s, mask):
    p = jax.nn.softmax(jnp.where(mask, s, NEG_INF), axis=-1)
    return jnp.where(mask, p, 0.0)

def rel_bucket(dist):
    n = jnp.maximum(dist, 0)
    exact = REL_BUCKETS // 2
    nf = jnp.maximum(n, exact).astype(jnp.float32)
    log_b = exact + (jnp.log(nf / exact) / math.log(REL_MAX_DIST / exact)
                     * (REL_BUCKETS - exact)).astype(jnp.int32)
    return jnp.where(n < exact, n, jnp.minimum(log_b, REL_BUCKETS - 1))

def fox_attention(q, k, v, f_logit, b_f):
    B, T, H, DH = q.shape
    nb = T // Q_BLOCK
    log_f = jax.nn.log_sigmoid(f_logit.astype(jnp.float32) + b_f.astype(jnp.float32))
    c = jnp.cumsum(log_f, axis=1).transpose(0, 2, 1)
    qb = q.reshape(B, nb, Q_BLOCK, H, DH).transpose(1, 0, 3, 2, 4)
    cqb = c.reshape(B, H, nb, Q_BLOCK).transpose(2, 0, 1, 3)
    kpos = jnp.arange(T)

    def block(args):
        i, qi, ci = args
        qpos = i * Q_BLOCK + jnp.arange(Q_BLOCK)
        s = jnp.einsum('bhqd,bkhd->bhqk', qi, k).astype(jnp.float32) * SCALE
        s = s + ci[..., None] - c[:, :, None, :]
        p = masked_softmax(s, kpos[None, :] <= qpos[:, None])
        return jnp.einsum('bhqk,bkhd->bqhd', p.astype(v.dtype), v)

    o = lax.map(block, (jnp.arange(nb), qb, cqb))
    return o.transpose(1, 0, 2, 3, 4).reshape(B, T, H * DH)

def compress_blocks(kv, pe, w1, w2):
    B, T, G, DH = kv.shape
    nc = (T - CMP_BLOCK) // CMP_STRIDE + 1
    idx = np.arange(nc)[:, None] * CMP_STRIDE + np.arange(CMP_BLOCK)[None, :]
    blk = kv[:, idx] + pe[:, None, :]
    blk = blk.transpose(0, 3, 1, 2, 4).reshape(B, G, nc, CMP_BLOCK * DH)
    return jax.nn.silu(blk @ w1) @ w2

def nsa_attention(q, k_cmp, v_cmp, k_slc, v_slc, k_win, v_win, gate_logit, rel_table,
                  pe_k, w1_k, w2_k, pe_v, w1_v, w2_v):
    B, T, H, DH = q.shape
    G, R = NSA_KV_GROUPS, NSA_REP
    nb = T // Q_BLOCK
    nc = (T - CMP_BLOCK) // CMP_STRIDE + 1
    ns = T // SLC_BLOCK
    n_sel = min(SLC_TOPK, ns)

    kc = compress_blocks(k_cmp, pe_k, w1_k, w2_k)
    vc = compress_blocks(v_cmp, pe_v, w1_v, w2_v)
    cmp_start = np.arange(nc) * CMP_STRIDE
    cmp_end = jnp.asarray(cmp_start + CMP_BLOCK - 1, dtype=jnp.int32)
    slc_start = np.arange(ns) * SLC_BLOCK
    overlap = jnp.asarray(((cmp_start[:, None] < slc_start[None, :] + SLC_BLOCK)
                           & (cmp_start[:, None] + CMP_BLOCK > slc_start[None, :])).astype(np.float32))

    tbl_heads = rel_table.T
    tbl_grp = tbl_heads.reshape(G, R, REL_BUCKETS)
    g_idx = jnp.arange(G)[None, :, None, None, None]
    r_idx = jnp.arange(R)[None, None, :, None, None]

    ks = k_slc.transpose(0, 2, 1, 3).reshape(B, G, ns, SLC_BLOCK, DH)
    vs = v_slc.transpose(0, 2, 1, 3).reshape(B, G, ns, SLC_BLOCK, DH)
    pad = ((0, 0), (0, 0), (WINDOW, 0), (0, 0))
    kwp = jnp.pad(k_win.transpose(0, 2, 1, 3), pad)
    vwp = jnp.pad(v_win.transpose(0, 2, 1, 3), pad)
    win_dist = jnp.asarray(np.arange(Q_BLOCK)[:, None] + WINDOW - np.arange(Q_BLOCK + WINDOW)[None, :],
                           dtype=jnp.int32)
    bias_win = tbl_heads[:, rel_bucket(win_dist)].reshape(G, R, Q_BLOCK, Q_BLOCK + WINDOW)

    qb = q.reshape(B, nb, Q_BLOCK, G, R, DH).transpose(1, 0, 3, 4, 2, 5)
    b_idx = jnp.arange(B)[:, None, None, None]
    gk_idx = jnp.arange(G)[None, :, None, None]
    j = jnp.arange(ns)

    def block(args):
        i, qi = args
        qpos = i * Q_BLOCK + jnp.arange(Q_BLOCK)
        s = jnp.einsum('bgrqd,bgcd->bgrqc', qi, kc).astype(jnp.float32) * SCALE
        bias = tbl_heads[:, rel_bucket(qpos[:, None] - cmp_end[None, :])].reshape(G, R, Q_BLOCK, nc)
        p_cmp = masked_softmax(s + bias, cmp_end[None, :] <= qpos[:, None])
        o_cmp = jnp.einsum('bgrqc,bgcd->bgrqd', p_cmp.astype(vc.dtype), vc)
        imp = jnp.einsum('bgrqc,cs->bgqs', p_cmp, overlap)
        cur = qpos // SLC_BLOCK
        forced = (j[None, :] == 0) | (j[None, :] == cur[:, None]) | (j[None, :] == cur[:, None] - 1)
        valid = j[None, :] * SLC_BLOCK <= qpos[:, None]
        imp = jnp.where(forced, FORCED_SCORE, jnp.where(valid, imp, -1.0))
        _, sel = lax.top_k(imp, n_sel)
        k_sel = ks[b_idx, gk_idx, sel].reshape(B, G, Q_BLOCK, n_sel * SLC_BLOCK, DH)
        v_sel = vs[b_idx, gk_idx, sel].reshape(B, G, Q_BLOCK, n_sel * SLC_BLOCK, DH)
        pos = (sel[..., None] * SLC_BLOCK + jnp.arange(SLC_BLOCK)).reshape(B, G, Q_BLOCK, n_sel * SLC_BLOCK)
        s = jnp.einsum('bgrqd,bgqkd->bgrqk', qi, k_sel).astype(jnp.float32) * SCALE
        bias = tbl_grp[g_idx, r_idx, rel_bucket(qpos[:, None] - pos)[:, :, None]]
        p = masked_softmax(s + bias, (pos <= qpos[:, None])[:, :, None])
        o_slc = jnp.einsum('bgrqk,bgqkd->bgrqd', p.astype(v_sel.dtype), v_sel)
        kw = lax.dynamic_slice_in_dim(kwp, i * Q_BLOCK, Q_BLOCK + WINDOW, axis=2)
        vw = lax.dynamic_slice_in_dim(vwp, i * Q_BLOCK, Q_BLOCK + WINDOW, axis=2)
        kpos = i * Q_BLOCK - WINDOW + jnp.arange(Q_BLOCK + WINDOW)
        wmask = ((kpos[None, :] >= 0) & (kpos[None, :] <= qpos[:, None])
                 & (qpos[:, None] - kpos[None, :] < WINDOW))
        s = jnp.einsum('bgrqd,bgkd->bgrqk', qi, kw).astype(jnp.float32) * SCALE + bias_win
        p = masked_softmax(s, wmask)
        o_win = jnp.einsum('bgrqk,bgkd->bgrqd', p.astype(vw.dtype), vw)
        return jnp.stack([o_cmp, o_slc, o_win], axis=-2)

    o = lax.map(block, (jnp.arange(nb), qb))
    o = o.transpose(1, 0, 4, 2, 3, 5, 6).reshape(B, T, H, 3, DH)
    gates = jax.nn.sigmoid(gate_logit)[..., None]
    return jnp.sum(gates * o, axis=3).reshape(B, T, H * DH)

def second_inputs(seed: int = 0) -> dict:
    key = jax.random.key(seed)
    ks = jax.random.split(key, 20)

    def w(k, shape, fan_in):
        return jax.random.normal(k, shape, jnp.float32) * fan_in ** -0.5

    def gain(k, shape):
        return 1.0 + 0.05 * jax.random.normal(k, shape, jnp.float32)

    nrm = lambda k, shape: jax.random.normal(k, shape, jnp.float32)
    L = DEPTH
    return {
        "x": nrm(ks[0], (BATCH, SEQ, D_MODEL)),
        "rel_bias_table": 0.5 * nrm(ks[1], (REL_BUCKETS, NSA_HEADS)),
        "g_attn": gain(ks[2], (L, D_MODEL)),
        "w_in": w(ks[3], (L, D_MODEL, IN_WIDTH), D_MODEL),
        "b_forget": 3.0 + 0.5 * nrm(ks[4], (L, FOX_HEADS)),
        "cmp_pe_k": 0.5 * nrm(ks[5], (L, CMP_BLOCK, HEAD_DIM)),
        "cmp_w1_k": w(ks[6], (L, CMP_BLOCK * HEAD_DIM, CMP_HIDDEN), CMP_BLOCK * HEAD_DIM),
        "cmp_w2_k": w(ks[7], (L, CMP_HIDDEN, HEAD_DIM), CMP_HIDDEN),
        "cmp_pe_v": 0.5 * nrm(ks[8], (L, CMP_BLOCK, HEAD_DIM)),
        "cmp_w1_v": w(ks[9], (L, CMP_BLOCK * HEAD_DIM, CMP_HIDDEN), CMP_BLOCK * HEAD_DIM),
        "cmp_w2_v": w(ks[10], (L, CMP_HIDDEN, HEAD_DIM), CMP_HIDDEN),
        "w_br_fox": w(ks[11], (L, FOX_W, D_MODEL), FOX_W),
        "w_br_nsa": w(ks[12], (L, NSA_W, D_MODEL), NSA_W),
        "w_out": w(ks[13], (L, D_MODEL, D_MODEL), D_MODEL),
        "g_mlp": gain(ks[14], (L, D_MODEL)),
        "w_ff1": w(ks[15], (L, D_MODEL, D_FF), D_MODEL),
        "w_ff2": w(ks[16], (L, D_FF, D_MODEL), D_FF),
        "g_final": gain(ks[17], (D_MODEL,)),
    }

def second_block(x, rel_bias_table, g_attn, w_in, b_forget, cmp_pe_k, cmp_w1_k, cmp_w2_k,
              cmp_pe_v, cmp_w1_v, cmp_w2_v, w_br_fox, w_br_nsa, w_out, g_mlp, w_ff1, w_ff2,
              g_final):
    B, T, _ = x.shape
    offsets = np.cumsum(IN_SPLITS)[:-1].tolist()
    for l in range(DEPTH):
        h = rms_norm_2(x, g_attn[l])
        z = h @ w_in[l]
        (fq, fk, fv, f_logit, nq, kc, vc, ksl, vsl, kwn, vwn, n_gate, g_a, g_b) = jnp.split(z, offsets, axis=-1)
        fox_h = lambda t: t.reshape(B, T, FOX_HEADS, HEAD_DIM)
        kv_h = lambda t: t.reshape(B, T, NSA_KV_GROUPS, HEAD_DIM)
        o_fox = fox_attention(fox_h(fq), fox_h(fk), fox_h(fv), f_logit, b_forget[l])
        o_nsa = nsa_attention(nq.reshape(B, T, NSA_HEADS, HEAD_DIM), kv_h(kc), kv_h(vc), kv_h(ksl), kv_h(vsl),
                              kv_h(kwn), kv_h(vwn), n_gate.reshape(B, T, NSA_HEADS, 3), rel_bias_table,
                              cmp_pe_k[l], cmp_w1_k[l], cmp_w2_k[l], cmp_pe_v[l], cmp_w1_v[l], cmp_w2_v[l])
        merged = jax.nn.sigmoid(g_a) * (o_fox @ w_br_fox[l]) + jax.nn.sigmoid(g_b) * (o_nsa @ w_br_nsa[l])
        x = x + merged @ w_out[l]
        h = rms_norm_2(x, g_mlp[l])
        x = x + jnp.square(jax.nn.relu(h @ w_ff1[l])) @ w_ff2[l]
    return rms_norm_2(x, g_final)


def setup_inputs(seed=0):
    out = dict(first_inputs(seed))
    for name, value in second_inputs(seed + 1).items():
        if name != "x":
            out[name + "_2"] = value
    return out


def reference(
    x, mem, norm_mix, w_comb, conv_w, mu_rwkv, w0, w_lora, a0, a_lora, g_lora, k_k, k_a, r_k,
    lnx_w, lnx_b, w_vres, mu_vres, v0, v_lora, branch_proj, gate_b, w_mix_out, norm_ca,
    norm_mem, ca_wq, ca_wkv, ca_wo, norm_ffn, ffn_up, ffn_conv_w, ffn_conv_b, ffn_down,
    norm_final, rel_bias_table_2, g_attn_2, w_in_2, b_forget_2, cmp_pe_k_2, cmp_w1_k_2,
    cmp_w2_k_2, cmp_pe_v_2, cmp_w1_v_2, cmp_w2_v_2, w_br_fox_2, w_br_nsa_2, w_out_2, g_mlp_2,
    w_ff1_2, w_ff2_2, g_final_2,
):
    x = first_block(
        x, mem, norm_mix, w_comb, conv_w, mu_rwkv, w0, w_lora, a0, a_lora, g_lora, k_k, k_a,
        r_k, lnx_w, lnx_b, w_vres, mu_vres, v0, v_lora, branch_proj, gate_b, w_mix_out, norm_ca,
        norm_mem, ca_wq, ca_wkv, ca_wo, norm_ffn, ffn_up, ffn_conv_w, ffn_conv_b, ffn_down,
        norm_final,
    )
    return second_block(
        x, rel_bias_table_2, g_attn_2, w_in_2, b_forget_2, cmp_pe_k_2, cmp_w1_k_2, cmp_w2_k_2,
        cmp_pe_v_2, cmp_w1_v_2, cmp_w2_v_2, w_br_fox_2, w_br_nsa_2, w_out_2, g_mlp_2, w_ff1_2,
        w_ff2_2, g_final_2,
    )


_drawn_inputs = setup_inputs


def setup_inputs(seed=0):
    import zlib

    import numpy as np

    out = dict(_drawn_inputs(seed))
    spreads = {}
    factors = {'k_k': 8.0,
     'lnx_w': 8.0,
     'lnx_b': 8.0,
     'gate_b': 8.0,
     'norm_ca': 8.0,
     'norm_mem': 8.0,
     'norm_ffn': 4.832,
     'ffn_conv_b': 4.404,
     'g_attn_2': 3.433,
     'cmp_pe_k_2': 6.316}
    for name, (base, spread) in spreads.items():
        noise = np.random.default_rng([zlib.crc32(name.encode()), seed]).standard_normal(out[name].shape)
        drawn = base * np.exp(spread * noise) if base else spread * noise
        out[name] = jnp.asarray(drawn.astype(out[name].dtype))
    for name, factor in factors.items():
        out[name] = (out[name] * factor).astype(out[name].dtype)
    return out
```

```python
import math
from contextlib import ExitStack

import numpy as np

import concourse.bass as bass
from concourse import mybir

P = 128
T = 512
NT = T // P
D = 1024
KD = D // P
MEM = 256
W = 512
NW = W // P
F = 2816
NF = F // P
NFF = 4096 // P
HD = 64
HEADS = 8
RING = 4
SLOT = 11 * P
NC_CMP = (T - 32) // 16 + 1
VEC_DIST = 1024
DECAY = math.exp(-0.5)
RMS_EPS = 1e-6
GN_EPS = 64e-5
NEG = -1e30

ALU = mybir.AluOpType
ACT = mybir.ActivationFunctionType
AX = mybir.AxisListType
F32 = mybir.dt.float32

PHASES = {
    "proj": (38, 8),
    "gates": (32, 9),
    "mix": (8, 8),
    "ca": (32, 8),
    "up": (44, 8),
    "down": (16, 11),
    "in2": (22, 8),
    "gates2": (24, 8),
    "out2": (8, 8),
    "ff1": (32, 8),
    "ff2": (32, 8),
}

VECS = [
    ("norm_mix", 8), ("conv_w", 12), ("mu_rwkv", 14), ("w0", 4), ("a0", 4), ("k_k", 4), ("k_a", 4), ("r_k", 4),
    ("lnx_w", 4), ("lnx_b", 4), ("gate_b", 24), ("norm_ca", 8), ("norm_mem", 8), ("norm_ffn", 8),
    ("ffn_conv_w", 132), ("ffn_conv_b", 44), ("norm_final", 8), ("g_attn_2", 8), ("g_mlp_2", 8), ("g_final_2", 8),
    ("pe_k", 16), ("pe_v", 16), ("b_forget", 8),
]
VEC_AT = {}
_n = 0
for _name, _cols in VECS:
    VEC_AT[_name] = _n
    _n += _cols
N_VEC = _n

CONSTS = [
    ("ident", 128), ("ones", 128), ("head_ones", 128), ("upper", 128), ("causal4", 512), ("neg_tri", 128),
    ("neg_ones", 128), ("neg_diag_t", 128), ("level", 896), ("flip", 128),
    ("causal_add", 128), ("cmp_add", 124), ("cmp_keep", 124),
]
CONST_AT = {}
_n = 0
for _name, _cols in CONSTS:
    CONST_AT[_name] = _n
    _n += _cols
N_CONST = _n


class Core:

    def __init__(self, nc, ctx, dram):
        self.nc, self.dram = nc, dram
        sb = lambda name, shape: ctx.enter_context(nc.sbuf_tensor(name, shape, F32))
        self.vec = sb("vec_sb", [P, N_VEC])
        self.const = sb("const_sb", [P, N_CONST])
        self.h = sb("h", [P, KD, T])
        self.xn = sb("xn", [P, KD, T])
        self.merged = sb("merged", [P, KD, T])
        self.ring = sb("weight_ring", [P, RING, SLOT])
        self.weights_in = [nc.alloc_semaphore(f"weights_in{s}") for s in range(RING)]
        self.groups_done = nc.alloc_semaphore("groups_done")
        self.banks_free = nc.alloc_semaphore("banks_free")
        self.stage_sems = []
        self.loaded = 0
        self.used = 0
        self.evacs = 0
        self.order = list(PHASES)
        self.preloaded = {}
        self.small = sb("small", [P, 64])
        self.arena = sb("arena", [P, 61, T])

    def c(self, name, lo=0, n=None):
        at = CONST_AT[name] + lo
        return self.const[:, at:at + (n if n else dict(CONSTS)[name] - lo)]

    def v(self, name, i):
        return self.vec[:, VEC_AT[name] + i:VEC_AT[name] + i + 1]

    def sem(self, name):
        self.stage_sems.append(self.nc.alloc_semaphore(name))
        return self.stage_sems[-1]

    def load_weights(self, sp, phase, lo, hi):
        src, cols, g0 = self.dram["w_" + phase], PHASES[phase][1] * P, self.loaded

        def load(g, i, at):
            if g >= RING:
                sp.wait_ge(self.groups_done, g - RING + 1 + i * RING)
            group = src[bass.ds(at + i * RING, 1)] if not isinstance(i, int) else src[at:at + 1]
            sp.dma_start(self.ring[:, g % RING, 0:cols], group.rearrange("a p n -> p (a n)"))\
                .then_inc(self.weights_in[g % RING], 16)

        n = hi - lo
        done = 0
        if g0 < RING:
            done = min(n, RING - g0)
            for j in range(done):
                load(g0 + j, 0, lo + j)
        turns = (n - done) // RING
        if turns > 1:
            with sp.Fori(0, turns) as i:
                for j in range(RING):
                    load(g0 + done + j, i, lo + done + j)
            done += turns * RING
        for j in range(done, n):
            load(g0 + j, 0, lo + j)
        self.loaded += n

    def stream(self, sp, phases):
        for phase in phases:
            n = PHASES[phase][0]
            lo = self.preloaded.pop(phase, 0)
            self.load_weights(sp, phase, lo, n)
        at = self.order.index(phases[-1]) + 1
        if at < len(self.order):
            self.load_weights(sp, self.order[at], 0, RING)
            self.preloaded[self.order[at]] = RING

    def wait_weights(self, pe, g, i=0, per=RING):
        pe.wait_ge(self.weights_in[g % RING], 16 * (g // RING + 1) + i * (16 * per // RING))


def in_turns(eng, n, per, body):
    turns = n // per
    done = 0
    if turns > 1:
        with eng.Fori(0, turns) as i:
            for j in range(per):
                body(i, j, 0)
        done = turns * per
    for j in range(done, n):
        body(0, j - done, done)


def pe_gemm(core, pe, n, kc, rhs, ps, width=T):
    g0, e0 = core.used, core.evacs
    assert RING % 4 == 0

    def step(i, j, done):
        g, e = g0 + done + j, e0 + done + j
        core.wait_weights(pe, g, i)
        pe.wait_ge(core.banks_free, e + 1 + i * RING)
        for k in range(kc):
            mm = pe.matmul(ps[:, e % 4, 0:width], core.ring[:, g % RING, k * P:(k + 1) * P], rhs(k),
                           start=(k == 0), stop=(k == kc - 1))
        mm.then_inc(core.groups_done, 1)

    in_turns(pe, n, RING, step)
    core.used += n
    core.evacs += n


def evacuate(core, eng, g0, e0, n, emit):

    def step(i, j, done):
        eng.wait_ge(core.groups_done, g0 + done + j + 1 + i * RING)
        tile = done + j + i * RING
        emit(tile, (e0 + done + j) % 4).then_inc(core.banks_free, 1)

    in_turns(eng, n, RING, step)


def at(buf, tile, lo=0, hi=T):
    if isinstance(tile, int):
        return buf[:, tile, lo:hi]
    return buf[:, bass.ds(tile, 1), lo:hi].rearrange("p a t -> p (a t)")


def setup_stage(core):
    nc, dram = core.nc, core.dram
    x_in, const_in, vec_in = core.sem("x_in"), core.sem("const_in"), core.sem("vec_in")
    wa_in, g_in = core.sem("wa_lora_in"), core.sem("g_lora_in")
    with nc.Block() as block:

        @block.sync
        def _(sp):
            sp.dma_start(core.h[:], dram["x_t"]).then_inc(x_in, 16)
            sp.dma_start(core.const[:], dram["const"]).then_inc(const_in, 16)
            core.load_weights(sp, "proj", 0, RING)
            core.preloaded["proj"] = RING
            sp.wait_ge(x_in, 16)
            sp.wait_ge(const_in, 16)

        @block.scalar
        def _(act):
            act.dma_start(core.vec[:], dram["vec"]).then_inc(vec_in, 16)
            act.dma_start(core.arena[:, 59, :], dram["wa_lora"]).then_inc(wa_in, 16)
            act.dma_start(core.arena[:, 60, :], dram["g_lora_t"]).then_inc(g_in, 16)
            act.wait_ge(vec_in, 16)
            act.wait_ge(wa_in, 16)
            act.wait_ge(g_in, 16)

        @block.vector
        def _(dve):
            dve.sem_inc(core.banks_free, 4)


def norm_stage(core, name, src, gain, dst, width=T, stream=None, src2=None):
    nc = core.nc
    squared = core.sem(name + "_squared")
    summed = core.sem(name + "_summed")
    steps = core.sem(name + "_steps")
    rooted = core.sem(name + "_rooted")
    steps_sq = core.sem(name + "_squared_too")
    with ExitStack() as ctx:
        ps = ctx.enter_context(nc.psum_tensor(name + "_ps", [P, T], F32))
        sq = core.arena[:, 40:48, 0:width]
        rstd = core.arena[:, 48, 0:width]
        with nc.Block() as block:

            @block.scalar
            def _(act):
                for k in range(0, KD, 2):
                    act.activation(sq[:, k, :], src(k), ACT.Square).then_inc(squared, 1)
                act.wait_ge(steps, 1)
                act.activation(rstd, rstd, ACT.Sqrt).then_inc(rooted, 1)

            @block.tensor
            def _(pe):
                for k in range(KD):
                    if k % 2 == 0:
                        pe.wait_ge(squared, k // 2 + 1)
                    else:
                        pe.wait_ge(steps_sq, k // 2 + 1)
                    mm = pe.matmul(ps[:, 0:width], core.c("ones"), sq[:, k, :], start=(k == 0), stop=(k == KD - 1))
                mm.then_inc(summed, 1)

            @block.vector
            def _(dve):
                for k in range(1, KD, 2):
                    dve.tensor_tensor(sq[:, k, :], src(k), src(k), ALU.mult).then_inc(steps_sq, 1)
                dve.wait_ge(summed, 1)
                dve.tensor_scalar(rstd, ps[:, 0:width], 1.0 / D, RMS_EPS, ALU.mult, ALU.add).then_inc(steps, 1)
                dve.wait_ge(rooted, 1)
                dve.reciprocal(rstd, rstd).then_inc(steps, 1)
                dve.wait_ge(steps, 2)
                for k in range(KD):
                    dve.scalar_tensor_tensor(dst(k), src(k), core.v(gain, k), rstd, ALU.mult, ALU.mult)


def proj_stage(core):
    nc = core.nc
    g0, e0 = core.used, core.evacs
    rwkv = core.arena[:, 12:26, :]
    qk = core.arena[:, 26:34, :]
    value = core.arena[:, 34:38, :]
    conv = core.arena[:, 38:50, :]
    diff = core.arena[:, 50:52, :]
    steps = core.sem("proj_steps")
    with ExitStack() as ctx:
        ps = ctx.enter_context(nc.psum_tensor("proj_ps", [P, 4, T], F32))
        ps_v = ctx.enter_context(nc.psum_tensor("proj_ps_v", [P, NT, T], F32))
        with nc.Block() as block:

            @block.sync
            def _(sp):
                core.stream(sp, ["proj"])

            @block.tensor
            def _(pe):
                x = lambda k: core.xn[:, k, :]
                pe_gemm(core, pe, 14, KD, x, ps)
                pe_gemm(core, pe, 12, KD, x, ps)
                pe_gemm(core, pe, 8, KD, x, ps)
                for g in range(4):
                    core.wait_weights(pe, core.used)
                    for half in range(2):
                        k = 2 * g + half
                        for i in range(NT):
                            mm = pe.matmul(ps_v[:, i, :], core.xn[:, k, i * P:(i + 1) * P],
                                           core.ring[:, core.used % RING, half * T:(half + 1) * T],
                                           start=(k == 0), stop=(k == KD - 1))
                    mm.then_inc(core.groups_done, 1)
                    core.used += 1

            @block.scalar
            def _(act):
                copy = lambda buf, scale: lambda tile, bank: act.activation(at(buf, tile), ps[:, bank, :], ACT.Copy, scale=scale)
                evacuate(core, act, g0, e0, 14, copy(rwkv, 1.0))
                evacuate(core, act, g0 + 14, e0 + 14, 12, copy(conv, 1.0))
                evacuate(core, act, g0 + 26, e0 + 26, 4, copy(qk, HD ** -0.5))
                evacuate(core, act, g0 + 30, e0 + 30, 4, copy(qk[:, 4:8, :], 1.0))
                act.wait_ge(core.groups_done, g0 + 38)
                for i in range(NT):
                    act.activation(value[:, i, :], ps_v[:, i, :], ACT.Copy)

            @block.vector
            def _(dve):
                n = 0
                for j in range(14):
                    p, d = rwkv[:, j, :], diff[:, j % 2, :]
                    dve.wait_ge(core.banks_free, 4 + e0 + j + 1)
                    dve.tensor_scalar(d[:, 0:1], p[:, 0:1], -1.0, None, ALU.mult).then_inc(steps, 1)
                    dve.tensor_tensor(d[:, 1:T], p[:, 0:T - 1], p[:, 1:T], ALU.subtract).then_inc(steps, 1)
                    n += 2
                    dve.wait_ge(steps, n)
                    dve.scalar_tensor_tensor(p, d, core.v("mu_rwkv", j), p, ALU.mult, ALU.add).then_inc(steps, 1)
                    n += 1
                for j in range(NW):
                    u, y, b = conv[:, 3 * j, :], conv[:, 3 * j + 1, :], conv[:, 3 * j + 2, :]
                    dve.wait_ge(core.banks_free, 4 + e0 + 14 + 3 * j + 3)
                    dve.tensor_tensor(u, u, y, ALU.mult).then_inc(steps, 1)
                    dve.wait_ge(steps, n + 1)
                    dve.tensor_scalar(y, u, core.v("conv_w", 8 + j), None, ALU.mult).then_inc(steps, 1)
                    dve.wait_ge(steps, n + 2)
                    dve.scalar_tensor_tensor(y[:, 1:T], u[:, 0:T - 1], core.v("conv_w", 4 + j), y[:, 1:T], ALU.mult, ALU.add)\
                       .then_inc(steps, 1)
                    dve.wait_ge(steps, n + 3)
                    dve.scalar_tensor_tensor(y[:, 2:T], u[:, 0:T - 2], core.v("conv_w", j), y[:, 2:T], ALU.mult, ALU.add)\
                       .then_inc(steps, 1)
                    dve.wait_ge(steps, n + 4)
                    dve.tensor_tensor(core.arena[:, j, :], y, b, ALU.mult).then_inc(steps, 1)
                    n += 5


def stick_breaking_stage(core):
    nc = core.nc
    query, key = core.arena[:, 26:30, :], core.arena[:, 30:34, :]
    value = core.arena[:, 34:38, :]
    flat = core.arena[:, 38:53, :].rearrange("p a t -> p (a t)")
    log_buf = [flat[:, b * 1280:(b + 1) * 1280] for b in range(2)]
    soft = [flat[:, 2560 + b * 1280:2560 + (b + 1) * 1280] for b in range(2)]
    att = [flat[:, 5120 + b * 1280:5120 + (b + 1) * 1280] for b in range(2)]
    start = [0, 512, 896, 1152]
    scores_ready = core.sem("sb_scores_ready")
    abs_ready = core.sem("sb_abs_ready")
    exp_ready = core.sem("sb_exp_ready")
    log_ready = core.sem("sb_log_ready")
    soft_part = core.sem("sb_soft_part")
    soft_ready = core.sem("sb_soft_ready")
    weight_ready = core.sem("sb_weight_ready")
    att_ready = core.sem("sb_att_ready")
    out_done = core.sem("sb_out_done")
    out_taken = core.sem("sb_out_taken")
    with ExitStack() as ctx:
        ps = ctx.enter_context(nc.psum_tensor("sb_ps", [P, 6, T], F32))
        ps_out = ctx.enter_context(nc.psum_tensor("sb_ps_out", [P, 2, T], F32))

        def tile(h, j):
            bank, lo = (j, 0) if j < 3 else (2, 256)
            return ps[:, 3 * (h % 2) + bank, lo:lo + T - j * P]

        def parts(h, buf):
            return [(ps[:, 3 * (h % 2) + m, 0:n], buf[h % 2][:, lo:lo + n]) for m, lo, n in ((0, 0, 512), (1, 512, 384), (2, 896, 384))]

        with nc.Block() as block:

            @block.tensor
            def _(pe):
                def scores(h):
                    c, off = h // 2, HD * (h % 2)
                    if h >= 2:
                        pe.wait_ge(att_ready, h - 1)
                    for j in range(NT):
                        mm = pe.matmul(tile(h, j), key[off:off + HD, c, j * P:(j + 1) * P], query[off:off + HD, c, j * P:T],
                                       start=(j < 3), stop=False, skip_group_check=True)
                    mm.then_inc(scores_ready, 1)

                def weights(h):
                    pe.wait_ge(soft_ready, h + 1)
                    for j in range(NT):
                        pe.matmul(tile(h, j)[:, 0:P], core.c("ident"), core.c("neg_diag_t"), start=False, stop=False,
                                  skip_group_check=True)
                        for m in range(j, NT):
                            mm = pe.matmul(tile(h, j)[:, (m - j) * P:T - j * P], core.c("neg_tri" if m == j else "neg_ones"),
                                           soft[h % 2][:, start[m]:start[m] + T - m * P], start=False, stop=(m == NT - 1),
                                           skip_group_check=True)
                    mm.then_inc(weight_ready, 1)

                def output(h):
                    c, off = h // 2, HD * (h % 2)
                    pe.wait_ge(att_ready, h + 1)
                    if c >= 2:
                        pe.wait_ge(out_taken, c - 1)
                    for j in range(NT):
                        mm = pe.matmul(ps_out[off:off + HD, c % 2, j * P:T], value[:, j, h * HD:(h + 1) * HD],
                                       att[h % 2][:, start[j]:start[j] + T - j * P], start=(j == 0), stop=(j == NT - 1),
                                       skip_group_check=True)
                    mm.then_inc(out_done, 1)

                scores(0)
                for h in range(HEADS):
                    if h + 1 < HEADS:
                        scores(h + 1)
                    weights(h)
                    if h >= 1:
                        output(h - 1)
                output(HEADS - 1)

            @block.scalar
            def _(act):
                def logs(h):
                    act.wait_ge(scores_ready, h + 1)
                    if h >= 2:
                        act.wait_ge(soft_part, h - 1)
                    for banks, cols in parts(h, log_buf):
                        ins = act.activation(cols, banks, ACT.Abs)
                    ins.then_inc(abs_ready, 1)
                    act.wait_ge(abs_ready, h + 1)
                    act.activation(log_buf[h % 2], log_buf[h % 2], ACT.Exp, scale=-1.0).then_inc(exp_ready, 1)
                    act.wait_ge(exp_ready, h + 1)
                    act.activation(log_buf[h % 2], log_buf[h % 2], ACT.Ln, bias=1.0).then_inc(log_ready, 1)

                def weights(h):
                    act.wait_ge(weight_ready, h + 1)
                    if h >= 2:
                        act.wait_ge(out_done, h - 1)
                    for i, (banks, cols) in enumerate(parts(h, att)):
                        ins = act.activation(cols, banks, ACT.Exp)
                    ins.then_inc(att_ready, 1)

                logs(0)
                for h in range(HEADS):
                    if h + 1 < HEADS:
                        logs(h + 1)
                    weights(h)

            @block.vector
            def _(dve):
                def softplus(h):
                    dve.wait_ge(log_ready, h + 1)
                    if h >= 2:
                        dve.wait_ge(weight_ready, h - 1)
                    for (banks, cols), (_, logs) in zip(parts(h, soft), parts(h, log_buf)):
                        ins = dve.scalar_tensor_tensor(cols, banks, 0.0, logs, ALU.max, ALU.add)
                    ins.then_inc(soft_part, 1)
                    dve.wait_ge(soft_part, h + 1)
                    for j in range(NT):
                        diag = soft[h % 2][:, start[j]:start[j] + P]
                        ins = dve.tensor_tensor(diag, diag, core.c("causal4", 0, P), ALU.mult)
                    ins.then_inc(soft_ready, 1)

                def take(c):
                    dve.wait_ge(out_done, 2 * c + 2)
                    dve.tensor_copy(core.arena[:, 4 + c, :], ps_out[:, c % 2, :]).then_inc(out_taken, 1)

                for h in range(HEADS):
                    softplus(h)
                    if h >= 2 and h % 2 == 0:
                        take(h // 2 - 1)
                take(NW - 1)


def clear_semaphores_stage(core):
    with core.nc.Block() as block:

        @block.sync
        def _(sp):
            for sem in core.stage_sems:
                sp.sem_clear(sem)

    for sem in core.stage_sems:
        core.nc.release_semaphore(sem)
    core.stage_sems = []


def time_mix_stage(core):
    nc, a = core.nc, core.arena
    r, k, v = a[:, 12:16, :], a[:, 16:20, :], a[:, 20:24, :]
    wa, xg, lora, g_lora = a[:, 24, :], a[:, 25, :], a[:, 59, :], a[:, 60, :]
    kk, bonus, key = a[:, 26:30, :], a[:, 30:34, :], a[:, 34:38, :]
    decay, rate, gate, sums = a[:, 38:42, :], a[:, 42:46, :], a[:, 46:50, :], a[:, 50:54, :]
    restart = a[:, 58, :]
    norm, rk = core.merged[:, 0:4, :], core.merged[:, 4:8, :]
    mid = core.small[:, 0:16]
    inner = core.sem("tm_inner")
    lora_out = core.sem("tm_lora_out")
    lora_taken = core.sem("tm_lora_taken")
    square = core.sem("tm_square")
    bonus_in = core.sem("tm_bonus_in")
    norm_sum = core.sem("tm_norm_sum")
    bonus_sum = core.sem("tm_bonus_sum")
    rooted = core.sem("tm_rooted")
    steps = core.sem("tm_steps")
    ready = core.sem("tm_restart")
    with ExitStack() as ctx:
        ps = ctx.enter_context(nc.psum_tensor("tm_ps", [P, 8, T], F32))
        with nc.Block() as block:

            @block.gpsimd
            def _(pool):
                pool.memset(restart, 1.0).then_inc(ready, 1)
                pool.wait_ge(ready, 1)
                pool.memset(restart[:, 0:T:P], 0.0).then_inc(ready, 1)

            @block.scalar
            def _(act):
                act.activation(wa[0:HD, :], wa[0:HD, :], ACT.Tanh).then_inc(inner, 1)
                act.activation(xg, xg, ACT.Sigmoid).then_inc(inner, 1)
                for c in range(NW):
                    act.wait_ge(lora_out, c + 1)
                    act.activation(decay[:, c, :], ps[:, 4 * (c % 2), :], ACT.Sigmoid, bias=core.v("w0", c))
                    act.activation(rate[:, c, :], ps[:, 4 * (c % 2) + 1, :], ACT.Sigmoid, bias=core.v("a0", c))
                    act.activation(gate[:, c, :], ps[:, 4 * (c % 2) + 2, :], ACT.Copy).then_inc(lora_taken, 1)
                for c in range(NW):
                    act.wait_ge(norm_sum, c + 1)
                    act.activation(norm[:, c, :], ps[:, 4 * (c % 2) + 3, :], ACT.Sqrt).then_inc(rooted, 1)

            @block.tensor
            def _(pe):
                pe.wait_ge(inner, 2)
                for c in range(NW):
                    if c >= 2:
                        pe.wait_ge(lora_taken, c - 1)
                    cols = slice(c * P, (c + 1) * P)
                    pe.matmul(ps[:, 4 * (c % 2), :], lora[0:HD, cols], wa[0:HD, :], start=True, stop=True)
                    pe.matmul(ps[:, 4 * (c % 2) + 1, :], lora[HD:P, cols], wa[HD:P, :], start=True, stop=True)
                    pe.matmul(ps[:, 4 * (c % 2) + 2, :], g_lora[:, cols], xg, start=True, stop=True).then_inc(lora_out, 1)
                for c in range(NW):
                    pe.wait_ge(square, c + 1)
                    if c >= 2:
                        pe.wait_ge(rooted, c - 1)
                    pe.matmul(ps[:, 4 * (c % 2) + 3, :], core.c("head_ones"), bonus[:, c, :], start=True, stop=True)\
                      .then_inc(norm_sum, 1)
                pe.wait_ge(lora_taken, NW)
                for c in range(NW):
                    pe.wait_ge(bonus_in, c + 1)
                    pe.matmul(ps[:, (0, 1, 4, 5)[c], :], core.c("head_ones"), rk[:, c, :], start=True, stop=True)\
                      .then_inc(bonus_sum, 1)

            @block.vector
            def _(dve):
                n = 0
                for c in range(NW):
                    dve.tensor_scalar(kk[:, c, :], k[:, c, :], core.v("k_k", c), None, ALU.mult).then_inc(steps, 1)
                    n += 1
                    dve.wait_ge(steps, n)
                    dve.tensor_tensor(bonus[:, c, :], kk[:, c, :], kk[:, c, :], ALU.mult).then_inc(square, 1)
                for c in range(NW):
                    dve.tensor_scalar(rk[:, c, :], r[:, c, :], core.v("r_k", c), None, ALU.mult).then_inc(steps, 1)
                    n += 1
                for c in range(NW):
                    dve.wait_ge(lora_taken, c + 1)
                    dve.tensor_scalar(key[:, c, :], rate[:, c, :], -1.0, core.v("k_a", c), ALU.add, ALU.mult).then_inc(steps, 1)
                    n += 1
                    dve.wait_ge(steps, n)
                    dve.scalar_tensor_tensor(key[:, c, :], key[:, c, :], 1.0, k[:, c, :], ALU.add, ALU.mult).then_inc(steps, 1)
                    n += 1
                    dve.wait_ge(steps, n)
                    dve.tensor_tensor(rk[:, c, :], rk[:, c, :], key[:, c, :], ALU.mult).then_inc(bonus_in, 1)
                dve.wait_ge(ready, 2)
                for c in range(NW):
                    dve.tensor_tensor_scan(sums[:, c, :], restart, decay[:, c, :], 0.0, ALU.mult, ALU.add).then_inc(steps, 1)
                n += NW
                dve.wait_ge(steps, n)
                for c in range(NW):
                    dve.tensor_copy(mid[:, 4 * c:4 * c + 4], sums[:, c, P // 2 - 1:T:P]).then_inc(steps, 1)
                n += NW
                dve.wait_ge(steps, n)
                for c in range(NW):
                    s3 = sums[:, c, :].rearrange("p (n t) -> p n t", t=P)
                    dve.tensor_tensor(s3, s3, mid[:, 4 * c:4 * c + 4].unsqueeze(2).broadcast_to([P, NT, P]), ALU.subtract)\
                       .then_inc(steps, 1)
                n += NW
                dve.wait_ge(steps, n)
                for c in range(NW):
                    dve.tensor_tensor(decay[:, c, :], sums[:, c, :], decay[:, c, :], ALU.subtract).then_inc(steps, 1)
                n += NW
                for c in range(NW):
                    dve.wait_ge(rooted, c + 1)
                    dve.tensor_scalar(norm[:, c, :], norm[:, c, :], 1e-12, None, ALU.max).then_inc(steps, 1)
                    n += 1
                    dve.wait_ge(steps, n)
                    dve.reciprocal(norm[:, c, :], norm[:, c, :]).then_inc(steps, 1)
                    n += 1
                    dve.wait_ge(steps, n)
                    dve.tensor_tensor(kk[:, c, :], kk[:, c, :], norm[:, c, :], ALU.mult).then_inc(steps, 1)
                    n += 1
                for c in range(NW):
                    dve.wait_ge(bonus_sum, c + 1)
                    dve.tensor_tensor(bonus[:, c, :], ps[:, (0, 1, 4, 5)[c], :], v[:, c, :], ALU.mult)


def time_mix_scale_stage(core):
    nc, a = core.nc, core.arena
    r, k_out, v, v_tok = a[:, 12:16, :], a[:, 16:20, :], a[:, 20:24, :], a[:, 12:16, :]
    kk, key, kk_tok, key_tok = a[:, 26:30, :], a[:, 34:38, :], a[:, 34:38, :], a[:, 26:30, :]
    before, rate, sums, upto = a[:, 38:42, :], a[:, 42:46, :], a[:, 50:54, :], a[:, 54:58, :]
    pair = core.merged[:].rearrange("p (c n) (m q t) -> p c (n m) q t", n=2, q=2, t=P)
    upto_ready = core.sem("ts_upto_ready")
    before_ready = core.sem("ts_before_ready")
    away_ready = core.sem("ts_away_ready")
    steps = core.sem("ts_steps")
    r_used = core.sem("ts_r_used")
    k_made = core.sem("ts_k_made")
    b_made = core.sem("ts_b_made")
    turned = core.sem("ts_turned")
    placed = core.sem("ts_placed")
    chunks = lambda x: x.rearrange("p (n t) -> p n t", t=P)
    with ExitStack() as ctx:
        ps = ctx.enter_context(nc.psum_tensor("ts_ps", [P, 8, T], F32))
        with nc.Block() as block:

            @block.scalar
            def _(act):
                for c in range(NW):
                    act.activation(upto[:, c, :], sums[:, c, :], ACT.Exp, scale=-DECAY).then_inc(upto_ready, 1)
                    act.activation(before[:, c, :], before[:, c, :], ACT.Exp, scale=-DECAY).then_inc(before_ready, 1)
                    act.wait_ge(upto_ready, c + 1)
                    act.activation(sums[:, c, :], sums[:, c, :], ACT.Exp, scale=DECAY).then_inc(away_ready, 1)
                act.activation(core.small[:, 16:32], core.small[:, 0:16], ACT.Exp, scale=-DECAY)
                for n in range(12):
                    act.wait_ge(turned, n + 1)
                    if n < 4:
                        act.wait_ge(r_used, NW)
                    else:
                        act.wait_ge(b_made, NW)
                    out = (v_tok, key_tok, kk_tok)[n // 4]
                    act.activation(out[:, n % 4, :], ps[:, n % 8, :], ACT.Copy).then_inc(placed, 1)

            @block.vector
            def _(dve):
                for c in range(NW):
                    dve.wait_ge(upto_ready, c + 1)
                    dve.tensor_tensor(pair[:, c, :, 1, :], chunks(r[:, c, :]), chunks(upto[:, c, :]), ALU.mult).then_inc(r_used, 1)
                for c in range(NW):
                    dve.wait_ge(before_ready, c + 1)
                    dve.tensor_tensor(pair[:, c, :, 0, :], chunks(kk[:, c, :]), chunks(before[:, c, :]), ALU.mult)
                    dve.wait_ge(away_ready, c + 1)
                    dve.tensor_tensor(k_out[:, c, :], key[:, c, :], sums[:, c, :], ALU.mult).then_inc(k_made, 1)
                    dve.tensor_tensor(rate[:, c, :], rate[:, c, :], kk[:, c, :], ALU.mult).then_inc(steps, 1)
                    dve.wait_ge(steps, c + 1)
                    dve.tensor_tensor(rate[:, c, :], rate[:, c, :], sums[:, c, :], ALU.mult).then_inc(b_made, 1)
                for c in range(NW):
                    dve.tensor_copy(core.small[:, 32 + 4 * c:36 + 4 * c], upto[:, c, P - 1:T:P])

            @block.tensor
            def _(pe):
                for n in range(12):
                    src = (v, k_out, rate)[n // 4]
                    if n == 4:
                        pe.wait_ge(k_made, NW)
                    if n == 8:
                        pe.wait_ge(b_made, NW)
                    if n >= 8:
                        pe.wait_ge(placed, n - 7)
                    for c in range(NW):
                        mm = pe.transpose(ps[:, n % 8, c * P:(c + 1) * P], src[:, c, (n % 4) * P:(n % 4 + 1) * P], core.c("ident"))
                    mm.then_inc(turned, 1)


def time_mix_chunks_stage(core):
    nc, a = core.nc, core.arena
    v_tok, key_tok, b_tok = a[:, 12:16, :], a[:, 26:30, :], a[:, 34:38, :]
    k_out, b_out = a[:, 16:20, :], a[:, 42:46, :]
    pair = core.merged[:].rearrange("p (c n) (m q t) -> p c (n m) q t", n=2, q=2, t=P)
    gram = a[:, 50:58, :]
    inv, inv_t = a[:, 38:40, :], a[:, 40:42, :]
    level = [a[:, 20:22, :], a[:, 22:24, :]]
    prod = a[:, 24:26, :]
    state = a[:, 58, 0:256]
    x_sb, sa = a[:, 59, :], a[:, 60, :]
    out = a[:, 8:12, :]
    from_start, to_end = core.small[:, 16:32], core.small[:, 32:48]
    LEVELS = 7
    gram_done = core.sem("tc_gram_done")
    gram_ready = core.sem("tc_gram_ready")
    units_ready = core.sem("tc_units_ready")
    level_ready = core.sem("tc_level_ready")
    prod_done = core.sem("tc_prod_done")
    prod_ready = core.sem("tc_prod_ready")
    step_done = core.sem("tc_step_done")
    step_ready = core.sem("tc_step_ready")
    x_done, x_ready = core.sem("tc_x_done"), core.sem("tc_x_ready")
    sa_done, sa_ready = core.sem("tc_sa_done"), core.sem("tc_sa_ready")
    end_done, out_ready = core.sem("tc_end_done"), core.sem("tc_out_ready")
    state_sum, state_ready = core.sem("tc_state_sum"), core.sem("tc_state_ready")
    heads = lambda x: x.rearrange("p a (m t) -> p (a m) t", t=P)
    with ExitStack() as ctx:
        ps = ctx.enter_context(nc.psum_tensor("tc_ps", [P, 8, T], F32))
        with nc.Block() as block:

            @block.tensor
            def _(pe):
                def grams(ch):
                    for h in range(HEADS):
                        c, rows, u = h // 2, slice(HD * (h % 2), HD * (h % 2) + HD), ch * HEADS + h
                        if u >= 2:
                            pe.wait_ge(gram_ready, u - 1)
                        qr = pair[rows, c, ch, :, :].rearrange("p q t -> p (q t)")
                        cols = slice(ch * P, (ch + 1) * P)
                        pe.matmul(ps[:, h % 2, 0:256], b_out[rows, c, cols], qr, start=True, stop=True)
                        pe.matmul(ps[:, h % 2, 256:512], k_out[rows, c, cols], qr, start=True, stop=True)\
                          .then_inc(gram_done, 1)

                def inverse(ch):
                    for n in range(LEVELS):
                        pe.wait_ge(level_ready, ch * LEVELS + n + 1)
                        if n == 0:
                            pe.wait_ge(units_ready, ch + 1)
                            if ch:
                                pe.wait_ge(out_ready, ch)
                                pe.wait_ge(state_ready, ch)
                        for half in range(2):
                            u = (ch * LEVELS + n) * 2 + half
                            if u >= 2:
                                pe.wait_ge(step_ready, u - 1)
                            for m in range(4):
                                h = 4 * half + m
                                mm = pe.matmul(ps[:, 2 + half, m * P:(m + 1) * P], heads(level[(ch * LEVELS + n) % 2])[:, h, :],
                                               heads(inv)[:, h, :], start=True, stop=True)
                            mm.then_inc(prod_done, 1)
                        for half in range(2):
                            u = (ch * LEVELS + n) * 2 + half
                            pe.wait_ge(prod_ready, u + 1)
                            for m in range(4):
                                h = 4 * half + m
                                pe.matmul(ps[:, 4 + half, m * P:(m + 1) * P], heads(inv_t)[:, h, :], heads(prod)[:, h, :],
                                          start=True, stop=True)
                                mm = pe.matmul(ps[:, 6 + half, m * P:(m + 1) * P], heads(prod)[:, h, :], heads(inv_t)[:, h, :],
                                               start=True, stop=True)
                            mm.then_inc(step_done, 1)

                def recur(ch):
                    if ch:
                        pe.wait_ge(state_ready, ch)
                    pe.wait_ge(step_ready, (ch + 1) * LEVELS * 2)
                    pe.wait_ge(gram_ready, (ch + 1) * HEADS)
                    for h in range(HEADS):
                        c, rows, cols = h // 2, slice(HD * (h % 2), HD * (h % 2) + HD), slice(h * HD, (h + 1) * HD)
                        x_ps = ps[:, 4 * (h % 2), c * HD:(c + 1) * HD]
                        if ch:
                            pe.matmul(x_ps, pair[rows, c, ch, 0, :], state[rows, c * HD:(c + 1) * HD],
                                      start=True, stop=False)
                        mm = pe.matmul(x_ps, gram[:, h, 256:384], v_tok[:, ch, cols], start=(ch == 0), stop=True)
                    mm.then_inc(x_done, 1)
                    pe.wait_ge(x_ready, ch + 1)
                    for h in range(HEADS):
                        cols = slice(h * HD, (h + 1) * HD)
                        mm = pe.matmul(ps[:, 1, cols], heads(inv_t)[:, h, :], x_sb[:, cols], start=True, stop=True)
                    mm.then_inc(sa_done, 1)
                    pe.wait_ge(sa_ready, ch + 1)
                    for h in range(HEADS):
                        c, rows, cols = h // 2, slice(HD * (h % 2), HD * (h % 2) + HD), slice(h * HD, (h + 1) * HD)
                        o, s = ps[rows, 2, c * P:(c + 1) * P], ps[rows, 3, c * HD:(c + 1) * HD]
                        if ch < NT - 1:
                            pe.matmul(s, key_tok[:, ch, cols], v_tok[:, ch, cols], start=True, stop=False)
                            pe.matmul(s, b_tok[:, ch, cols], sa[:, cols], start=False, stop=True)
                        if ch:
                            pe.matmul(o, state[rows, c * HD:(c + 1) * HD], pair[rows, c, ch, 1, :], start=True, stop=False)
                        pe.matmul(o, v_tok[:, ch, cols], gram[:, h, 384:512], start=(ch == 0), stop=False)
                        mm = pe.matmul(o, sa[:, cols], gram[:, h, 128:256], start=False, stop=True)
                    mm.then_inc(end_done, 1)

                for ch in range(NT):
                    grams(ch)
                    inverse(ch)
                    recur(ch)

            @block.gpsimd
            def _(pool):
                for ch in range(NT):
                    if ch:
                        pool.wait_ge(sa_done, ch)
                    ident = core.c("ident").unsqueeze(1).broadcast_to([P, HEADS, P])
                    pool.tensor_copy(heads(inv), ident)
                    pool.tensor_copy(heads(inv_t), ident).then_inc(units_ready, 1)
                    pool.wait_ge(gram_ready, (ch + 1) * HEADS)
                    for n in range(LEVELS):
                        g = ch * LEVELS + n
                        if g >= 2:
                            pool.wait_ge(prod_done, 2 * (g - 1))
                        pool.tensor_tensor(heads(level[g % 2]), gram[:, :, 0:P],
                                           core.c("level", n * P, P).unsqueeze(1).broadcast_to([P, HEADS, P]), ALU.mult)\
                            .then_inc(level_ready, 1)

            @block.scalar
            def _(act):
                for ch in range(NT):
                    for n in range(LEVELS):
                        for half in range(2):
                            u = (ch * LEVELS + n) * 2 + half
                            act.wait_ge(prod_done, u + 1)
                            act.activation(prod[:, half, :], ps[:, 2 + half, :], ACT.Copy).then_inc(prod_ready, 1)
                    act.wait_ge(x_done, ch + 1)
                    for odd in range(2):
                        ins = act.activation(x_sb.rearrange("p (c n v) -> p c n v", n=2, v=HD)[:, :, odd, :],
                                             ps[:, 4 * odd, 0:256].rearrange("p (c v) -> p c v", v=HD), ACT.Copy)
                    ins.then_inc(x_ready, 1)
                    act.wait_ge(end_done, ch + 1)
                    act.activation(out[:, :, ch * P:(ch + 1) * P], ps[:, 2, :].rearrange("p (c t) -> p c t", t=P), ACT.Copy)\
                       .then_inc(out_ready, 1)

            @block.vector
            def _(dve):
                for ch in range(NT):
                    if ch:
                        dve.wait_ge(end_done, ch)
                        dve.wait_ge(level_ready, ch * LEVELS)
                    for h in range(HEADS):
                        dve.wait_ge(gram_done, ch * HEADS + h + 1)
                        dve.tensor_tensor(gram[:, h, :], ps[:, h % 2, :], core.c("causal4"), ALU.mult).then_inc(gram_ready, 1)
                    dve.wait_ge(units_ready, ch + 1)
                    for n in range(LEVELS):
                        for half in range(2):
                            u = (ch * LEVELS + n) * 2 + half
                            dve.wait_ge(step_done, u + 1)
                            if u >= 2:
                                dve.wait_ge(step_ready, u - 1)
                            dve.tensor_tensor(inv[:, half, :], inv[:, half, :], ps[:, 4 + half, :], ALU.subtract)
                            dve.tensor_tensor(inv_t[:, half, :], inv_t[:, half, :], ps[:, 6 + half, :], ALU.subtract)\
                               .then_inc(step_ready, 1)
                    dve.wait_ge(sa_done, ch + 1)
                    dve.tensor_scalar(sa, ps[:, 1, :], -1.0, None, ALU.mult).then_inc(sa_ready, 1)
                    if ch < NT - 1:
                        dve.wait_ge(end_done, ch + 1)
                        if ch:
                            dve.tensor_tensor(state, state, ps[:, 3, 0:256], ALU.add).then_inc(state_sum, 1)
                        else:
                            dve.tensor_copy(state, ps[:, 3, 0:256]).then_inc(state_sum, 1)
                        dve.wait_ge(state_sum, ch + 1)
                        for c in range(NW):
                            part = state[:, c * HD:(c + 1) * HD]
                            ins = dve.tensor_scalar(part, part, to_end[:, 4 * c + ch:4 * c + ch + 1],
                                                    from_start[:, 4 * c + ch + 1:4 * c + ch + 2], ALU.mult, ALU.mult)
                        ins.then_inc(state_ready, 1)


def time_mix_out_stage(core):
    nc, a = core.nc, core.arena
    out, bonus, gate = a[:, 8:12, :], a[:, 30:34, :], a[:, 46:50, :]
    square, rstd = a[:, 50:54, :], a[:, 54:58, :]
    mean_done, centred = core.sem("to_mean_done"), core.sem("to_centred")
    squared, var_done = core.sem("to_squared"), core.sem("to_var_done")
    steps, rooted = core.sem("to_steps"), core.sem("to_rooted")
    with ExitStack() as ctx:
        ps = ctx.enter_context(nc.psum_tensor("to_ps", [P, 8, T], F32))
        with nc.Block() as block:

            @block.tensor
            def _(pe):
                for c in range(NW):
                    pe.matmul(ps[:, c, :], core.c("head_ones"), out[:, c, :], start=True, stop=True).then_inc(mean_done, 1)
                for c in range(NW):
                    pe.wait_ge(squared, c + 1)
                    pe.matmul(ps[:, 4 + c, :], core.c("head_ones"), square[:, c, :], start=True, stop=True).then_inc(var_done, 1)

            @block.scalar
            def _(act):
                for c in range(NW):
                    act.wait_ge(centred, c + 1)
                    act.activation(square[:, c, :], out[:, c, :], ACT.Square).then_inc(squared, 1)
                for c in range(NW):
                    act.wait_ge(steps, c + 1)
                    act.activation(rstd[:, c, :], rstd[:, c, :], ACT.Sqrt).then_inc(rooted, 1)

            @block.vector
            def _(dve):
                for c in range(NW):
                    dve.wait_ge(mean_done, c + 1)
                    dve.scalar_tensor_tensor(out[:, c, :], ps[:, c, :], -1.0 / HD, out[:, c, :], ALU.mult, ALU.add)\
                       .then_inc(centred, 1)
                for c in range(NW):
                    dve.wait_ge(var_done, c + 1)
                    dve.tensor_scalar(rstd[:, c, :], ps[:, 4 + c, :], 1.0 / HD, GN_EPS, ALU.mult, ALU.add).then_inc(steps, 1)
                n = NW
                for c in range(NW):
                    dve.tensor_scalar(bonus[:, c, :], bonus[:, c, :], core.v("lnx_b", c), None, ALU.add).then_inc(steps, 1)
                n += NW
                for c in range(NW):
                    dve.wait_ge(rooted, c + 1)
                    dve.reciprocal(rstd[:, c, :], rstd[:, c, :]).then_inc(steps, 1)
                    n += 1
                    dve.wait_ge(steps, n)
                    dve.scalar_tensor_tensor(out[:, c, :], out[:, c, :], core.v("lnx_w", c), rstd[:, c, :], ALU.mult, ALU.mult)\
                       .then_inc(steps, 1)
                    n += 1
                    dve.wait_ge(steps, n)
                    dve.tensor_tensor(out[:, c, :], out[:, c, :], bonus[:, c, :], ALU.add).then_inc(steps, 1)
                    n += 1
                    dve.wait_ge(steps, n)
                    dve.tensor_tensor(out[:, c, :], out[:, c, :], gate[:, c, :], ALU.mult)


def pe_gemm_deep(core, pe, n, per_tile, blocks, rhs, ps):
    g0, e0 = core.used, core.evacs
    assert 2 * per_tile % RING == 0 and n % 2 == 0

    def step(i, j, done):
        e = e0 + done + j
        pe.wait_ge(core.banks_free, e + 3 + i * 2)
        for q in range(per_tile):
            g = g0 + (done + j) * per_tile + q
            core.wait_weights(pe, g, i, 2 * per_tile)
            for b in range(blocks):
                k = q * blocks + b
                mm = pe.matmul(ps[:, e % 2, :], core.ring[:, g % RING, b * P:(b + 1) * P], rhs(k),
                               start=(k == 0), stop=(k == per_tile * blocks - 1))
            mm.then_inc(core.groups_done, 1)

    in_turns(pe, n, 2, step)
    core.used += n * per_tile
    core.evacs += n


def gates_stage(core):
    nc, a = core.nc, core.arena
    ys = a[:, 0:12, :]
    open_gate = a[:, 50:53, :]
    part = a[:, 53:55, :]
    g0 = core.used
    pairs_done = core.sem("gt_pairs_done")
    pairs_free = core.sem("gt_pairs_free")
    opened = core.sem("gt_opened")
    summed = core.sem("gt_summed")
    with ExitStack() as ctx:
        ps = ctx.enter_context(nc.psum_tensor("gt_ps", [P, 6, T], F32))
        with nc.Block() as block:

            @block.sync
            def _(sp):
                core.stream(sp, ["gates"])

            @block.tensor
            def _(pe):
                with pe.Fori(0, KD) as d:
                    for m in range(36):
                        n, k = m // 12, m % 12
                        if k == 0:
                            pe.wait_ge(pairs_free, d * 3 + n + 1)
                        g = g0 + m // 9
                        if m % 9 == 0:
                            core.wait_weights(pe, g, d)
                        w = core.ring[:, g % RING, (m % 9) * P:(m % 9 + 1) * P]
                        if k < KD:
                            mm = pe.matmul(ps[:, 2 * n, :], w, core.xn[:, k, :], start=(k == 0), stop=(k == KD - 1))
                        else:
                            mm = pe.matmul(ps[:, 2 * n + 1, :], w, ys[:, 4 * n + k - KD, :], start=(k == KD), stop=(k == 11))
                        if m % 9 == 8:
                            mm.then_inc(core.groups_done, 1)
                        elif k == 11:
                            mm.then_inc(pairs_done, 1)
                core.used += 32

            def wait_pair(eng, d, n):
                if n < 2:
                    eng.wait_ge(pairs_done, 2 * d + n + 1)
                else:
                    eng.wait_ge(core.groups_done, g0 + 4 * d + 4)

            @block.scalar
            def _(act):
                for d in range(KD):
                    for n in range(3):
                        wait_pair(act, d, n)
                        if d:
                            act.wait_ge(pairs_free, 3 + 3 * (d - 1) + n + 1)
                        act.activation(open_gate[:, n, :], ps[:, 2 * n, :], ACT.Sigmoid, bias=core.v("gate_b", 8 * n + d))\
                           .then_inc(opened, 1)

            @block.vector
            def _(dve):
                dve.sem_inc(pairs_free, 3)
                for d in range(KD):
                    for n in range(3):
                        dve.wait_ge(opened, 3 * d + n + 1)
                        wait_pair(dve, d, n)
                        to = core.merged[:, d, :] if n == 0 else part[:, n - 1, :]
                        dve.tensor_tensor(to, open_gate[:, n, :], ps[:, 2 * n + 1, :], ALU.mult).then_inc(pairs_free, 1)
                        if n:
                            dve.wait_ge(pairs_free, 3 + 3 * d + n + 1)
                            if n == 2:
                                dve.wait_ge(summed, 2 * d + 1)
                            dve.tensor_tensor(core.merged[:, d, :], core.merged[:, d, :], to, ALU.add).then_inc(summed, 1)


def residual_stage(core, name, phase, rhs, per_tile=1, n0=0, extra=None):
    nc = core.nc
    g0, e0 = core.used, core.evacs
    with ExitStack() as ctx:
        ps = ctx.enter_context(nc.psum_tensor(name + "_ps", [P, 4, T], F32))
        with nc.Block() as block:

            @block.sync
            def _(sp):
                core.stream(sp, [phase])

            @block.tensor
            def _(pe):
                if per_tile == 1:
                    pe_gemm(core, pe, KD, KD, rhs, ps)
                else:
                    pe_gemm_deep(core, pe, KD, per_tile, PHASES[phase][1], rhs, ps)

            @block.vector
            def _(dve):
                banks = 4 if per_tile == 1 else 2
                for d in range(KD):
                    dve.wait_ge(core.groups_done, g0 + (d + 1) * per_tile)
                    dve.tensor_tensor(core.h[:, d, :], core.h[:, d, :], ps[:, (e0 + d) % banks, :], ALU.add)\
                       .then_inc(core.banks_free, 1)


def load_memory_stage(core):
    mem_in = core.sem("mem_in")
    with core.nc.Block() as block:

        @block.sync
        def _(sp):
            sp.dma_start(memory(core), core.dram["mem_t"]).then_inc(mem_in, 16)
            sp.wait_ge(mem_in, 16)


def memory(core):
    return core.arena[:, 12:16, :].rearrange("p a (n t) -> p (a n) t", n=2)


def cross_projections_stage(core):
    nc, a = core.nc, core.arena
    mem_n = memory(core)
    keys = a[:, 16:20, :].rearrange("p a (n t) -> p (a n) t", n=2)
    values = a[:, 20:24, :]
    queries = a[:, 24:32, :]
    g0, e0 = core.used, core.evacs
    with ExitStack() as ctx:
        ps = ctx.enter_context(nc.psum_tensor("cp_ps", [P, 4, T], F32))
        ps_v = ctx.enter_context(nc.psum_tensor("cp_ps_v", [P, 4, T], F32))
        with nc.Block() as block:

            @block.sync
            def _(sp):
                core.load_weights(sp, "ca", RING, 24)
                core.load_weights(sp, "ca", 24, 24 + RING)
                core.preloaded["ca"] = 24 + RING

            @block.tensor
            def _(pe):
                pe_gemm(core, pe, 8, KD, lambda k: mem_n[:, k, :], ps, MEM)
                for k in range(KD):
                    core.wait_weights(pe, core.used)
                    for i in range(2):
                        for half in range(2):
                            mm = pe.matmul(ps_v[:, 2 * i + half, :], mem_n[:, k, i * P:(i + 1) * P],
                                           core.ring[:, core.used % RING, half * T:(half + 1) * T],
                                           start=(k == 0), stop=(k == KD - 1))
                    mm.then_inc(core.groups_done, 1)
                    core.used += 1
                pe_gemm(core, pe, 8, KD, lambda k: core.xn[:, k, :], ps)

            @block.scalar
            def _(act):
                for n in range(8):
                    act.wait_ge(core.groups_done, g0 + n + 1)
                    act.activation(keys[:, n, :], ps[:, (e0 + n) % 4, 0:MEM], ACT.Copy).then_inc(core.banks_free, 1)
                act.wait_ge(core.groups_done, g0 + 16)
                for n in range(4):
                    act.activation(values[:, n, :], ps_v[:, n, :], ACT.Copy)
                for n in range(8):
                    act.wait_ge(core.groups_done, g0 + 16 + n + 1)
                    act.activation(queries[:, n, :], ps[:, (e0 + 8 + n) % 4, :], ACT.Copy, scale=1.0 / 16)\
                       .then_inc(core.banks_free, 1)


class Unit:

    def __init__(self, scores, n, values, add=None, add_query=None, keep=None, gate=None, first=True, last=True, group=0):
        self.scores, self.n, self.values = scores, n, values
        self.add, self.add_query, self.keep, self.gate = add, add_query, keep, gate
        self.first, self.last, self.group = first, last, group


def attention_stage(core, name, units, take):
    nc, a = core.nc, core.arena
    score_sb, turned_sb, stats = a[:, 45:49, :], a[:, 49:51, :], a[:, 51, :]
    count = len(units)
    scores_done = core.sem(name + "_scores_done")
    biased = core.sem(name + "_biased")
    max_ready = core.sem(name + "_max_ready")
    exp_ready = core.sem(name + "_exp_ready")
    inverse = core.sem(name + "_inverse")
    prob_ready = core.sem(name + "_prob_ready")
    turned = core.sem(name + "_turned")
    turned_ready = core.sem(name + "_turned_ready")
    out_done = core.sem(name + "_out_done")
    taken = core.sem(name + "_taken")
    groups = units[-1].group + 1
    last_of = {g: max(i for i, x in enumerate(units) if x.group == g) for g in range(groups)}
    stat = lambda u, n: stats[:, 4 * (u % 4) + n:4 * (u % 4) + n + 1]
    with ExitStack() as ctx:
        ps = ctx.enter_context(nc.psum_tensor(name + "_ps", [P, 8, T], F32))
        with nc.Block() as block:

            @block.tensor
            def _(pe):
                def scores(u):
                    x = units[u]
                    if u >= 4:
                        pe.wait_ge(exp_ready, u - 3)
                    for n, (lhs, rhs) in enumerate(x.scores):
                        mm = pe.matmul(ps[:, u % 4, 0:x.n], lhs, rhs, start=(n == 0), stop=(n == len(x.scores) - 1))
                    mm.then_inc(scores_done, 1)

                def turn(u):
                    x = units[u]
                    pe.wait_ge(prob_ready, u + 1)
                    if u >= 2:
                        pe.wait_ge(turned_ready, u - 1)
                    for lo in range(0, x.n, P):
                        n = min(P, x.n - lo)
                        mm = pe.transpose(ps[0:n, 4 + u % 2, lo:lo + P], score_sb[:, u % 4, lo:lo + n], core.c("ident"))
                    mm.then_inc(turned, 1)

                def output(u):
                    x = units[u]
                    pe.wait_ge(turned_ready, u + 1)
                    if x.group >= 2:
                        pe.wait_ge(taken, x.group - 1)
                    blocks = (x.n + P - 1) // P
                    for out, lhs, blk in x.values:
                        n = min(P, x.n - blk * P)
                        mm = pe.matmul(ps[out[0], 6 + x.group % 2, out[1]], lhs, turned_sb[0:n, u % 2, blk * P:(blk + 1) * P],
                                       start=(x.first and blk == 0), stop=(x.last and blk == blocks - 1), skip_group_check=True)
                    mm.then_inc(out_done, 1)

                for u in range(min(3, count)):
                    scores(u)
                for u in range(count):
                    if u + 3 < count:
                        scores(u + 3)
                    turn(u)
                    if u:
                        output(u - 1)
                output(count - 1)

            @block.scalar
            def _(act):
                def exps(u):
                    x = units[u]
                    act.wait_ge(max_ready, u + 1)
                    src = ps[:, u % 4, 0:x.n] if x.add is None else score_sb[:, u % 4, 0:x.n]
                    if x.add is None and u >= 4:
                        act.wait_ge(turned, u - 3)
                    act.activation(score_sb[:, u % 4, 0:x.n], src, ACT.Exp, bias=stat(u, 0), accum_out=stat(u, 1))\
                       .then_inc(exp_ready, 1)

                def place(u):
                    x = units[u]
                    act.wait_ge(turned, u + 1)
                    if u >= 2:
                        act.wait_ge(out_done, u - 1)
                    rows = min(P, x.n)
                    width = (x.n + P - 1) // P * P
                    act.activation(turned_sb[0:rows, u % 2, 0:width], ps[0:rows, 4 + u % 2, 0:width], ACT.Copy)\
                       .then_inc(turned_ready, 1)

                exps(0)
                for u in range(count):
                    if u + 1 < count:
                        exps(u + 1)
                    place(u)

            @block.vector
            def _(dve):
                def maxima(u):
                    x = units[u]
                    dve.wait_ge(scores_done, u + 1)
                    src = ps[:, u % 4, 0:x.n]
                    if x.add is not None:
                        if u >= 4:
                            dve.wait_ge(turned, u - 3)
                        dst = score_sb[:, u % 4, 0:x.n]
                        if x.add_query is not None:
                            dve.scalar_tensor_tensor(dst, src, x.add_query, x.add, ALU.add, ALU.add).then_inc(biased, 1)
                        else:
                            dve.tensor_tensor(dst, src, x.add, ALU.add).then_inc(biased, 1)
                        dve.wait_ge(biased, u + 1)
                        src = dst
                    elif u >= 4:
                        dve.wait_ge(exp_ready, u - 3)
                    dve.tensor_reduce(stat(u, 0), src, AX.X, ALU.max, negate=True).then_inc(max_ready, 1)

                def normalize(u):
                    x = units[u]
                    dve.wait_ge(exp_ready, u + 1)
                    dve.reciprocal(stat(u, 2), stat(u, 1)).then_inc(inverse, 1)
                    dve.wait_ge(inverse, u + 1)
                    p = score_sb[:, u % 4, 0:x.n]
                    if x.keep is not None:
                        dve.scalar_tensor_tensor(p, p, stat(u, 2), x.keep, ALU.mult, ALU.mult).then_inc(kept, 1)
                        kept_n[0] += 1
                        dve.wait_ge(kept, kept_n[0])
                        dve.tensor_scalar(p, p, x.gate, None, ALU.mult).then_inc(prob_ready, 1)
                    elif x.gate is not None:
                        dve.tensor_scalar(p, p, stat(u, 2), x.gate, ALU.mult, ALU.mult).then_inc(prob_ready, 1)
                    else:
                        dve.tensor_scalar(p, p, stat(u, 2), None, ALU.mult).then_inc(prob_ready, 1)

                kept, kept_n = (core.sem(name + "_kept") if any(x.keep is not None for x in units) else None), [0]
                for u in range(min(2, count)):
                    maxima(u)
                nxt = 0
                for u in range(count):
                    if u + 2 < count:
                        maxima(u + 2)
                    normalize(u)
                    if nxt < groups and last_of[nxt] <= u - 2:
                        dve.wait_ge(out_done, last_of[nxt] + 1)
                        take(dve, nxt, ps[:, 6 + nxt % 2, :]).then_inc(taken, 1)
                        nxt += 1
                for g in range(nxt, groups):
                    dve.wait_ge(out_done, last_of[g] + 1)
                    take(dve, g, ps[:, 6 + g % 2, :]).then_inc(taken, 1)


def cross_attention_stage(core):
    a = core.arena
    keys = a[:, 16:20, :].rearrange("p a (n t) -> p (a n) t", n=2)
    values = a[:, 20:24, :].rearrange("p (i n) t -> p i (n t)", n=2)
    queries = a[:, 24:32, :]
    units = []
    for h in range(4):
        for pair in range(2):
            for i in (2 * pair, 2 * pair + 1):
                cols = slice(i * P, (i + 1) * P)
                scores = [(queries[:, 2 * h + f, cols], keys[:, 2 * h + f, :]) for f in range(2)]
                vals = []
                for f in range(2):
                    for blk in range(2):
                        lo = f * 2 * P + (i % 2) * P
                        vals.append(((slice(0, P), slice(lo, lo + P)),
                                     values[:, blk, h * 256 + f * P:h * 256 + (f + 1) * P], blk))
                units.append(Unit(scores, MEM, vals, group=2 * h + pair))

    def take(dve, g, bank):
        h, pair = g // 2, g % 2
        return dve.tensor_copy(core.merged[:, 2 * h:2 * h + 2, pair * 256:pair * 256 + 256], bank.rearrange("p (f t) -> p f t", f=2))

    attention_stage(core, "ca", units, take)


def ffn_up_stage(core):
    nc, a = core.nc, core.arena
    hidden, taps = a[:, 12:34, :], a[:, 34:38, :]
    g0, e0 = core.used, core.evacs
    now = core.sem("fu_now")
    steps = core.sem("fu_steps")
    gated = core.sem("fu_gated")
    made = core.sem("fu_made")
    with ExitStack() as ctx:
        ps = ctx.enter_context(nc.psum_tensor("fu_ps", [P, 4, T], F32))
        with nc.Block() as block:

            @block.sync
            def _(sp):
                core.stream(sp, ["up"])

            @block.tensor
            def _(pe):
                pe_gemm(core, pe, 2 * NF, KD, lambda k: core.xn[:, k, :], ps)

            which = lambda n: n // 2 + NF * (n % 2)

            @block.scalar
            def _(act):
                for n in range(2 * NF):
                    act.wait_ge(core.groups_done, g0 + n + 1)
                    if n >= 4:
                        act.wait_ge(made, n // 2 - 1)
                    act.activation(taps[:, n % 4, :], ps[:, (e0 + n) % 4, :], ACT.Identity, scale=core.v("ffn_conv_w", 88 + which(n)),
                                   bias=core.v("ffn_conv_b", which(n))).then_inc(now, 1)
                    if n % 2:
                        act.wait_ge(core.banks_free, 4 + e0 + n)
                        act.activation(taps[:, (n - 1) % 4, :], taps[:, (n - 1) % 4, :], ACT.Silu).then_inc(gated, 1)

            @block.vector
            def _(dve):
                for n in range(2 * NF):
                    y, x = taps[:, n % 4, :], ps[:, (e0 + n) % 4, :]
                    dve.wait_ge(now, n + 1)
                    dve.scalar_tensor_tensor(y[:, 1:T], x[:, 0:T - 1], core.v("ffn_conv_w", 44 + which(n)), y[:, 1:T],
                                             ALU.mult, ALU.add).then_inc(steps, 1)
                    dve.wait_ge(steps, n + 1)
                    dve.scalar_tensor_tensor(y[:, 2:T], x[:, 0:T - 2], core.v("ffn_conv_w", which(n)), y[:, 2:T],
                                             ALU.mult, ALU.add).then_inc(core.banks_free, 1)
                    if n % 2:
                        dve.wait_ge(core.banks_free, 4 + e0 + n + 1)
                        dve.wait_ge(gated, n // 2 + 1)
                        dve.tensor_tensor(hidden[:, n // 2, :], taps[:, (n - 1) % 4, :], y, ALU.mult).then_inc(made, 1)


def bias_stage(core):
    nc, a, dram = core.nc, core.arena, core.dram
    bucket = a[0:32, 49:51, :].rearrange("p a t -> p (a t)")
    table = core.small[0:32, 48:56]
    row = a[0:HEADS, 51:53, :].rearrange("p a t -> p (a t)")
    SPREAD = 896
    spread = a[:, 12:26, :].rearrange("p a t -> p (a t)").rearrange("p (h y) -> p h y", h=HEADS)
    window = a[:, 35:43, :]
    summary = a[:, 43:45, :].rearrange("p a t -> p (a t)")[:, 0:NT * HEADS * NC_CMP]
    mask = a[:, 8, :]
    scratch = nc.dram_tensor("bias_rows", (HEADS * VEC_DIST,), F32)
    bucket_in, table_in, row_out = core.sem("bi_bucket_in"), core.sem("bi_table_in"), core.sem("bi_row_out")
    row_done, row_ready = core.sem("bi_row_done"), core.sem("bi_row_ready")
    spread_in = core.sem("bi_spread_in")
    head_in = core.sem("bi_head_in")
    flipped, cleared = core.sem("bi_flipped"), core.sem("bi_cleared")
    w_taken = core.sem("bi_w_taken")
    with ExitStack() as ctx:
        ps = ctx.enter_context(nc.psum_tensor("bi_ps", [P, 8, T], F32))
        with nc.Block() as block:

            @block.sync
            def _(sp):
                sp.dma_start(bucket, dram["bucket"]).then_inc(bucket_in, 16)
                sp.dma_start(table, dram["table"]).then_inc(table_in, 16)
                sp.dma_start(a[0:HEADS, 9:11, :].rearrange("p a t -> p (a t)"), dram["head_row"]).then_inc(head_in, 16)
                sp.wait_ge(row_ready, 2)
                sp.dma_start(scratch.ap().rearrange("(h y) -> h y", h=HEADS), row).then_inc(row_out, 16)
                sp.wait_ge(row_out, 16)
                sp.dma_start(spread, bass.AP(scratch, 0, [[1, P], [VEC_DIST, HEADS], [1, SPREAD]])).then_inc(spread_in, 16)
                sp.wait_ge(head_in, 16)

            @block.tensor
            def _(pe):
                pe.wait_ge(bucket_in, 16)
                pe.wait_ge(table_in, 16)
                for n in range(2):
                    pe.matmul(ps[0:HEADS, n, :], table, bucket[:, n * T:(n + 1) * T], start=True, stop=True).then_inc(row_done, 1)
                pe.wait_ge(spread_in, 16)
                for h in range(HEADS):
                    if h == 6:
                        pe.wait_ge(w_taken, 2)
                    pe.matmul(ps[:, (2 + h) % 8, :], core.c("flip"), spread[:, h, 0:T], start=True, stop=True).then_inc(flipped, 1)
                pe.wait_ge(w_taken, 4)
                per = HEADS * NC_CMP
                for i in range(NT):
                    lo = 415 - i * P
                    pe.matmul(ps[:, 2 + i // 2, (i % 2) * per:(i % 2 + 1) * per], core.c("flip"),
                              spread[:, :, lo:lo + 16 * (NC_CMP - 1) + 1:16], start=True, stop=True).then_inc(flipped, 1)

            @block.scalar
            def _(act):
                for n in range(2):
                    act.wait_ge(row_done, n + 1)
                    act.activation(row[:, n * T:(n + 1) * T], ps[0:HEADS, n, :], ACT.Copy).then_inc(row_ready, 1)

            @block.vector
            def _(dve):
                dve.memset(mask, 0.0).then_inc(cleared, 1)
                dve.wait_ge(cleared, 1)
                dve.tensor_copy(mask[:, T - P:T], core.c("causal_add")).then_inc(cleared, 1)
                dve.wait_ge(cleared, 2)
                dve.wait_ge(row_ready, 2)
                for h in range(HEADS):
                    dve.wait_ge(flipped, h + 1)
                    dve.tensor_tensor(window[:, h, :], ps[:, (2 + h) % 8, :], mask, ALU.add).then_inc(w_taken, 1)
                half = NT * HEADS * NC_CMP // 2
                for n in range(2):
                    dve.wait_ge(flipped, HEADS + 2 * n + 2)
                    view = lambda x: x.rearrange("p (i h b) -> p i h b", i=2, h=HEADS)
                    mask_add = core.c("cmp_add", 2 * n * NC_CMP, 2 * NC_CMP).rearrange("p (i b) -> p i b", i=2)
                    dve.tensor_tensor(view(summary[:, n * half:(n + 1) * half]), view(ps[:, 2 + n, 0:half]),
                                      mask_add.unsqueeze(2).broadcast_to([P, 2, HEADS, NC_CMP]), ALU.add)


def second_projections_stage(core):
    nc, a, dram = core.nc, core.arena, core.dram
    by_feature = a[:, 12:28, :]
    fox_value = a[:, 28:32, :]
    group_value = a[:, 32:34, :].rearrange("p a (n t) -> p (a n) t", n=2)
    logits = a[:, 34, 0:NT * 32].rearrange("p (i n) -> p i n", i=NT)
    small_w = a[:, 11, 0:KD * 32].rearrange("p (k n) -> p k n", k=KD)
    g0, e0 = core.used, core.evacs
    small_in = core.sem("sp_small_in")
    small_done = core.sem("sp_small_done")
    fox_taken = core.sem("sp_fox_taken")
    with ExitStack() as ctx:
        ps = ctx.enter_context(nc.psum_tensor("sp_ps", [P, 4, T], F32))
        ps_v = ctx.enter_context(nc.psum_tensor("sp_ps_v", [P, 4, T], F32))
        with nc.Block() as block:

            @block.sync
            def _(sp):
                core.stream(sp, ["in2"])

            @block.tensor
            def _(pe):
                pe_gemm(core, pe, 16, KD, lambda k: core.xn[:, k, :], ps)
                for g in range(4):
                    core.wait_weights(pe, core.used)
                    for half in range(2):
                        k = 2 * g + half
                        for i in range(NT):
                            mm = pe.matmul(ps_v[:, i, :], core.xn[:, k, i * P:(i + 1) * P],
                                           core.ring[:, core.used % RING, half * T:(half + 1) * T],
                                           start=(k == 0), stop=(k == KD - 1))
                    mm.then_inc(core.groups_done, 1)
                    core.used += 1
                pe.wait_ge(core.banks_free, 4 + e0 + 16)
                for g in range(2):
                    core.wait_weights(pe, core.used)
                    for quarter in range(4):
                        k = 4 * g + quarter
                        for i in range(NT):
                            mm = pe.matmul(ps[:, i, 0:256], core.xn[:, k, i * P:(i + 1) * P],
                                           core.ring[:, core.used % RING, quarter * 256:(quarter + 1) * 256],
                                           start=(k == 0), stop=(k == KD - 1))
                    mm.then_inc(core.groups_done, 1)
                    core.used += 1
                pe.wait_ge(small_in, 16)
                pe.wait_ge(fox_taken, NT)
                for i in range(NT):
                    for k in range(KD):
                        mm = pe.matmul(ps_v[:, 0, i * 32:(i + 1) * 32], core.xn[:, k, i * P:(i + 1) * P], small_w[:, k, :],
                                       start=(k == 0), stop=(k == KD - 1))
                mm.then_inc(small_done, 1)

            @block.scalar
            def _(act):
                act.dma_start(small_w.rearrange("p k n -> p (k n)"), dram["w_small2"]).then_inc(small_in, 16)
                for n in range(16):
                    scale = HD ** -0.5 if n < 4 or 8 <= n < 12 else 1.0
                    act.wait_ge(core.groups_done, g0 + n + 1)
                    act.activation(by_feature[:, n, :], ps[:, (e0 + n) % 4, :], ACT.Copy, scale=scale).then_inc(core.banks_free, 1)
                act.wait_ge(core.groups_done, g0 + 20)
                for i in range(NT):
                    act.activation(fox_value[:, i, :], ps_v[:, i, :], ACT.Copy).then_inc(fox_taken, 1)
                act.wait_ge(core.groups_done, g0 + 22)
                for i in range(NT):
                    act.activation(group_value[:, i, :], ps[:, i, 0:256], ACT.Copy)
                act.wait_ge(small_done, 1)
                act.activation(logits, ps_v[:, 0, 0:NT * 32].rearrange("p (i n) -> p i n", i=NT), ACT.Copy)
                act.wait_ge(small_in, 16)


def forget_stage(core):
    nc, a = core.nc, core.arena
    logits = a[:, 34, 0:NT * 32].rearrange("p (i n) -> p i n", i=NT)
    gates = a[:, 34, 128:128 + NT * 24].rearrange("p (i n) -> p i n", i=NT)
    x = a[:, 34, 256:288].rearrange("p (i n) -> p i n", i=NT)
    soft = a[:, 34, 288:320].rearrange("p (i n) -> p i n", i=NT)
    row = a[0:HEADS, 11, :]
    sums = core.small[:, 0:32].rearrange("p (i n) -> p i n", i=NT)
    shifted, logged, steps = core.sem("fg_shifted"), core.sem("fg_logged"), core.sem("fg_steps")
    soft_ready, summed = core.sem("fg_soft_ready"), core.sem("fg_summed")
    with ExitStack() as ctx:
        ps = ctx.enter_context(nc.psum_tensor("fg_ps", [P, 2, T], F32))
        with nc.Block() as block:

            @block.vector
            def _(dve):
                bias = core.vec[:, VEC_AT["b_forget"]:VEC_AT["b_forget"] + 8].unsqueeze(1).broadcast_to([P, NT, 8])
                dve.tensor_tensor(x, logits[:, :, 0:8], bias, ALU.add).then_inc(shifted, 1)
                dve.wait_ge(shifted, 1)
                dve.wait_ge(logged, 3)
                dve.tensor_scalar(x, x, -1.0, 0.0, ALU.mult, ALU.max).then_inc(steps, 1)
                dve.wait_ge(steps, 1)
                dve.tensor_tensor(soft, soft, x, ALU.add).then_inc(soft_ready, 1)
                dve.wait_ge(summed, 1)
                dve.tensor_scalar(sums, ps[:, 0, 0:32].rearrange("p (i n) -> p i n", i=NT), -1.0, None, ALU.mult)

            @block.scalar
            def _(act):
                act.wait_ge(shifted, 1)
                act.activation(soft, x, ACT.Abs).then_inc(logged, 1)
                act.wait_ge(logged, 1)
                act.activation(soft, soft, ACT.Exp, scale=-1.0).then_inc(logged, 1)
                act.wait_ge(logged, 2)
                act.activation(soft, soft, ACT.Ln, bias=1.0).then_inc(logged, 1)
                act.activation(gates, logits[:, :, 8:32], ACT.Sigmoid)
                act.wait_ge(summed, 1)
                act.activation(row, ps[0:HEADS, 1, :], ACT.Copy)

            @block.tensor
            def _(pe):
                pe.wait_ge(soft_ready, 1)
                for i in range(NT):
                    for j in range(i + 1):
                        pe.matmul(ps[:, 0, i * 8:(i + 1) * 8], core.c("upper" if j == i else "ones"), soft[:, j, :],
                                  start=(j == 0), stop=(j == i))
                for i in range(NT):
                    for j in range(i + 1):
                        mm = pe.matmul(ps[0:HEADS, 1, i * P:(i + 1) * P], soft[:, j, :], core.c("upper" if j == i else "ones"),
                                       start=(j == 0), stop=(j == i))
                mm.then_inc(summed, 1)


def compress_stage(core):
    nc, a, dram = core.nc, core.arena, core.dram
    B = NC_CMP
    shifted = a[:, 53:57, :].rearrange("p (s g) t -> p s g t", s=2)
    w1 = [core.merged[:].rearrange("p a t -> p (a t)").rearrange("p (l m) -> p l m", l=16),
          a[:, 45:53, :].rearrange("p a t -> p (a t)").rearrange("p (l m) -> p l m", l=16)]
    w2 = a[:, 59, 0:256].rearrange("p (s f d) -> p s f d", s=2, f=2)
    w2_k = a[:, 59, 256:512].rearrange("p (f d) -> p f d", f=2)
    hidden = a[:, 57, 0:8 * B].rearrange("p (s f n) -> p s f n", s=2, f=2)
    bias = a[:, 57, 256:260].rearrange("p (s f) -> p s f", s=2)
    keys, values = a[:, 58, 0:B], a[0:B, 58, 128:256]
    w1_in = [core.sem("cm_w1_k_in"), core.sem("cm_w1_v_in")]
    w2_in = [core.sem("cm_w2_k_in"), core.sem("cm_w2_v_in")]
    shift_in = [core.sem(f"cm_shift_in{n}") for n in range(4)]
    copied, pos_done, pos_ready = core.sem("cm_copied"), core.sem("cm_pos_done"), core.sem("cm_pos_ready")
    hidden_done, hidden_ready, out_done = core.sem("cm_hidden_done"), core.sem("cm_hidden_ready"), core.sem("cm_out_done")
    with ExitStack() as ctx:
        ps = ctx.enter_context(nc.psum_tensor("cm_ps", [P, 8, T], F32))
        with nc.Block() as block:

            @block.sync
            def _(sp):
                for s, name in enumerate("kv"):
                    sp.dma_start(w1[s], dram["cmp_w1_" + name]).then_inc(w1_in[s], 16)
                    sp.dma_start(w2[:, s], dram["cmp_w2_" + name]).then_inc(w2_in[s], 16)
                for s in range(2):
                    src = a[:, 24 + s, :]
                    for g in range(2):
                        rows = slice(HD * g, HD * g + HD)
                        sp.dma_start(shifted[HD:P, s, g, 0:T - 1], src[rows, 1:T]).then_inc(shift_in[2 * s + g], 16)
                for n in range(4):
                    sp.wait_ge(shift_in[n], 16)

            @block.gpsimd
            def _(pool):
                for s in range(2):
                    for g in range(2):
                        ins = pool.tensor_copy(shifted[0:HD, s, g, 0:T - 1], a[HD * g:HD * g + HD, 24 + s, 0:T - 1])
                ins.then_inc(copied, 1)

            @block.tensor
            def _(pe):
                pe.wait_ge(copied, 1)
                for s in range(2):
                    pe.wait_ge(w1_in[s], 16)
                    at_pe = VEC_AT["pe_" + "kv"[s]]
                    for f in range(2):
                        for l in range(16):
                            mm = pe.matmul(ps[:, 4 * s + f, 0:1], w1[s][:, l, f * P:(f + 1) * P], core.vec[:, at_pe + l:at_pe + l + 1],
                                           start=(l == 0), stop=(l == 15))
                        mm.then_inc(pos_done, 1)
                    pe.wait_ge(shift_in[2 * s], 16)
                    pe.wait_ge(shift_in[2 * s + 1], 16)
                    for f in range(2):
                        for l in range(16):
                            mm = pe.matmul(ps[:, 4 * s + 2 + f, 0:2 * B], w1[s][:, l, f * P:(f + 1) * P],
                                           shifted[:, s, :, 2 * l:2 * l + 16 * (B - 1) + 1:16], start=(l == 0), stop=(l == 15))
                        mm.then_inc(hidden_done, 1)
                pe.wait_ge(hidden_ready, 4)
                pe.wait_ge(w2_in[0], 16)
                pe.wait_ge(w2_in[1], 16)
                pe.wait_ge(pos_ready, 4)
                for g in range(2):
                    for f in range(2):
                        pe.matmul(ps[HD * g:HD * g + HD, 0, 0:B], w2[:, 0, f, :], hidden[:, 0, f, g * B:(g + 1) * B],
                                  start=(f == 0), stop=(f == 1))
                for g in range(2):
                    for f in range(2):
                        mm = pe.matmul(ps[0:B, 1, g * HD:(g + 1) * HD], hidden[:, 1, f, g * B:(g + 1) * B], w2[:, 1, f, :],
                                       start=(f == 0), stop=(f == 1))
                mm.then_inc(out_done, 1)

            @block.vector
            def _(dve):
                for n in range(4):
                    dve.wait_ge(pos_done, n + 1)
                    dve.tensor_copy(bias[:, n // 2, n % 2:n % 2 + 1], ps[:, 4 * (n // 2) + n % 2, 0:1]).then_inc(pos_ready, 1)
                dve.wait_ge(out_done, 1)
                dve.tensor_copy(keys, ps[:, 0, 0:B])
                dve.tensor_copy(values, ps[0:B, 1, 0:P])

            @block.scalar
            def _(act):
                for n in range(4):
                    act.wait_ge(hidden_done, n + 1)
                    act.wait_ge(pos_ready, n + 1)
                    act.activation(hidden[:, n // 2, n % 2, :], ps[:, 4 * (n // 2) + 2 + n % 2, 0:2 * B], ACT.Silu,
                                   bias=bias[:, n // 2, n % 2:n % 2 + 1]).then_inc(hidden_ready, 1)


def fox_attention_stage(core):
    a = core.arena
    query, key, value = a[:, 12:16, :], a[:, 16:20, :], a[:, 28:32, :]
    head_row = a[0:HEADS, 9:11, :].rearrange("p a t -> p (a t)")
    row, mask = a[0:HEADS, 11, :], a[:, 8, :]
    units = []
    for h in range(HEADS):
        c, rows = h // 2, slice(HD * (h % 2), HD * (h % 2) + HD)
        for i in range(NT):
            n = (i + 1) * P
            cols = slice(i * P, (i + 1) * P)
            scores = [(query[rows, c, cols], key[rows, c, 0:n]), (head_row[:, h * P:(h + 1) * P], row[:, 0:n])]
            vals = [((rows, cols), value[:, j, h * HD:(h + 1) * HD], j) for j in range(i + 1)]
            units.append(Unit(scores, n, vals, add=mask[:, T - n:T], add_query=core.small[:, i * 8 + h:i * 8 + h + 1], group=c))
    attention_stage(core, "fox", units, lambda dve, g, bank: dve.tensor_copy(a[:, g, :], bank))


def sparse_attention_stage(core):
    a = core.arena
    query, select_key, window_key = a[:, 20:24, :], a[:, 26, :], a[:, 27, :]
    group_value = a[:, 32:34, :].rearrange("p a (n t) -> p (a n) t", n=2)
    gates = a[:, 34, 128:128 + NT * 24]
    window = a[:, 35:43, :]
    summary = a[:, 43:45, :].rearrange("p a t -> p (a t)")[:, 0:NT * HEADS * NC_CMP]
    cmp_key, cmp_value = a[:, 58, 0:NC_CMP], a[0:NC_CMP, 58, 128:256]
    units = []
    for h2 in range(HEADS):
        h, c, rows = h2, h2 // 2, slice(HD * (h2 % 2), HD * (h2 % 2) + HD)
        g = h // 4
        q_rows = slice(HD * g, HD * g + HD)
        for i in range(NT):
            n = (i + 1) * P
            cols = slice(i * P, (i + 1) * P)
            q = query[q_rows, h % 4, cols]
            gate = lambda b: gates[:, i * 24 + 3 * h + b:i * 24 + 3 * h + b + 1]
            for b, k in ((1, select_key), (2, window_key)):
                lo = P * (b - 1) + g * HD
                vals = [((rows, cols), group_value[:, j, lo:lo + HD], j) for j in range(i + 1)]
                units.append(Unit([(q, k[q_rows, 0:n])], n, vals, add=window[:, h, T - n:T], gate=gate(b), first=(b == 1),
                                  last=False, group=c))
            add = summary[:, (i * HEADS + h) * NC_CMP:(i * HEADS + h + 1) * NC_CMP]
            units.append(Unit([(q, cmp_key[q_rows, :])], NC_CMP, [((rows, cols), cmp_value[:, g * HD:(g + 1) * HD], 0)], add=add,
                              keep=core.c("cmp_keep", i * NC_CMP, NC_CMP), gate=gate(0), first=False, last=True, group=c))
    attention_stage(core, "nsa", units, lambda dve, g, bank: dve.tensor_copy(a[:, 4 + g, :], bank))


def second_gates_stage(core):
    nc, a = core.nc, core.arena
    ys = a[:, 0:8, :]
    opened_gate, part = a[:, 50:52, :], a[:, 53, :]
    g0 = core.used
    tiles_free = core.sem("g2_tiles_free")
    opened, summed = core.sem("g2_opened"), core.sem("g2_summed")
    branch_done = core.sem("g2_branch_done")
    with ExitStack() as ctx:
        ps = ctx.enter_context(nc.psum_tensor("g2_ps", [P, 8, T], F32))
        with nc.Block() as block:

            @block.sync
            def _(sp):
                core.stream(sp, ["gates2"])

            @block.tensor
            def _(pe):
                with pe.Fori(0, KD // 4) as turn:
                    for q in range(4):
                        bank = 4 * (q % 2)
                        pe.wait_ge(tiles_free, turn * 4 + q + 1)
                        for n in range(3):
                            g = g0 + 3 * q + n
                            core.wait_weights(pe, g, turn, 12)
                            for b in range(KD):
                                w = core.ring[:, g % RING, b * P:(b + 1) * P]
                                if n < 2:
                                    mm = pe.matmul(ps[:, bank + n, :], w, core.xn[:, b, :], start=(b == 0), stop=(b == KD - 1))
                                else:
                                    mm = pe.matmul(ps[:, bank + 2 + b // 4, :], w, ys[:, b, :], start=(b % 4 == 0), stop=(b % 4 == 3))
                            mm.then_inc(core.groups_done, 1)
                core.used += 24

            @block.scalar
            def _(act):
                for d in range(KD):
                    for n in range(2):
                        act.wait_ge(core.groups_done, g0 + 3 * d + n + 1)
                        if d:
                            act.wait_ge(tiles_free, 2 + d)
                        act.activation(opened_gate[:, n, :], ps[:, 4 * (d % 2) + n, :], ACT.Sigmoid).then_inc(opened, 1)

            @block.vector
            def _(dve):
                dve.sem_inc(tiles_free, 2)
                for d in range(KD):
                    dve.wait_ge(core.groups_done, g0 + 3 * d + 3)
                    dve.wait_ge(opened, 2 * d + 2)
                    if d:
                        dve.wait_ge(summed, d)
                    dve.tensor_tensor(part, opened_gate[:, 1, :], ps[:, 4 * (d % 2) + 3, :], ALU.mult).then_inc(branch_done, 1)
                    dve.tensor_tensor(core.merged[:, d, :], opened_gate[:, 0, :], ps[:, 4 * (d % 2) + 2, :], ALU.mult)\
                       .then_inc(tiles_free, 1)
                    dve.wait_ge(branch_done, d + 1)
                    dve.wait_ge(tiles_free, 2 + d + 1)
                    dve.tensor_tensor(core.merged[:, d, :], core.merged[:, d, :], part, ALU.add).then_inc(summed, 1)


def ff1_stage(core):
    nc = core.nc
    hidden, part = core.arena[:, 0:32, :], core.arena[:, 32:34, :]
    g0, e0 = core.used, core.evacs
    lifted = core.sem("f1_lifted")
    with ExitStack() as ctx:
        ps = ctx.enter_context(nc.psum_tensor("f1_ps", [P, 4, T], F32))
        with nc.Block() as block:

            @block.sync
            def _(sp):
                core.stream(sp, ["ff1"])

            @block.tensor
            def _(pe):
                pe_gemm(core, pe, NFF, KD, lambda k: core.xn[:, k, :], ps)

            @block.vector
            def _(dve):
                for n in range(NFF):
                    bank = ps[:, (e0 + n) % 4, :]
                    dve.wait_ge(core.groups_done, g0 + n + 1)
                    dve.tensor_scalar(part[:, n % 2, :], bank, 0.0, None, ALU.max).then_inc(lifted, 1)
                    dve.wait_ge(lifted, n + 1)
                    dve.tensor_tensor(hidden[:, n, :], part[:, n % 2, :], bank, ALU.mult).then_inc(core.banks_free, 1)


def store_stage(core):
    out_stored = core.sem("out_stored")
    with core.nc.Block() as block:

        @block.sync
        def _(sp):
            sp.dma_start(core.dram["out"], core.merged[:]).then_inc(out_stored, 16)
            sp.wait_ge(out_stored, 16)


def norm_h(name, gain):
    return lambda core: norm_stage(core, name, lambda k: core.h[:, k, :], gain, lambda k: core.xn[:, k, :])


def norm_memory(core):
    norm_stage(core, "nmem", lambda k: memory(core)[:, k, :], "norm_mem", lambda k: memory(core)[:, k, :], MEM)


FIRST = [
    setup_stage,
    norm_h("nmix", "norm_mix"),
    proj_stage,
    stick_breaking_stage,
    time_mix_stage,
    time_mix_scale_stage,
    time_mix_chunks_stage,
    time_mix_out_stage,
    gates_stage,
    lambda core: residual_stage(core, "mix", "mix", lambda k: core.merged[:, k, :]),
    load_memory_stage,
    norm_memory,
    norm_h("nca", "norm_ca"),
    cross_projections_stage,
    cross_attention_stage,
    lambda core: residual_stage(core, "cawo", "ca", lambda k: core.merged[:, k, :]),
    norm_h("nffn", "norm_ffn"),
    ffn_up_stage,
    lambda core: residual_stage(core, "down", "down", lambda k: core.arena[:, 12 + k, :], per_tile=2),
    lambda core: norm_stage(core, "nfirst", lambda k: core.h[:, k, :], "norm_final", lambda k: core.h[:, k, :]),
]

SECOND = [
    norm_h("nattn", "g_attn_2"),
    bias_stage,
    second_projections_stage,
    forget_stage,
    compress_stage,
    fox_attention_stage,
    sparse_attention_stage,
    second_gates_stage,
    lambda core: residual_stage(core, "out2", "out2", lambda k: core.merged[:, k, :]),
    norm_h("nmlp", "g_mlp_2"),
    ff1_stage,
    lambda core: residual_stage(core, "ff2", "ff2", lambda k: core.arena[:, k, :], per_tile=4),
    lambda core: norm_stage(core, "nfinal", lambda k: core.h[:, k, :], "g_final_2", lambda k: core.merged[:, k, :]),
    store_stage,
]
STAGES = FIRST + [clear_semaphores_stage] + SECOND


def hybrid_decoder_kernel(nc, dram, stages):
    with ExitStack() as ctx:
        core = Core(nc, ctx, dram)
        for stage in stages:
            stage(core)



def _tiles(w):
    k, n = w.shape
    return w.reshape(k // P, P, n // P, P).transpose(2, 1, 0, 3).reshape(n // P, P, k)


def _by_rows(w, per):
    k, n = w.shape
    return w.reshape(k // (per * P), per, P, n).transpose(0, 2, 1, 3).reshape(k // (per * P), P, per * n)


def _columns(v):
    return v.reshape(-1, P).T


def _constants():
    c = {name: np.zeros((P, cols), np.float32) for name, cols in CONSTS}
    i = np.arange(P)
    row, col = i[:, None], i[None, :]
    c["ident"][:] = row == col
    c["ones"][:] = 1.0
    c["head_ones"][:] = row // HD == col // HD
    c["upper"][:] = row <= col
    c["causal4"][:] = np.concatenate([row < col, row <= col, row < col, row <= col], axis=1)
    c["neg_tri"][:] = -1.0 * (row >= col)
    c["neg_ones"][:] = -1.0
    c["neg_diag_t"][:] = np.where(row < col, 0.0, NEG)
    for n in range(7):
        b = 1 << n
        c["level"][:, n * P:(n + 1) * P] = (col // b % 2 == 1) & (row // b == col // b - 1)
    c["flip"][:] = row + col == P - 1
    c["causal_add"][:] = np.where(col <= row, 0.0, NEG)
    for t in range(NT):
        for b in range(NC_CMP):
            ok = 16 * b + 31 <= t * P + i
            c["cmp_add"][:, t * NC_CMP + b] = np.where(ok, 0.0, NEG)
            c["cmp_keep"][:, t * NC_CMP + b] = ok
    return np.concatenate([c[name] for name, _ in CONSTS], axis=1)


def _bucket_rows():
    dist = np.maximum(511 - np.arange(VEC_DIST), 0)
    exact = 16
    nf = np.maximum(dist, exact).astype(np.float32)
    log_b = exact + (np.log(nf / np.float32(exact)) / np.float32(math.log(128 / exact)) * np.float32(32 - exact)).astype(np.int32)
    bucket = np.where(dist < exact, dist, np.minimum(log_b, 31))
    return (np.arange(32)[:, None] == bucket[None, :]).astype(np.float32)


def _layout(i):
    f = lambda name: np.asarray(i[name])[0]
    w_comb, w_in = f("w_comb"), f("w_in_2")
    a = {}
    a["x_t"] = np.asarray(i["x"])[0].T.reshape(KD, P, T).transpose(1, 0, 2)
    a["mem_t"] = np.asarray(i["mem"])[0].T.reshape(KD, P, MEM).transpose(1, 0, 2)
    conv, sb, gate, rwkv = w_comb[:, 0:1536], w_comb[:, 1536:3072], w_comb[:, 3072:6144], w_comb[:, 6144:]
    ct = _tiles(conv)
    order = [x for t in range(4) for x in (4 + t, 8 + t, t)]
    a["w_proj"] = np.concatenate([_tiles(rwkv), ct[order], _tiles(sb[:, 0:1024]), _by_rows(sb[:, 1024:], 2)])
    gt = _tiles(gate).reshape(3, 8, P, 1024)
    bt = np.stack([_tiles(f("branch_proj")[n]) for n in range(3)])
    both = np.concatenate([gt, bt], axis=3)
    a["w_gates"] = both.transpose(1, 2, 0, 3).reshape(8, P, 4, 9 * P).transpose(0, 2, 1, 3).reshape(32, P, 9 * P)
    a["w_mix"] = _tiles(f("w_mix_out"))
    kv = f("ca_wkv")
    a["w_ca"] = np.concatenate([_tiles(kv[:, 0:1024]), _by_rows(kv[:, 1024:], 1), _tiles(f("ca_wq")), _tiles(f("ca_wo"))])
    up = _tiles(f("ffn_up"))
    a["w_up"] = up[[x for t in range(NF) for x in (t, NF + t)]]
    a["w_down"] = _tiles(f("ffn_down")).reshape(8, P, 2, 11 * P).transpose(0, 2, 1, 3).reshape(16, P, 11 * P)
    cuts = np.cumsum((512, 512, 512, 8, 512, 128, 128, 128, 128, 128, 128, 24, 1024, 1024))[:-1]
    fq, fk, fv, fl, nq, kc, vc, ksl, vsl, kwn, vwn, ng, ga, gb = np.split(w_in, cuts, axis=1)
    nq = nq.reshape(D, 2, 4, HD).transpose(0, 2, 1, 3).reshape(D, 512)
    a["w_in2"] = np.concatenate([_tiles(np.concatenate([fq, fk, nq, kc, vc, ksl, kwn], axis=1)), _by_rows(fv, 2),
                                 _by_rows(np.concatenate([vsl, vwn], axis=1), 4)])
    a["w_small2"] = _by_rows(np.concatenate([fl, ng], axis=1), 8)[0]
    bf, bn = _tiles(f("w_br_fox_2")), _tiles(f("w_br_nsa_2"))
    a["w_gates2"] = np.stack([_tiles(ga), _tiles(gb), np.concatenate([bf, bn], axis=2)], axis=1).reshape(24, P, 1024)
    a["w_out2"] = _tiles(f("w_out_2"))
    a["w_ff1"] = _tiles(f("w_ff1_2"))
    a["w_ff2"] = _tiles(f("w_ff2_2")).reshape(8, P, 4, 1024).transpose(0, 2, 1, 3).reshape(32, P, 1024)
    a["wa_lora"] = np.concatenate([f("w_lora"), f("a_lora")])
    a["g_lora_t"] = f("g_lora")
    a["table"] = np.asarray(i["rel_bias_table_2"])
    for s in "kv":
        a["cmp_w1_" + s] = f(f"cmp_w1_{s}_2").reshape(16, P, 256).transpose(1, 0, 2)
        a["cmp_w2_" + s] = f(f"cmp_w2_{s}_2").reshape(2, P, HD).transpose(1, 0, 2)
    vec = {
        "norm_mix": i["norm_mix"], "conv_w": i["conv_w"], "mu_rwkv": i["mu_rwkv"], "w0": i["w0"], "a0": i["a0"],
        "k_k": i["k_k"], "k_a": i["k_a"], "r_k": i["r_k"], "lnx_w": i["lnx_w"], "lnx_b": i["lnx_b"],
        "gate_b": i["gate_b"], "norm_ca": i["norm_ca"], "norm_mem": i["norm_mem"], "norm_ffn": i["norm_ffn"],
        "ffn_conv_w": i["ffn_conv_w"], "ffn_conv_b": i["ffn_conv_b"], "norm_final": i["norm_final"],
        "g_attn_2": i["g_attn_2"], "g_mlp_2": i["g_mlp_2"], "g_final_2": i["g_final_2"],
        "pe_k": i["cmp_pe_k_2"], "pe_v": i["cmp_pe_v_2"],
    }
    cols = {name: _columns(np.asarray(v)) for name, v in vec.items()}
    cols["b_forget"] = np.broadcast_to(f("b_forget_2"), (P, 8))
    a["vec"] = np.concatenate([cols[name] for name, _ in VECS], axis=1)
    a["const"] = _constants()
    a["bucket"] = _bucket_rows()
    a["head_row"] = np.repeat(np.eye(HEADS, dtype=np.float32), P, axis=1)
    return {name: np.ascontiguousarray(v) for name, v in a.items()}


def kernel(**inputs):
    import concourse.bacc as bacc
    from concourse.bass_utils import run_bass_kernel_spmd

    arrays = _layout(inputs)
    nc = bacc.Bacc("TRN2", target_bir_lowering=False, num_devices=1)
    dram = {n: nc.dram_tensor(n, a.shape, mybir.dt.from_np(a.dtype), kind="ExternalInput").ap() for n, a in arrays.items()}
    dram["out"] = nc.dram_tensor("out", (P, KD, T), F32, kind="ExternalOutput").ap()
    hybrid_decoder_kernel(nc, dram, STAGES)
    r = run_bass_kernel_spmd(nc, [arrays], core_ids=[0])
    return r.results[0]["out"].transpose(1, 0, 2).reshape(1, D, T).transpose(0, 2, 1)
```

```python
import math
from contextlib import ExitStack

import numpy as np

import concourse.bass as bass
from concourse import mybir

P = 128
T = 512
NT = T // P
D = 1024
KD = D // P
MEM = 256
W = 512
NW = W // P
F = 2816
NF = F // P

HD = 64
HEADS = 8
RING = 4
SLOT = 11 * P
TILES = 71
XN_HI, XN_LO = 55, 63
NC_CMP = (T - 32) // 16 + 1
VEC_DIST = 1024
DECAY = math.exp(-0.5)
RMS_EPS = 1e-6
GN_EPS = 64e-5
NEG = -1e30

ALU = mybir.AluOpType
ACT = mybir.ActivationFunctionType
AX = mybir.AxisListType
F32 = mybir.dt.float32
F32R = mybir.dt.float32r

PHASES = {
    "proj": (38, 8),
    "gates": (32, 9),
    "mix": (8, 8),
    "ca": (32, 8),
    "up": (44, 8),
    "down": (16, 11),
    "in2": (22, 8),
    "gates2": (24, 8),
    "out2": (8, 8),
    "ff1a": (16, 8),
    "ff2a": (16, 8),
    "ff1b": (16, 8),
    "ff2b": (16, 8),
}

VECS = [
    ("norm_mix", 8), ("conv_w", 12), ("mu_rwkv", 14), ("w0", 4), ("a0", 4), ("k_k", 4), ("k_a", 4), ("r_k", 4),
    ("lnx_w", 4), ("lnx_b", 4), ("gate_b", 24), ("norm_ca", 8), ("norm_mem", 8), ("norm_ffn", 8),
    ("ffn_conv_w", 132), ("ffn_conv_b", 44), ("norm_final", 8), ("g_attn_2", 8), ("g_mlp_2", 8), ("g_final_2", 8),
    ("pe_k", 16), ("pe_v", 16), ("b_forget", 8),
]
VEC_AT = {}
_n = 0
for _name, _cols in VECS:
    VEC_AT[_name] = _n
    _n += _cols
N_VEC = _n

CONSTS = [
    ("ident", 128), ("ones", 128), ("head_ones", 128), ("upper", 128), ("causal4", 512), ("neg_tri", 128),
    ("neg_ones", 128), ("neg_diag_t", 128), ("level", 896), ("flip", 128),
    ("causal_add", 128), ("cmp_add", 124), ("cmp_keep", 124),
]
CONST_AT = {}
_n = 0
for _name, _cols in CONSTS:
    CONST_AT[_name] = _n
    _n += _cols
N_CONST = _n


class Core:

    def __init__(self, nc, ctx, dram):
        self.nc, self.dram = nc, dram
        sb = lambda name, shape, dt=F32: ctx.enter_context(nc.sbuf_tensor(name, shape, dt))
        self.vec = sb("vec_sb", [P, N_VEC])
        self.const = sb("const_sb", [P, N_CONST])
        self.small = sb("small", [P, 64])
        self.h = sb("h", [P, KD, T])
        self.raw = sb("weights_raw", [P, 2, SLOT])
        self.w_hi = sb("weights_hi", [P, 2, SLOT], F32R)
        self.w_lo = sb("weights_lo", [P, 2, SLOT], F32R)
        base = nc.sbuf_base
        self.arena = sb("arena", [P, TILES, T])
        self.parts = [nc.alloc_sbuf_tensor_at(f"arena_parts_{i}", [P, min(8, TILES - i), T], F32R, offset=base + i * T * 4)
                      for i in range(0, TILES, 8)]
        self.weights_in = [nc.alloc_semaphore(f"weights_in{s}") for s in range(2)]
        self.hi_ready = nc.alloc_semaphore("weights_hi_ready")
        self.lo_ready = nc.alloc_semaphore("weights_lo_ready")
        self.groups_done = nc.alloc_semaphore("groups_done")
        self.banks_free = nc.alloc_semaphore("banks_free")
        self.stage_sems = []
        self.loaded = 0
        self.used = 0
        self.evacs = 0
        self.order = list(PHASES)
        self.preloaded = {}
        self.cols = [blocks * P for n, blocks in PHASES.values() for _ in range(n)]

    def c(self, name, lo=0, n=None):
        at = CONST_AT[name] + lo
        return self.const[:, at:at + (n if n else dict(CONSTS)[name] - lo)]

    def v(self, name, i):
        return self.vec[:, VEC_AT[name] + i:VEC_AT[name] + i + 1]

    def sem(self, name):
        self.stage_sems.append(self.nc.alloc_semaphore(name))
        return self.stage_sems[-1]

    def part(self, tile, lo=0, hi=T):
        return self.parts[tile // 8][:, tile % 8, lo:hi]

    def pair(self, hi, lo, tile):
        return self.part(hi + tile), self.part(lo + tile)

    def load_weights(self, sp, phase, lo, hi):
        src, cols, g0 = self.dram["w_" + phase], PHASES[phase][1] * P, self.loaded

        def load(g, i, at):
            if g >= 2:
                sp.wait_ge(self.lo_ready, g - 1 + i * RING)
            group = src[bass.ds(at + i * RING, 1)] if not isinstance(i, int) else src[at:at + 1]
            sp.dma_start(self.raw[:, g % 2, 0:cols], group.rearrange("a p n -> p (a n)"))\
                .then_inc(self.weights_in[g % 2], 16)

        n = hi - lo
        done = 0
        if g0 == 0:
            done = 2
            for j in range(done):
                load(g0 + j, 0, lo + j)
        turns = (n - done) // RING
        if turns > 1:
            with sp.Fori(0, turns) as i:
                for j in range(RING):
                    load(g0 + done + j, i, lo + done + j)
            done += turns * RING
        for j in range(done, n):
            load(g0 + j, 0, lo + j)
        self.loaded += n

    def stream(self, sp, phase):
        self.load_weights(sp, phase, self.preloaded.pop(phase, 0), PHASES[phase][0])
        at = self.order.index(phase) + 1
        if at < len(self.order):
            self.load_weights(sp, self.order[at], 0, RING)
            self.preloaded[self.order[at]] = RING

    def split_hi(self, act, g):
        if g >= len(self.cols):
            return
        act.wait_ge(self.weights_in[g % 2], 16 * (g // 2 + 1))
        if g >= 2:
            act.wait_ge(self.groups_done, g - 1)
        cols = self.cols[g]
        act.activation(self.w_hi[:, g % 2, 0:cols], self.raw[:, g % 2, 0:cols], ACT.Copy).then_inc(self.hi_ready, 1)

    def split_lo(self, dve, g):
        if g >= len(self.cols):
            return
        dve.wait_ge(self.hi_ready, g + 1)
        cols = self.cols[g]
        dve.tensor_tensor(self.w_lo[:, g % 2, 0:cols], self.raw[:, g % 2, 0:cols], self.w_hi[:, g % 2, 0:cols].bitcast(F32),
                          ALU.subtract).then_inc(self.lo_ready, 1)

    def wait_weights(self, pe, g, i=0, per=RING):
        pe.wait_ge(self.lo_ready, g + 1 + i * per)

    def weights(self, g, lo, hi):
        return self.w_hi[:, g % 2, lo:hi], self.w_lo[:, g % 2, lo:hi]


def product(pe, out, left, right, start, stop):
    pe.matmul(out, left[0], right[0], start=start, stop=False)
    pe.matmul(out, left[0], right[1], start=False, stop=False)
    return pe.matmul(out, left[1], right[0], start=False, stop=stop)


def in_turns(eng, n, per, body):
    turns = n // per
    done = 0
    if turns > 1:
        with eng.Fori(0, turns) as i:
            for j in range(per):
                body(i, j, 0)
        done = turns * per
    for j in range(done, n):
        body(0, j - done, done)


def pe_gemm(core, pe, n, kc, rhs, ps, width=T):
    g0, e0 = core.used, core.evacs

    def step(i, j, done):
        g, e = g0 + done + j, e0 + done + j
        core.wait_weights(pe, g, i)
        pe.wait_ge(core.banks_free, e + 1 + i * RING)
        for k in range(kc):
            mm = product(pe, ps[:, e % 4, 0:width], core.weights(g, k * P, (k + 1) * P), rhs(k), k == 0, k == kc - 1)
        mm.then_inc(core.groups_done, 1)

    in_turns(pe, n, RING, step)
    core.used += n
    core.evacs += n


def pe_by_token(core, pe, groups, width, rhs, tiles, bank):
    per = core.cols[core.used] // width
    for q in range(groups):
        core.wait_weights(pe, core.used)
        for b in range(per):
            k = q * per + b
            x = rhs(k)
            for i in range(tiles):
                for lo in range(0, width, T):
                    n = min(T, width - lo)
                    mm = product(pe, bank(i, lo // T)[:, 0:n], (x[0][:, i * P:(i + 1) * P], x[1][:, i * P:(i + 1) * P]),
                                 core.weights(core.used, b * width + lo, b * width + lo + n), k == 0, k == groups * per - 1)
        mm.then_inc(core.groups_done, 1)
        core.used += 1




def setup_stage(core):
    nc, dram = core.nc, core.dram
    x_in, const_in, vec_in = core.sem("x_in"), core.sem("const_in"), core.sem("vec_in")
    wa_in, g_in = core.sem("wa_lora_in"), core.sem("g_lora_in")
    with nc.Block() as block:

        @block.sync
        def _(sp):
            sp.dma_start(core.h[:], dram["x_t"]).then_inc(x_in, 16)
            sp.dma_start(core.const[:], dram["const"]).then_inc(const_in, 16)
            core.load_weights(sp, "proj", 0, RING)
            core.preloaded["proj"] = RING
            sp.wait_ge(x_in, 16)
            sp.wait_ge(const_in, 16)

        @block.scalar
        def _(act):
            act.dma_start(core.vec[:], dram["vec"]).then_inc(vec_in, 16)
            act.dma_start(core.arena[:, 53, :], dram["wa_lora"]).then_inc(wa_in, 16)
            act.dma_start(core.arena[:, 54, :], dram["g_lora_t"]).then_inc(g_in, 16)
            for g in range(2):
                core.split_hi(act, g)
            act.wait_ge(vec_in, 16)
            act.wait_ge(wa_in, 16)
            act.wait_ge(g_in, 16)

        @block.vector
        def _(dve):
            dve.sem_inc(core.banks_free, 4)
            for g in range(2):
                core.split_lo(dve, g)


def norm_stage(core, name, src, gain, split=None, dst=None, width=T, scratch=40):
    nc = core.nc
    squared = core.sem(name + "_squared")
    squared_too = core.sem(name + "_squared_too")
    summed = core.sem(name + "_summed")
    steps = core.sem(name + "_steps")
    rooted = core.sem(name + "_rooted")
    scaled = core.sem(name + "_scaled")
    upper = core.sem(name + "_upper")
    with ExitStack() as ctx:
        ps = ctx.enter_context(nc.psum_tensor(name + "_ps", [P, T], F32))
        sq = core.arena[:, scratch:scratch + KD, 0:width]
        rstd = core.arena[:, scratch + KD, 0:width]
        with nc.Block() as block:

            @block.scalar
            def _(act):
                for k in range(0, KD, 2):
                    act.activation(sq[:, k, :], src(k), ACT.Square).then_inc(squared, 1)
                act.wait_ge(steps, 1)
                act.activation(rstd, rstd, ACT.Sqrt).then_inc(rooted, 1)
                if split:
                    for k in range(KD):
                        act.wait_ge(scaled, k + 1)
                        act.activation(split(k)[0], sq[:, k, :], ACT.Copy).then_inc(upper, 1)

            @block.tensor
            def _(pe):
                for k in range(KD):
                    if k % 2 == 0:
                        pe.wait_ge(squared, k // 2 + 1)
                    else:
                        pe.wait_ge(squared_too, k // 2 + 1)
                    mm = pe.matmul(ps[:, 0:width], core.c("ones"), sq[:, k, :], start=(k == 0), stop=(k == KD - 1))
                mm.then_inc(summed, 1)

            @block.vector
            def _(dve):
                for k in range(1, KD, 2):
                    dve.tensor_tensor(sq[:, k, :], src(k), src(k), ALU.mult).then_inc(squared_too, 1)
                dve.wait_ge(summed, 1)
                dve.tensor_scalar(rstd, ps[:, 0:width], 1.0 / D, RMS_EPS, ALU.mult, ALU.add).then_inc(steps, 1)
                dve.wait_ge(rooted, 1)
                dve.reciprocal(rstd, rstd).then_inc(steps, 1)
                dve.wait_ge(steps, 2)

                def lower(k):
                    dve.wait_ge(upper, k + 1)
                    dve.tensor_tensor(split(k)[1], sq[:, k, :], split(k)[0].bitcast(F32), ALU.subtract)

                for k in range(KD):
                    to = sq[:, k, :] if split else dst(k)
                    dve.scalar_tensor_tensor(to, src(k), core.v(gain, k), rstd, ALU.mult, ALU.mult).then_inc(scaled, 1)
                    if split and k >= 2:
                        lower(k - 2)
                if split:
                    lower(KD - 2)
                    lower(KD - 1)


def proj_stage(core):
    nc = core.nc
    g0, e0 = core.used, core.evacs
    rwkv = core.arena[:, 12:26, :]
    qk = core.arena[:, 26:34, :]
    value = core.arena[:, 34:38, :]
    conv = core.arena[:, 38:50, :]
    diff = core.arena[:, 50:52, :]
    steps = core.sem("proj_steps")
    with ExitStack() as ctx:
        ps = ctx.enter_context(nc.psum_tensor("proj_ps", [P, 4, T], F32))
        ps_v = ctx.enter_context(nc.psum_tensor("proj_ps_v", [P, NT, T], F32))
        with nc.Block() as block:

            @block.sync
            def _(sp):
                core.stream(sp, "proj")

            @block.tensor
            def _(pe):
                x = lambda k: core.pair(XN_HI, XN_LO, k)
                pe_gemm(core, pe, 14, KD, x, ps)
                pe_gemm(core, pe, 12, KD, x, ps)
                pe_gemm(core, pe, 8, KD, x, ps)
                pe_by_token(core, pe, 4, T, x, NT, lambda i, half: ps_v[:, i, :])

            @block.scalar
            def _(act):
                for n in range(38):
                    core.split_hi(act, g0 + n + 2)
                    if n < 34:
                        act.wait_ge(core.groups_done, g0 + n + 1)
                        to = rwkv[:, n, :] if n < 14 else conv[:, n - 14, :] if n < 26 else qk[:, n - 26, :]
                        act.activation(to, ps[:, (e0 + n) % 4, :], ACT.Copy, scale=HD ** -0.5 if 26 <= n < 30 else 1.0)\
                           .then_inc(core.banks_free, 1)
                act.wait_ge(core.groups_done, g0 + 38)
                for i in range(NT):
                    act.activation(value[:, i, :], ps_v[:, i, :], ACT.Copy)

            @block.vector
            def _(dve):
                count = [0]

                def chained(ins):
                    ins.then_inc(steps, 1)
                    count[0] += 1

                def settled():
                    dve.wait_ge(steps, count[0])

                def shift(j):
                    p, d = rwkv[:, j, :], diff[:, j % 2, :]
                    dve.wait_ge(core.banks_free, 4 + e0 + j + 1)
                    chained(dve.tensor_scalar(d[:, 0:1], p[:, 0:1], -1.0, None, ALU.mult))
                    chained(dve.tensor_tensor(d[:, 1:T], p[:, 0:T - 1], p[:, 1:T], ALU.subtract))
                    settled()
                    chained(dve.scalar_tensor_tensor(p, d, core.v("mu_rwkv", j), p, ALU.mult, ALU.add))

                def convolve(j):
                    u, y, b = conv[:, 3 * j, :], conv[:, 3 * j + 1, :], conv[:, 3 * j + 2, :]
                    dve.wait_ge(core.banks_free, 4 + e0 + 14 + 3 * j + 3)
                    chained(dve.tensor_tensor(u, u, y, ALU.mult))
                    settled()
                    chained(dve.tensor_scalar(y, u, core.v("conv_w", 8 + j), None, ALU.mult))
                    settled()
                    chained(dve.scalar_tensor_tensor(y[:, 1:T], u[:, 0:T - 1], core.v("conv_w", 4 + j), y[:, 1:T],
                                                     ALU.mult, ALU.add))
                    settled()
                    chained(dve.scalar_tensor_tensor(y[:, 2:T], u[:, 0:T - 2], core.v("conv_w", j), y[:, 2:T],
                                                     ALU.mult, ALU.add))
                    settled()
                    chained(dve.tensor_tensor(core.arena[:, j, :], y, b, ALU.mult))

                for n in range(38):
                    core.split_lo(dve, g0 + n + 2)
                    if 1 <= n < 15:
                        shift(n - 1)
                    if n >= 17 and (n - 17) % 3 == 0 and (n - 17) // 3 < NW:
                        convolve((n - 17) // 3)


def stick_breaking_stage(core):
    nc = core.nc
    query, key = core.arena[:, 26:30, :], core.arena[:, 30:34, :]
    value = core.arena[:, 34:38, :]
    flat = core.arena[:, 38:53, :].rearrange("p a t -> p (a t)")
    log_buf = [flat[:, b * 1280:(b + 1) * 1280] for b in range(2)]
    soft = [flat[:, 2560 + b * 1280:2560 + (b + 1) * 1280] for b in range(2)]
    att = [flat[:, 5120 + b * 1280:5120 + (b + 1) * 1280] for b in range(2)]
    start = [0, 512, 896, 1152]
    scores_ready = core.sem("sb_scores_ready")
    abs_ready = core.sem("sb_abs_ready")
    exp_ready = core.sem("sb_exp_ready")
    log_ready = core.sem("sb_log_ready")
    soft_part = core.sem("sb_soft_part")
    soft_ready = core.sem("sb_soft_ready")
    weight_ready = core.sem("sb_weight_ready")
    att_ready = core.sem("sb_att_ready")
    out_done = core.sem("sb_out_done")
    out_taken = core.sem("sb_out_taken")
    with ExitStack() as ctx:
        ps = ctx.enter_context(nc.psum_tensor("sb_ps", [P, 6, T], F32))
        ps_out = ctx.enter_context(nc.psum_tensor("sb_ps_out", [P, 2, T], F32))

        def tile(h, j):
            bank, lo = (j, 0) if j < 3 else (2, 256)
            return ps[:, 3 * (h % 2) + bank, lo:lo + T - j * P]

        def parts(h, buf):
            return [(ps[:, 3 * (h % 2) + m, 0:n], buf[h % 2][:, lo:lo + n]) for m, lo, n in ((0, 0, 512), (1, 512, 384), (2, 896, 384))]

        with nc.Block() as block:

            @block.tensor
            def _(pe):
                def scores(h):
                    c, off = h // 2, HD * (h % 2)
                    if h >= 2:
                        pe.wait_ge(att_ready, h - 1)
                    for j in range(NT):
                        mm = pe.matmul(tile(h, j), key[off:off + HD, c, j * P:(j + 1) * P], query[off:off + HD, c, j * P:T],
                                       start=(j < 3), stop=False, skip_group_check=True)
                    mm.then_inc(scores_ready, 1)

                def weights(h):
                    pe.wait_ge(soft_ready, h + 1)
                    for j in range(NT):
                        pe.matmul(tile(h, j)[:, 0:P], core.c("ident"), core.c("neg_diag_t"), start=False, stop=False,
                                  skip_group_check=True)
                        for m in range(j, NT):
                            mm = pe.matmul(tile(h, j)[:, (m - j) * P:T - j * P], core.c("neg_tri" if m == j else "neg_ones"),
                                           soft[h % 2][:, start[m]:start[m] + T - m * P], start=False, stop=(m == NT - 1),
                                           skip_group_check=True)
                    mm.then_inc(weight_ready, 1)

                def output(h):
                    c, off = h // 2, HD * (h % 2)
                    pe.wait_ge(att_ready, h + 1)
                    if c >= 2:
                        pe.wait_ge(out_taken, c - 1)
                    for j in range(NT):
                        mm = pe.matmul(ps_out[off:off + HD, c % 2, j * P:T], value[:, j, h * HD:(h + 1) * HD],
                                       att[h % 2][:, start[j]:start[j] + T - j * P], start=(j == 0), stop=(j == NT - 1),
                                       skip_group_check=True)
                    mm.then_inc(out_done, 1)

                scores(0)
                for h in range(HEADS):
                    if h + 1 < HEADS:
                        scores(h + 1)
                    weights(h)
                    if h >= 1:
                        output(h - 1)
                output(HEADS - 1)

            @block.scalar
            def _(act):
                def logs(h):
                    act.wait_ge(scores_ready, h + 1)
                    if h >= 2:
                        act.wait_ge(soft_part, h - 1)
                    for banks, cols in parts(h, log_buf):
                        ins = act.activation(cols, banks, ACT.Abs)
                    ins.then_inc(abs_ready, 1)
                    act.wait_ge(abs_ready, h + 1)
                    act.activation(log_buf[h % 2], log_buf[h % 2], ACT.Exp, scale=-1.0).then_inc(exp_ready, 1)
                    act.wait_ge(exp_ready, h + 1)
                    act.activation(log_buf[h % 2], log_buf[h % 2], ACT.Ln, bias=1.0).then_inc(log_ready, 1)

                def weights(h):
                    act.wait_ge(weight_ready, h + 1)
                    if h >= 2:
                        act.wait_ge(out_done, h - 1)
                    for i, (banks, cols) in enumerate(parts(h, att)):
                        ins = act.activation(cols, banks, ACT.Exp)
                    ins.then_inc(att_ready, 1)

                logs(0)
                for h in range(HEADS):
                    if h + 1 < HEADS:
                        logs(h + 1)
                    weights(h)

            @block.vector
            def _(dve):
                def softplus(h):
                    dve.wait_ge(log_ready, h + 1)
                    if h >= 2:
                        dve.wait_ge(weight_ready, h - 1)
                    for (banks, cols), (_, logs) in zip(parts(h, soft), parts(h, log_buf)):
                        ins = dve.scalar_tensor_tensor(cols, banks, 0.0, logs, ALU.max, ALU.add)
                    ins.then_inc(soft_part, 1)
                    dve.wait_ge(soft_part, h + 1)
                    for j in range(NT):
                        diag = soft[h % 2][:, start[j]:start[j] + P]
                        ins = dve.tensor_tensor(diag, diag, core.c("causal4", 0, P), ALU.mult)
                    ins.then_inc(soft_ready, 1)

                def take(c):
                    dve.wait_ge(out_done, 2 * c + 2)
                    dve.tensor_copy(core.arena[:, 4 + c, :], ps_out[:, c % 2, :]).then_inc(out_taken, 1)

                for h in range(HEADS):
                    softplus(h)
                    if h >= 2 and h % 2 == 0:
                        take(h // 2 - 1)
                take(NW - 1)


def clear_semaphores_stage(core):
    with core.nc.Block() as block:

        @block.sync
        def _(sp):
            for sem in core.stage_sems:
                sp.sem_clear(sem)

    for sem in core.stage_sems:
        core.nc.release_semaphore(sem)
    core.stage_sems = []


def time_mix_stage(core):
    nc, a = core.nc, core.arena
    r, k, v = a[:, 12:16, :], a[:, 16:20, :], a[:, 20:24, :]
    wa, xg, lora, g_lora = a[:, 24, :], a[:, 25, :], a[:, 53, :], a[:, 54, :]
    kk, bonus, key = a[:, 26:30, :], a[:, 30:34, :], a[:, 34:38, :]
    decay, rate, gate, sums = a[:, 38:42, :], a[:, 42:46, :], a[:, 46:50, :], a[:, 50:54, :]
    restart = a[:, 58, :]
    norm, rk = a[:, 61:65, :], a[:, 65:69, :]
    mid = core.small[:, 0:16]
    inner = core.sem("tm_inner")
    lora_out = core.sem("tm_lora_out")
    lora_taken = core.sem("tm_lora_taken")
    square = core.sem("tm_square")
    bonus_in = core.sem("tm_bonus_in")
    norm_sum = core.sem("tm_norm_sum")
    bonus_sum = core.sem("tm_bonus_sum")
    rooted = core.sem("tm_rooted")
    steps = core.sem("tm_steps")
    ready = core.sem("tm_restart")
    with ExitStack() as ctx:
        ps = ctx.enter_context(nc.psum_tensor("tm_ps", [P, 8, T], F32))
        with nc.Block() as block:

            @block.gpsimd
            def _(pool):
                pool.memset(restart, 1.0).then_inc(ready, 1)
                pool.wait_ge(ready, 1)
                pool.memset(restart[:, 0:T:P], 0.0).then_inc(ready, 1)

            @block.scalar
            def _(act):
                act.activation(wa[0:HD, :], wa[0:HD, :], ACT.Tanh).then_inc(inner, 1)
                act.activation(xg, xg, ACT.Sigmoid).then_inc(inner, 1)
                for c in range(NW):
                    act.wait_ge(lora_out, c + 1)
                    act.activation(decay[:, c, :], ps[:, 4 * (c % 2), :], ACT.Sigmoid, bias=core.v("w0", c))
                    act.activation(rate[:, c, :], ps[:, 4 * (c % 2) + 1, :], ACT.Sigmoid, bias=core.v("a0", c))
                    act.activation(gate[:, c, :], ps[:, 4 * (c % 2) + 2, :], ACT.Copy).then_inc(lora_taken, 1)
                for c in range(NW):
                    act.wait_ge(norm_sum, c + 1)
                    act.activation(norm[:, c, :], ps[:, 4 * (c % 2) + 3, :], ACT.Sqrt).then_inc(rooted, 1)

            @block.tensor
            def _(pe):
                pe.wait_ge(inner, 2)
                for c in range(NW):
                    if c >= 2:
                        pe.wait_ge(lora_taken, c - 1)
                    cols = slice(c * P, (c + 1) * P)
                    pe.matmul(ps[:, 4 * (c % 2), :], lora[0:HD, cols], wa[0:HD, :], start=True, stop=True)
                    pe.matmul(ps[:, 4 * (c % 2) + 1, :], lora[HD:P, cols], wa[HD:P, :], start=True, stop=True)
                    pe.matmul(ps[:, 4 * (c % 2) + 2, :], g_lora[:, cols], xg, start=True, stop=True).then_inc(lora_out, 1)
                for c in range(NW):
                    pe.wait_ge(square, c + 1)
                    if c >= 2:
                        pe.wait_ge(rooted, c - 1)
                    pe.matmul(ps[:, 4 * (c % 2) + 3, :], core.c("head_ones"), bonus[:, c, :], start=True, stop=True)\
                      .then_inc(norm_sum, 1)
                pe.wait_ge(lora_taken, NW)
                for c in range(NW):
                    pe.wait_ge(bonus_in, c + 1)
                    pe.matmul(ps[:, (0, 1, 4, 5)[c], :], core.c("head_ones"), rk[:, c, :], start=True, stop=True)\
                      .then_inc(bonus_sum, 1)

            @block.vector
            def _(dve):
                n = 0
                for c in range(NW):
                    dve.tensor_scalar(kk[:, c, :], k[:, c, :], core.v("k_k", c), None, ALU.mult).then_inc(steps, 1)
                    n += 1
                    dve.wait_ge(steps, n)
                    dve.tensor_tensor(bonus[:, c, :], kk[:, c, :], kk[:, c, :], ALU.mult).then_inc(square, 1)
                for c in range(NW):
                    dve.tensor_scalar(rk[:, c, :], r[:, c, :], core.v("r_k", c), None, ALU.mult).then_inc(steps, 1)
                    n += 1
                for c in range(NW):
                    dve.wait_ge(lora_taken, c + 1)
                    dve.tensor_scalar(key[:, c, :], rate[:, c, :], -1.0, core.v("k_a", c), ALU.add, ALU.mult).then_inc(steps, 1)
                    n += 1
                    dve.wait_ge(steps, n)
                    dve.scalar_tensor_tensor(key[:, c, :], key[:, c, :], 1.0, k[:, c, :], ALU.add, ALU.mult).then_inc(steps, 1)
                    n += 1
                    dve.wait_ge(steps, n)
                    dve.tensor_tensor(rk[:, c, :], rk[:, c, :], key[:, c, :], ALU.mult).then_inc(bonus_in, 1)
                dve.wait_ge(ready, 2)
                for c in range(NW):
                    dve.tensor_tensor_scan(sums[:, c, :], restart, decay[:, c, :], 0.0, ALU.mult, ALU.add).then_inc(steps, 1)
                n += NW
                dve.wait_ge(steps, n)
                for c in range(NW):
                    dve.tensor_copy(mid[:, 4 * c:4 * c + 4], sums[:, c, P // 2 - 1:T:P]).then_inc(steps, 1)
                n += NW
                dve.wait_ge(steps, n)
                for c in range(NW):
                    s3 = sums[:, c, :].rearrange("p (n t) -> p n t", t=P)
                    dve.tensor_tensor(s3, s3, mid[:, 4 * c:4 * c + 4].unsqueeze(2).broadcast_to([P, NT, P]), ALU.subtract)\
                       .then_inc(steps, 1)
                n += NW
                dve.wait_ge(steps, n)
                for c in range(NW):
                    dve.tensor_tensor(decay[:, c, :], sums[:, c, :], decay[:, c, :], ALU.subtract).then_inc(steps, 1)
                n += NW
                for c in range(NW):
                    dve.wait_ge(rooted, c + 1)
                    dve.tensor_scalar(norm[:, c, :], norm[:, c, :], 1e-12, None, ALU.max).then_inc(steps, 1)
                    n += 1
                    dve.wait_ge(steps, n)
                    dve.reciprocal(norm[:, c, :], norm[:, c, :]).then_inc(steps, 1)
                    n += 1
                    dve.wait_ge(steps, n)
                    dve.tensor_tensor(kk[:, c, :], kk[:, c, :], norm[:, c, :], ALU.mult).then_inc(steps, 1)
                    n += 1
                for c in range(NW):
                    dve.wait_ge(bonus_sum, c + 1)
                    dve.tensor_tensor(bonus[:, c, :], ps[:, (0, 1, 4, 5)[c], :], v[:, c, :], ALU.mult)


def time_mix_scale_stage(core):
    nc, a = core.nc, core.arena
    r, k_out, v, v_tok = a[:, 12:16, :], a[:, 16:20, :], a[:, 20:24, :], a[:, 12:16, :]
    kk, key, kk_tok, key_tok = a[:, 26:30, :], a[:, 34:38, :], a[:, 34:38, :], a[:, 26:30, :]
    before, rate, sums, upto = a[:, 38:42, :], a[:, 42:46, :], a[:, 50:54, :], a[:, 54:58, :]
    pair = a[:, 61:69, :].rearrange("p (c n) (m q t) -> p c (n m) q t", n=2, q=2, t=P)
    upto_ready = core.sem("ts_upto_ready")
    before_ready = core.sem("ts_before_ready")
    away_ready = core.sem("ts_away_ready")
    steps = core.sem("ts_steps")
    r_used = core.sem("ts_r_used")
    k_made = core.sem("ts_k_made")
    b_made = core.sem("ts_b_made")
    turned = core.sem("ts_turned")
    placed = core.sem("ts_placed")
    chunks = lambda x: x.rearrange("p (n t) -> p n t", t=P)
    with ExitStack() as ctx:
        ps = ctx.enter_context(nc.psum_tensor("ts_ps", [P, 8, T], F32))
        with nc.Block() as block:

            @block.scalar
            def _(act):
                for c in range(NW):
                    act.activation(upto[:, c, :], sums[:, c, :], ACT.Exp, scale=-DECAY).then_inc(upto_ready, 1)
                    act.activation(before[:, c, :], before[:, c, :], ACT.Exp, scale=-DECAY).then_inc(before_ready, 1)
                    act.wait_ge(upto_ready, c + 1)
                    act.activation(sums[:, c, :], sums[:, c, :], ACT.Exp, scale=DECAY).then_inc(away_ready, 1)
                act.activation(core.small[:, 16:32], core.small[:, 0:16], ACT.Exp, scale=-DECAY)
                for n in range(12):
                    act.wait_ge(turned, n + 1)
                    if n < 4:
                        act.wait_ge(r_used, NW)
                    else:
                        act.wait_ge(b_made, NW)
                    out = (v_tok, key_tok, kk_tok)[n // 4]
                    act.activation(out[:, n % 4, :], ps[:, n % 8, :], ACT.Copy).then_inc(placed, 1)

            @block.vector
            def _(dve):
                for c in range(NW):
                    dve.wait_ge(upto_ready, c + 1)
                    dve.tensor_tensor(pair[:, c, :, 1, :], chunks(r[:, c, :]), chunks(upto[:, c, :]), ALU.mult).then_inc(r_used, 1)
                for c in range(NW):
                    dve.wait_ge(before_ready, c + 1)
                    dve.tensor_tensor(pair[:, c, :, 0, :], chunks(kk[:, c, :]), chunks(before[:, c, :]), ALU.mult)
                    dve.wait_ge(away_ready, c + 1)
                    dve.tensor_tensor(k_out[:, c, :], key[:, c, :], sums[:, c, :], ALU.mult).then_inc(k_made, 1)
                    dve.tensor_tensor(rate[:, c, :], rate[:, c, :], kk[:, c, :], ALU.mult).then_inc(steps, 1)
                    dve.wait_ge(steps, c + 1)
                    dve.tensor_tensor(rate[:, c, :], rate[:, c, :], sums[:, c, :], ALU.mult).then_inc(b_made, 1)
                for c in range(NW):
                    dve.tensor_copy(core.small[:, 32 + 4 * c:36 + 4 * c], upto[:, c, P - 1:T:P])

            @block.tensor
            def _(pe):
                for n in range(12):
                    src = (v, k_out, rate)[n // 4]
                    if n == 4:
                        pe.wait_ge(k_made, NW)
                    if n == 8:
                        pe.wait_ge(b_made, NW)
                    if n >= 8:
                        pe.wait_ge(placed, n - 7)
                    for c in range(NW):
                        mm = pe.transpose(ps[:, n % 8, c * P:(c + 1) * P], src[:, c, (n % 4) * P:(n % 4 + 1) * P], core.c("ident"))
                    mm.then_inc(turned, 1)


def time_mix_chunks_stage(core):
    nc, a = core.nc, core.arena
    v_tok, key_tok, b_tok = a[:, 12:16, :], a[:, 26:30, :], a[:, 34:38, :]
    k_out, b_out = a[:, 16:20, :], a[:, 42:46, :]
    pair = a[:, 61:69, :].rearrange("p (c n) (m q t) -> p c (n m) q t", n=2, q=2, t=P)
    gram = a[:, 50:58, :]
    inv, inv_t = a[:, 38:40, :], a[:, 40:42, :]
    level = [a[:, 20:22, :], a[:, 22:24, :]]
    prod = a[:, 24:26, :]
    state = a[:, 58, 0:256]
    x_sb, sa = a[:, 59, :], a[:, 60, :]
    out = a[:, 8:12, :]
    from_start, to_end = core.small[:, 16:32], core.small[:, 32:48]
    LEVELS = 7
    gram_done = core.sem("tc_gram_done")
    gram_ready = core.sem("tc_gram_ready")
    units_ready = core.sem("tc_units_ready")
    level_ready = core.sem("tc_level_ready")
    prod_done = core.sem("tc_prod_done")
    prod_ready = core.sem("tc_prod_ready")
    step_done = core.sem("tc_step_done")
    step_ready = core.sem("tc_step_ready")
    x_done, x_ready = core.sem("tc_x_done"), core.sem("tc_x_ready")
    sa_done, sa_ready = core.sem("tc_sa_done"), core.sem("tc_sa_ready")
    end_done, out_ready = core.sem("tc_end_done"), core.sem("tc_out_ready")
    state_sum, state_ready = core.sem("tc_state_sum"), core.sem("tc_state_ready")
    heads = lambda x: x.rearrange("p a (m t) -> p (a m) t", t=P)
    with ExitStack() as ctx:
        ps = ctx.enter_context(nc.psum_tensor("tc_ps", [P, 8, T], F32))
        with nc.Block() as block:

            @block.tensor
            def _(pe):
                def grams(ch):
                    for h in range(HEADS):
                        c, rows, u = h // 2, slice(HD * (h % 2), HD * (h % 2) + HD), ch * HEADS + h
                        if u >= 2:
                            pe.wait_ge(gram_ready, u - 1)
                        qr = pair[rows, c, ch, :, :].rearrange("p q t -> p (q t)")
                        cols = slice(ch * P, (ch + 1) * P)
                        pe.matmul(ps[:, h % 2, 0:256], b_out[rows, c, cols], qr, start=True, stop=True)
                        pe.matmul(ps[:, h % 2, 256:512], k_out[rows, c, cols], qr, start=True, stop=True)\
                          .then_inc(gram_done, 1)

                def inverse(ch):
                    for n in range(LEVELS):
                        pe.wait_ge(level_ready, ch * LEVELS + n + 1)
                        if n == 0:
                            pe.wait_ge(units_ready, ch + 1)
                            if ch:
                                pe.wait_ge(out_ready, ch)
                                pe.wait_ge(state_ready, ch)
                        for half in range(2):
                            u = (ch * LEVELS + n) * 2 + half
                            if u >= 2:
                                pe.wait_ge(step_ready, u - 1)
                            for m in range(4):
                                h = 4 * half + m
                                mm = pe.matmul(ps[:, 2 + half, m * P:(m + 1) * P], heads(level[(ch * LEVELS + n) % 2])[:, h, :],
                                               heads(inv)[:, h, :], start=True, stop=True)
                            mm.then_inc(prod_done, 1)
                        for half in range(2):
                            u = (ch * LEVELS + n) * 2 + half
                            pe.wait_ge(prod_ready, u + 1)
                            for m in range(4):
                                h = 4 * half + m
                                pe.matmul(ps[:, 4 + half, m * P:(m + 1) * P], heads(inv_t)[:, h, :], heads(prod)[:, h, :],
                                          start=True, stop=True)
                                mm = pe.matmul(ps[:, 6 + half, m * P:(m + 1) * P], heads(prod)[:, h, :], heads(inv_t)[:, h, :],
                                               start=True, stop=True)
                            mm.then_inc(step_done, 1)

                def recur(ch):
                    if ch:
                        pe.wait_ge(state_ready, ch)
                    pe.wait_ge(step_ready, (ch + 1) * LEVELS * 2)
                    pe.wait_ge(gram_ready, (ch + 1) * HEADS)
                    for h in range(HEADS):
                        c, rows, cols = h // 2, slice(HD * (h % 2), HD * (h % 2) + HD), slice(h * HD, (h + 1) * HD)
                        x_ps = ps[:, 4 * (h % 2), c * HD:(c + 1) * HD]
                        if ch:
                            pe.matmul(x_ps, pair[rows, c, ch, 0, :], state[rows, c * HD:(c + 1) * HD],
                                      start=True, stop=False)
                        mm = pe.matmul(x_ps, gram[:, h, 256:384], v_tok[:, ch, cols], start=(ch == 0), stop=True)
                    mm.then_inc(x_done, 1)
                    pe.wait_ge(x_ready, ch + 1)
                    for h in range(HEADS):
                        cols = slice(h * HD, (h + 1) * HD)
                        mm = pe.matmul(ps[:, 1, cols], heads(inv_t)[:, h, :], x_sb[:, cols], start=True, stop=True)
                    mm.then_inc(sa_done, 1)
                    pe.wait_ge(sa_ready, ch + 1)
                    for h in range(HEADS):
                        c, rows, cols = h // 2, slice(HD * (h % 2), HD * (h % 2) + HD), slice(h * HD, (h + 1) * HD)
                        o, s = ps[rows, 2, c * P:(c + 1) * P], ps[rows, 3, c * HD:(c + 1) * HD]
                        if ch < NT - 1:
                            pe.matmul(s, key_tok[:, ch, cols], v_tok[:, ch, cols], start=True, stop=False)
                            pe.matmul(s, b_tok[:, ch, cols], sa[:, cols], start=False, stop=True)
                        if ch:
                            pe.matmul(o, state[rows, c * HD:(c + 1) * HD], pair[rows, c, ch, 1, :], start=True, stop=False)
                        pe.matmul(o, v_tok[:, ch, cols], gram[:, h, 384:512], start=(ch == 0), stop=False)
                        mm = pe.matmul(o, sa[:, cols], gram[:, h, 128:256], start=False, stop=True)
                    mm.then_inc(end_done, 1)

                for ch in range(NT):
                    grams(ch)
                    inverse(ch)
                    recur(ch)

            @block.gpsimd
            def _(pool):
                for ch in range(NT):
                    if ch:
                        pool.wait_ge(sa_done, ch)
                    ident = core.c("ident").unsqueeze(1).broadcast_to([P, HEADS, P])
                    pool.tensor_copy(heads(inv), ident)
                    pool.tensor_copy(heads(inv_t), ident).then_inc(units_ready, 1)
                    pool.wait_ge(gram_ready, (ch + 1) * HEADS)
                    for n in range(LEVELS):
                        g = ch * LEVELS + n
                        if g >= 2:
                            pool.wait_ge(prod_done, 2 * (g - 1))
                        pool.tensor_tensor(heads(level[g % 2]), gram[:, :, 0:P],
                                           core.c("level", n * P, P).unsqueeze(1).broadcast_to([P, HEADS, P]), ALU.mult)\
                            .then_inc(level_ready, 1)

            @block.scalar
            def _(act):
                for ch in range(NT):
                    for n in range(LEVELS):
                        for half in range(2):
                            u = (ch * LEVELS + n) * 2 + half
                            act.wait_ge(prod_done, u + 1)
                            act.activation(prod[:, half, :], ps[:, 2 + half, :], ACT.Copy).then_inc(prod_ready, 1)
                    act.wait_ge(x_done, ch + 1)
                    for odd in range(2):
                        ins = act.activation(x_sb.rearrange("p (c n v) -> p c n v", n=2, v=HD)[:, :, odd, :],
                                             ps[:, 4 * odd, 0:256].rearrange("p (c v) -> p c v", v=HD), ACT.Copy)
                    ins.then_inc(x_ready, 1)
                    act.wait_ge(end_done, ch + 1)
                    act.activation(out[:, :, ch * P:(ch + 1) * P], ps[:, 2, :].rearrange("p (c t) -> p c t", t=P), ACT.Copy)\
                       .then_inc(out_ready, 1)

            @block.vector
            def _(dve):
                for ch in range(NT):
                    if ch:
                        dve.wait_ge(end_done, ch)
                        dve.wait_ge(level_ready, ch * LEVELS)
                    for h in range(HEADS):
                        dve.wait_ge(gram_done, ch * HEADS + h + 1)
                        dve.tensor_tensor(gram[:, h, :], ps[:, h % 2, :], core.c("causal4"), ALU.mult).then_inc(gram_ready, 1)
                    dve.wait_ge(units_ready, ch + 1)
                    for n in range(LEVELS):
                        for half in range(2):
                            u = (ch * LEVELS + n) * 2 + half
                            dve.wait_ge(step_done, u + 1)
                            if u >= 2:
                                dve.wait_ge(step_ready, u - 1)
                            dve.tensor_tensor(inv[:, half, :], inv[:, half, :], ps[:, 4 + half, :], ALU.subtract)
                            dve.tensor_tensor(inv_t[:, half, :], inv_t[:, half, :], ps[:, 6 + half, :], ALU.subtract)\
                               .then_inc(step_ready, 1)
                    dve.wait_ge(sa_done, ch + 1)
                    dve.tensor_scalar(sa, ps[:, 1, :], -1.0, None, ALU.mult).then_inc(sa_ready, 1)
                    if ch < NT - 1:
                        dve.wait_ge(end_done, ch + 1)
                        if ch:
                            dve.tensor_tensor(state, state, ps[:, 3, 0:256], ALU.add).then_inc(state_sum, 1)
                        else:
                            dve.tensor_copy(state, ps[:, 3, 0:256]).then_inc(state_sum, 1)
                        dve.wait_ge(state_sum, ch + 1)
                        for c in range(NW):
                            part = state[:, c * HD:(c + 1) * HD]
                            ins = dve.tensor_scalar(part, part, to_end[:, 4 * c + ch:4 * c + ch + 1],
                                                    from_start[:, 4 * c + ch + 1:4 * c + ch + 2], ALU.mult, ALU.mult)
                        ins.then_inc(state_ready, 1)


def time_mix_out_stage(core):
    nc, a = core.nc, core.arena
    out, bonus, gate = a[:, 8:12, :], a[:, 30:34, :], a[:, 46:50, :]
    square, rstd = a[:, 50:54, :], a[:, 54:58, :]
    mean_done, centred = core.sem("to_mean_done"), core.sem("to_centred")
    squared, var_done = core.sem("to_squared"), core.sem("to_var_done")
    steps, rooted = core.sem("to_steps"), core.sem("to_rooted")
    with ExitStack() as ctx:
        ps = ctx.enter_context(nc.psum_tensor("to_ps", [P, 8, T], F32))
        with nc.Block() as block:

            @block.tensor
            def _(pe):
                for c in range(NW):
                    pe.matmul(ps[:, c, :], core.c("head_ones"), out[:, c, :], start=True, stop=True).then_inc(mean_done, 1)
                for c in range(NW):
                    pe.wait_ge(squared, c + 1)
                    pe.matmul(ps[:, 4 + c, :], core.c("head_ones"), square[:, c, :], start=True, stop=True).then_inc(var_done, 1)

            @block.scalar
            def _(act):
                for c in range(NW):
                    act.wait_ge(centred, c + 1)
                    act.activation(square[:, c, :], out[:, c, :], ACT.Square).then_inc(squared, 1)
                for c in range(NW):
                    act.wait_ge(steps, c + 1)
                    act.activation(rstd[:, c, :], rstd[:, c, :], ACT.Sqrt).then_inc(rooted, 1)

            @block.vector
            def _(dve):
                for c in range(NW):
                    dve.wait_ge(mean_done, c + 1)
                    dve.scalar_tensor_tensor(out[:, c, :], ps[:, c, :], -1.0 / HD, out[:, c, :], ALU.mult, ALU.add)\
                       .then_inc(centred, 1)
                for c in range(NW):
                    dve.wait_ge(var_done, c + 1)
                    dve.tensor_scalar(rstd[:, c, :], ps[:, 4 + c, :], 1.0 / HD, GN_EPS, ALU.mult, ALU.add).then_inc(steps, 1)
                n = NW
                for c in range(NW):
                    dve.tensor_scalar(bonus[:, c, :], bonus[:, c, :], core.v("lnx_b", c), None, ALU.add).then_inc(steps, 1)
                n += NW
                for c in range(NW):
                    dve.wait_ge(rooted, c + 1)
                    dve.reciprocal(rstd[:, c, :], rstd[:, c, :]).then_inc(steps, 1)
                    n += 1
                    dve.wait_ge(steps, n)
                    dve.scalar_tensor_tensor(out[:, c, :], out[:, c, :], core.v("lnx_w", c), rstd[:, c, :], ALU.mult, ALU.mult)\
                       .then_inc(steps, 1)
                    n += 1
                    dve.wait_ge(steps, n)
                    dve.tensor_tensor(out[:, c, :], out[:, c, :], bonus[:, c, :], ALU.add).then_inc(steps, 1)
                    n += 1
                    dve.wait_ge(steps, n)
                    dve.tensor_tensor(out[:, c, :], out[:, c, :], gate[:, c, :], ALU.mult)


def pe_gemm_deep(core, pe, n, per_tile, blocks, rhs, ps):
    g0, e0 = core.used, core.evacs
    assert 2 * per_tile % RING == 0 and n % 2 == 0

    def step(i, j, done):
        e = e0 + done + j
        pe.wait_ge(core.banks_free, e + 3 + i * 2)
        for q in range(per_tile):
            g = g0 + (done + j) * per_tile + q
            core.wait_weights(pe, g, i, 2 * per_tile)
            for b in range(blocks):
                k = q * blocks + b
                mm = product(pe, ps[:, e % 2, :], core.weights(g, b * P, (b + 1) * P), rhs(k), k == 0,
                             k == per_tile * blocks - 1)
            mm.then_inc(core.groups_done, 1)

    in_turns(pe, n, 2, step)
    core.used += n * per_tile
    core.evacs += n


def split_stage(core, name, n, src, hi, lo):
    upper = core.sem(name + "_upper")
    with core.nc.Block() as block:

        @block.scalar
        def _(act):
            for k in range(n):
                act.activation(core.part(hi + k), core.arena[:, src + k, :], ACT.Copy).then_inc(upper, 1)

        @block.vector
        def _(dve):
            for k in range(n):
                dve.wait_ge(upper, k + 1)
                dve.tensor_tensor(core.part(lo + k), core.arena[:, src + k, :],
                                  core.part(hi + k).bitcast(F32), ALU.subtract)


def gates_stage(core):
    nc, a = core.nc, core.arena
    open_gate = a[:, 0:3, :]
    part = a[:, 3:5, :]
    total = a[:, 5:7, :]
    g0 = core.used
    pairs_free = core.sem("gt_pairs_free")
    opened = core.sem("gt_opened")
    summed = core.sem("gt_summed")
    upper = core.sem("gt_upper")
    with ExitStack() as ctx:
        ps = ctx.enter_context(nc.psum_tensor("gt_ps", [P, 6, T], F32))
        with nc.Block() as block:

            @block.sync
            def _(sp):
                core.stream(sp, "gates")

            @block.tensor
            def _(pe):
                with pe.Fori(0, KD) as d:
                    for m in range(36):
                        n, k = m // 12, m % 12
                        if k == 0:
                            pe.wait_ge(pairs_free, d * 3 + n + 1)
                        g = g0 + m // 9
                        if m % 9 == 0:
                            core.wait_weights(pe, g, d)
                        w = core.weights(g, (m % 9) * P, (m % 9 + 1) * P)
                        if k < KD:
                            mm = product(pe, ps[:, 2 * n, :], w, core.pair(36, 44, k), k == 0, k == KD - 1)
                        else:
                            mm = product(pe, ps[:, 2 * n + 1, :], w, core.pair(12, 24, 4 * n + k - KD), k == KD, k == 11)
                        if m % 9 == 8:
                            mm.then_inc(core.groups_done, 1)
                core.used += 32

            @block.scalar
            def _(act):
                for d in range(KD):
                    for m in range(4):
                        core.split_hi(act, g0 + 4 * d + m + 2)
                        if m:
                            n = m - 1
                            act.wait_ge(core.groups_done, g0 + 4 * d + m + 1)
                            if d:
                                act.wait_ge(pairs_free, 3 + 3 * (d - 1) + n + 1)
                            act.activation(open_gate[:, n, :], ps[:, 2 * n, :], ACT.Sigmoid, bias=core.v("gate_b", 8 * n + d))\
                               .then_inc(opened, 1)
                        elif d:
                            act.wait_ge(summed, 2 * d)
                            act.activation(core.pair(XN_HI, XN_LO, d - 1)[0], total[:, (d - 1) % 2, :], ACT.Copy).then_inc(upper, 1)
                act.wait_ge(summed, 2 * KD)
                act.activation(core.pair(XN_HI, XN_LO, KD - 1)[0], total[:, (KD - 1) % 2, :], ACT.Copy).then_inc(upper, 1)

            @block.vector
            def _(dve):
                def lower(d):
                    hi, lo = core.pair(XN_HI, XN_LO, d)
                    dve.wait_ge(upper, d + 1)
                    dve.tensor_tensor(lo, total[:, d % 2, :], hi.bitcast(F32), ALU.subtract)

                dve.sem_inc(pairs_free, 3)
                for d in range(KD):
                    for m in range(4):
                        core.split_lo(dve, g0 + 4 * d + m + 2)
                        if m == 0:
                            if d:
                                lower(d - 1)
                            continue
                        n = m - 1
                        dve.wait_ge(opened, 3 * d + n + 1)
                        to = total[:, d % 2, :] if n == 0 else part[:, n - 1, :]
                        dve.tensor_tensor(to, open_gate[:, n, :], ps[:, 2 * n + 1, :], ALU.mult).then_inc(pairs_free, 1)
                        if n:
                            dve.wait_ge(pairs_free, 3 + 3 * d + n + 1)
                            if n == 2:
                                dve.wait_ge(summed, 2 * d + 1)
                            dve.tensor_tensor(total[:, d % 2, :], total[:, d % 2, :], to, ALU.add).then_inc(summed, 1)
                lower(KD - 1)


def residual_stage(core, name, phase, rhs, per_tile=1):
    nc = core.nc
    g0, e0 = core.used, core.evacs
    with ExitStack() as ctx:
        ps = ctx.enter_context(nc.psum_tensor(name + "_ps", [P, 4, T], F32))
        with nc.Block() as block:

            @block.sync
            def _(sp):
                core.stream(sp, phase)

            @block.tensor
            def _(pe):
                if per_tile == 1:
                    pe_gemm(core, pe, KD, KD, rhs, ps)
                else:
                    pe_gemm_deep(core, pe, KD, per_tile, PHASES[phase][1], rhs, ps)

            @block.scalar
            def _(act):
                for n in range(KD * per_tile):
                    core.split_hi(act, g0 + n + 2)

            @block.vector
            def _(dve):
                banks = 4 if per_tile == 1 else 2
                for n in range(KD * per_tile):
                    core.split_lo(dve, g0 + n + 2)
                    if (n + 1) % per_tile == 0:
                        d = n // per_tile
                        dve.wait_ge(core.groups_done, g0 + n + 1)
                        dve.tensor_tensor(core.h[:, d, :], core.h[:, d, :], ps[:, (e0 + d) % banks, :], ALU.add)\
                           .then_inc(core.banks_free, 1)


def load_memory_stage(core):
    mem_in = core.sem("mem_in")
    with core.nc.Block() as block:

        @block.sync
        def _(sp):
            sp.dma_start(memory(core), core.dram["mem_t"]).then_inc(mem_in, 16)
            sp.wait_ge(mem_in, 16)


def memory(core):
    return core.arena[:, 12:16, :].rearrange("p a (n t) -> p (a n) t", n=2)


def memory_parts(core, k):
    halves = lambda tile: core.part(tile + k // 2, (k % 2) * MEM, (k % 2 + 1) * MEM)
    return halves(32), halves(36)


def cross_projections_stage(core):
    nc, a = core.nc, core.arena
    keys = a[:, 16:20, :].rearrange("p a (n t) -> p (a n) t", n=2)
    values = a[:, 20:24, :]
    queries = a[:, 24:32, :]
    g0, e0 = core.used, core.evacs
    with ExitStack() as ctx:
        ps = ctx.enter_context(nc.psum_tensor("cp_ps", [P, 4, T], F32))
        ps_v = ctx.enter_context(nc.psum_tensor("cp_ps_v", [P, 4, T], F32))
        with nc.Block() as block:

            @block.sync
            def _(sp):
                core.load_weights(sp, "ca", RING, 24)
                core.load_weights(sp, "ca", 24, 24 + RING)
                core.preloaded["ca"] = 24 + RING

            @block.tensor
            def _(pe):
                pe_gemm(core, pe, 8, KD, lambda k: memory_parts(core, k), ps, MEM)
                pe_by_token(core, pe, KD, 2 * T, lambda k: memory_parts(core, k), 2, lambda i, half: ps_v[:, 2 * i + half, :])
                pe_gemm(core, pe, 8, KD, lambda k: core.pair(XN_HI, XN_LO, k), ps)

            @block.scalar
            def _(act):
                for n in range(24):
                    core.split_hi(act, g0 + n + 2)
                    act.wait_ge(core.groups_done, g0 + n + 1)
                    if n < 8:
                        act.activation(keys[:, n, :], ps[:, (e0 + n) % 4, 0:MEM], ACT.Copy).then_inc(core.banks_free, 1)
                    elif n >= 16:
                        act.activation(queries[:, n - 16, :], ps[:, (e0 + n - 8) % 4, :], ACT.Copy, scale=1.0 / 16)\
                           .then_inc(core.banks_free, 1)
                    if n == 15:
                        for m in range(4):
                            act.activation(values[:, m, :], ps_v[:, m, :], ACT.Copy)

            @block.vector
            def _(dve):
                for n in range(24):
                    core.split_lo(dve, g0 + n + 2)


class Unit:

    def __init__(self, scores, n, values, add=None, add_query=None, keep=None, gate=None, first=True, last=True, group=0):
        self.scores, self.n, self.values = scores, n, values
        self.add, self.add_query, self.keep, self.gate = add, add_query, keep, gate
        self.first, self.last, self.group = first, last, group


def attention_stage(core, name, units, take):
    nc, a = core.nc, core.arena
    score_sb, turned_sb, stats = a[:, 45:49, :], a[:, 49:51, :], a[:, 51, :]
    count = len(units)
    scores_done = core.sem(name + "_scores_done")
    biased = core.sem(name + "_biased")
    max_ready = core.sem(name + "_max_ready")
    exp_ready = core.sem(name + "_exp_ready")
    inverse = core.sem(name + "_inverse")
    prob_ready = core.sem(name + "_prob_ready")
    turned = core.sem(name + "_turned")
    turned_ready = core.sem(name + "_turned_ready")
    out_done = core.sem(name + "_out_done")
    taken = core.sem(name + "_taken")
    groups = units[-1].group + 1
    last_of = {g: max(i for i, x in enumerate(units) if x.group == g) for g in range(groups)}
    stat = lambda u, n: stats[:, 4 * (u % 4) + n:4 * (u % 4) + n + 1]
    with ExitStack() as ctx:
        ps = ctx.enter_context(nc.psum_tensor(name + "_ps", [P, 8, T], F32))
        with nc.Block() as block:

            @block.tensor
            def _(pe):
                def scores(u):
                    x = units[u]
                    if u >= 4:
                        pe.wait_ge(exp_ready, u - 3)
                    for n, (lhs, rhs) in enumerate(x.scores):
                        mm = pe.matmul(ps[:, u % 4, 0:x.n], lhs, rhs, start=(n == 0), stop=(n == len(x.scores) - 1))
                    mm.then_inc(scores_done, 1)

                def turn(u):
                    x = units[u]
                    pe.wait_ge(prob_ready, u + 1)
                    if u >= 2:
                        pe.wait_ge(turned_ready, u - 1)
                    for lo in range(0, x.n, P):
                        n = min(P, x.n - lo)
                        mm = pe.transpose(ps[0:n, 4 + u % 2, lo:lo + P], score_sb[:, u % 4, lo:lo + n], core.c("ident"))
                    mm.then_inc(turned, 1)

                def output(u):
                    x = units[u]
                    pe.wait_ge(turned_ready, u + 1)
                    if x.group >= 2:
                        pe.wait_ge(taken, x.group - 1)
                    blocks = (x.n + P - 1) // P
                    for out, lhs, blk in x.values:
                        n = min(P, x.n - blk * P)
                        mm = pe.matmul(ps[out[0], 6 + x.group % 2, out[1]], lhs, turned_sb[0:n, u % 2, blk * P:(blk + 1) * P],
                                       start=(x.first and blk == 0), stop=(x.last and blk == blocks - 1), skip_group_check=True)
                    mm.then_inc(out_done, 1)

                for u in range(min(3, count)):
                    scores(u)
                for u in range(count):
                    if u + 3 < count:
                        scores(u + 3)
                    turn(u)
                    if u:
                        output(u - 1)
                output(count - 1)

            @block.scalar
            def _(act):
                def exps(u):
                    x = units[u]
                    act.wait_ge(max_ready, u + 1)
                    src = ps[:, u % 4, 0:x.n] if x.add is None else score_sb[:, u % 4, 0:x.n]
                    if x.add is None and u >= 4:
                        act.wait_ge(turned, u - 3)
                    act.activation(score_sb[:, u % 4, 0:x.n], src, ACT.Exp, bias=stat(u, 0), accum_out=stat(u, 1))\
                       .then_inc(exp_ready, 1)

                def place(u):
                    x = units[u]
                    act.wait_ge(turned, u + 1)
                    if u >= 2:
                        act.wait_ge(out_done, u - 1)
                    rows = min(P, x.n)
                    width = (x.n + P - 1) // P * P
                    act.activation(turned_sb[0:rows, u % 2, 0:width], ps[0:rows, 4 + u % 2, 0:width], ACT.Copy)\
                       .then_inc(turned_ready, 1)

                exps(0)
                for u in range(count):
                    if u + 1 < count:
                        exps(u + 1)
                    place(u)

            @block.vector
            def _(dve):
                def maxima(u):
                    x = units[u]
                    dve.wait_ge(scores_done, u + 1)
                    src = ps[:, u % 4, 0:x.n]
                    if x.add is not None:
                        if u >= 4:
                            dve.wait_ge(turned, u - 3)
                        dst = score_sb[:, u % 4, 0:x.n]
                        if x.add_query is not None:
                            dve.scalar_tensor_tensor(dst, src, x.add_query, x.add, ALU.add, ALU.add).then_inc(biased, 1)
                        else:
                            dve.tensor_tensor(dst, src, x.add, ALU.add).then_inc(biased, 1)
                        dve.wait_ge(biased, u + 1)
                        src = dst
                    elif u >= 4:
                        dve.wait_ge(exp_ready, u - 3)
                    dve.tensor_reduce(stat(u, 0), src, AX.X, ALU.max, negate=True).then_inc(max_ready, 1)

                def normalize(u):
                    x = units[u]
                    dve.wait_ge(exp_ready, u + 1)
                    dve.reciprocal(stat(u, 2), stat(u, 1)).then_inc(inverse, 1)
                    dve.wait_ge(inverse, u + 1)
                    p = score_sb[:, u % 4, 0:x.n]
                    if x.keep is not None:
                        dve.scalar_tensor_tensor(p, p, stat(u, 2), x.keep, ALU.mult, ALU.mult).then_inc(kept, 1)
                        kept_n[0] += 1
                        dve.wait_ge(kept, kept_n[0])
                        dve.tensor_scalar(p, p, x.gate, None, ALU.mult).then_inc(prob_ready, 1)
                    elif x.gate is not None:
                        dve.tensor_scalar(p, p, stat(u, 2), x.gate, ALU.mult, ALU.mult).then_inc(prob_ready, 1)
                    else:
                        dve.tensor_scalar(p, p, stat(u, 2), None, ALU.mult).then_inc(prob_ready, 1)

                kept, kept_n = (core.sem(name + "_kept") if any(x.keep is not None for x in units) else None), [0]
                for u in range(min(2, count)):
                    maxima(u)
                nxt = 0
                for u in range(count):
                    if u + 2 < count:
                        maxima(u + 2)
                    normalize(u)
                    if nxt < groups and last_of[nxt] <= u - 2:
                        dve.wait_ge(out_done, last_of[nxt] + 1)
                        take(dve, nxt, ps[:, 6 + nxt % 2, :]).then_inc(taken, 1)
                        nxt += 1
                for g in range(nxt, groups):
                    dve.wait_ge(out_done, last_of[g] + 1)
                    take(dve, g, ps[:, 6 + g % 2, :]).then_inc(taken, 1)


def cross_attention_stage(core):
    a = core.arena
    keys = a[:, 16:20, :].rearrange("p a (n t) -> p (a n) t", n=2)
    values = a[:, 20:24, :].rearrange("p (i n) t -> p i (n t)", n=2)
    queries = a[:, 24:32, :]
    units = []
    for h in range(4):
        for pair in range(2):
            for i in (2 * pair, 2 * pair + 1):
                cols = slice(i * P, (i + 1) * P)
                scores = [(queries[:, 2 * h + f, cols], keys[:, 2 * h + f, :]) for f in range(2)]
                vals = []
                for f in range(2):
                    for blk in range(2):
                        lo = f * 2 * P + (i % 2) * P
                        vals.append(((slice(0, P), slice(lo, lo + P)),
                                     values[:, blk, h * 256 + f * P:h * 256 + (f + 1) * P], blk))
                units.append(Unit(scores, MEM, vals, group=2 * h + pair))

    def take(dve, g, bank):
        h, pair = g // 2, g % 2
        return dve.tensor_copy(a[:, 2 * h:2 * h + 2, pair * 256:pair * 256 + 256], bank.rearrange("p (f t) -> p f t", f=2))

    attention_stage(core, "ca", units, take)


def ffn_up_stage(core):
    nc, a = core.nc, core.arena
    taps, hidden = a[:, 44:48, :], a[:, 48:50, :]
    g0, e0 = core.used, core.evacs
    now = core.sem("fu_now")
    steps = core.sem("fu_steps")
    gated = core.sem("fu_gated")
    made = core.sem("fu_made")
    upper = core.sem("fu_upper")
    lower_done = core.sem("fu_lower_done")
    with ExitStack() as ctx:
        ps = ctx.enter_context(nc.psum_tensor("fu_ps", [P, 4, T], F32))
        with nc.Block() as block:

            @block.sync
            def _(sp):
                core.stream(sp, "up")

            @block.tensor
            def _(pe):
                pe_gemm(core, pe, 2 * NF, KD, lambda k: core.pair(XN_HI, XN_LO, k), ps)

            which = lambda n: n // 2 + NF * (n % 2)

            @block.scalar
            def _(act):
                def split(j):
                    act.wait_ge(made, j + 1)
                    act.activation(core.pair(0, NF, j)[0], hidden[:, j % 2, :], ACT.Copy).then_inc(upper, 1)

                for n in range(2 * NF):
                    core.split_hi(act, g0 + n + 2)
                    if n % 2 and n >= 3:
                        split(n // 2 - 1)
                    act.wait_ge(core.groups_done, g0 + n + 1)
                    if n >= 4:
                        act.wait_ge(made, n // 2 - 1)
                    act.activation(taps[:, n % 4, :], ps[:, (e0 + n) % 4, :], ACT.Identity, scale=core.v("ffn_conv_w", 88 + which(n)),
                                   bias=core.v("ffn_conv_b", which(n))).then_inc(now, 1)
                    if n % 2:
                        act.wait_ge(core.banks_free, 4 + e0 + n)
                        act.activation(taps[:, (n - 1) % 4, :], taps[:, (n - 1) % 4, :], ACT.Silu).then_inc(gated, 1)
                split(NF - 1)

            @block.vector
            def _(dve):
                def lower(j):
                    hi, lo = core.pair(0, NF, j)
                    dve.wait_ge(upper, j + 1)
                    dve.tensor_tensor(lo, hidden[:, j % 2, :], hi.bitcast(F32), ALU.subtract).then_inc(lower_done, 1)

                for n in range(2 * NF):
                    core.split_lo(dve, g0 + n + 2)
                    if n % 2 == 0 and n >= 4:
                        lower(n // 2 - 2)
                    y, x = taps[:, n % 4, :], ps[:, (e0 + n) % 4, :]
                    dve.wait_ge(now, n + 1)
                    dve.scalar_tensor_tensor(y[:, 1:T], x[:, 0:T - 1], core.v("ffn_conv_w", 44 + which(n)), y[:, 1:T],
                                             ALU.mult, ALU.add).then_inc(steps, 1)
                    dve.wait_ge(steps, n + 1)
                    dve.scalar_tensor_tensor(y[:, 2:T], x[:, 0:T - 2], core.v("ffn_conv_w", which(n)), y[:, 2:T],
                                             ALU.mult, ALU.add).then_inc(core.banks_free, 1)
                    if n % 2:
                        dve.wait_ge(core.banks_free, 4 + e0 + n + 1)
                        dve.wait_ge(gated, n // 2 + 1)
                        dve.tensor_tensor(hidden[:, n // 2 % 2, :], taps[:, (n - 1) % 4, :], y, ALU.mult).then_inc(made, 1)
                lower(NF - 2)
                lower(NF - 1)


def bias_stage(core):
    nc, a, dram = core.nc, core.arena, core.dram
    bucket = a[0:32, 49:51, :].rearrange("p a t -> p (a t)")
    table = core.small[0:32, 48:56]
    row = a[0:HEADS, 51:53, :].rearrange("p a t -> p (a t)")
    SPREAD = 896
    spread = a[:, 12:26, :].rearrange("p a t -> p (a t)").rearrange("p (h y) -> p h y", h=HEADS)
    window = a[:, 35:43, :]
    summary = a[:, 43:45, :].rearrange("p a t -> p (a t)")[:, 0:NT * HEADS * NC_CMP]
    mask = a[:, 8, :]
    scratch = nc.dram_tensor("bias_rows", (HEADS * VEC_DIST,), F32)
    bucket_in, table_in, row_out = core.sem("bi_bucket_in"), core.sem("bi_table_in"), core.sem("bi_row_out")
    row_done, row_ready = core.sem("bi_row_done"), core.sem("bi_row_ready")
    spread_in = core.sem("bi_spread_in")
    head_in = core.sem("bi_head_in")
    flipped, cleared = core.sem("bi_flipped"), core.sem("bi_cleared")
    w_taken = core.sem("bi_w_taken")
    with ExitStack() as ctx:
        ps = ctx.enter_context(nc.psum_tensor("bi_ps", [P, 8, T], F32))
        with nc.Block() as block:

            @block.sync
            def _(sp):
                sp.dma_start(bucket, dram["bucket"]).then_inc(bucket_in, 16)
                sp.dma_start(table, dram["table"]).then_inc(table_in, 16)
                sp.dma_start(a[0:HEADS, 9:11, :].rearrange("p a t -> p (a t)"), dram["head_row"]).then_inc(head_in, 16)
                sp.wait_ge(row_ready, 2)
                sp.dma_start(scratch.ap().rearrange("(h y) -> h y", h=HEADS), row).then_inc(row_out, 16)
                sp.wait_ge(row_out, 16)
                sp.dma_start(spread, bass.AP(scratch, 0, [[1, P], [VEC_DIST, HEADS], [1, SPREAD]])).then_inc(spread_in, 16)
                sp.wait_ge(head_in, 16)

            @block.tensor
            def _(pe):
                pe.wait_ge(bucket_in, 16)
                pe.wait_ge(table_in, 16)
                for n in range(2):
                    pe.matmul(ps[0:HEADS, n, :], table, bucket[:, n * T:(n + 1) * T], start=True, stop=True).then_inc(row_done, 1)
                pe.wait_ge(spread_in, 16)
                for h in range(HEADS):
                    if h == 6:
                        pe.wait_ge(w_taken, 2)
                    pe.matmul(ps[:, (2 + h) % 8, :], core.c("flip"), spread[:, h, 0:T], start=True, stop=True).then_inc(flipped, 1)
                pe.wait_ge(w_taken, 4)
                per = HEADS * NC_CMP
                for i in range(NT):
                    lo = 415 - i * P
                    pe.matmul(ps[:, 2 + i // 2, (i % 2) * per:(i % 2 + 1) * per], core.c("flip"),
                              spread[:, :, lo:lo + 16 * (NC_CMP - 1) + 1:16], start=True, stop=True).then_inc(flipped, 1)

            @block.scalar
            def _(act):
                for n in range(2):
                    act.wait_ge(row_done, n + 1)
                    act.activation(row[:, n * T:(n + 1) * T], ps[0:HEADS, n, :], ACT.Copy).then_inc(row_ready, 1)

            @block.vector
            def _(dve):
                dve.memset(mask, 0.0).then_inc(cleared, 1)
                dve.wait_ge(cleared, 1)
                dve.tensor_copy(mask[:, T - P:T], core.c("causal_add")).then_inc(cleared, 1)
                dve.wait_ge(cleared, 2)
                dve.wait_ge(row_ready, 2)
                for h in range(HEADS):
                    dve.wait_ge(flipped, h + 1)
                    dve.tensor_tensor(window[:, h, :], ps[:, (2 + h) % 8, :], mask, ALU.add).then_inc(w_taken, 1)
                half = NT * HEADS * NC_CMP // 2
                for n in range(2):
                    dve.wait_ge(flipped, HEADS + 2 * n + 2)
                    view = lambda x: x.rearrange("p (i h b) -> p i h b", i=2, h=HEADS)
                    mask_add = core.c("cmp_add", 2 * n * NC_CMP, 2 * NC_CMP).rearrange("p (i b) -> p i b", i=2)
                    dve.tensor_tensor(view(summary[:, n * half:(n + 1) * half]), view(ps[:, 2 + n, 0:half]),
                                      mask_add.unsqueeze(2).broadcast_to([P, 2, HEADS, NC_CMP]), ALU.add)


def second_projections_stage(core):
    nc, a, dram = core.nc, core.arena, core.dram
    by_feature = a[:, 12:28, :]
    fox_value = a[:, 28:32, :]
    group_value = a[:, 32:34, :].rearrange("p a (n t) -> p (a n) t", n=2)
    logits = a[:, 34, 0:NT * 32].rearrange("p (i n) -> p i n", i=NT)
    small_w, small_hi, small_lo = a[:, 11, 0:KD * 32], core.part(54, 0, KD * 32), core.part(54, KD * 32, 2 * KD * 32)
    g0, e0 = core.used, core.evacs
    small_in = core.sem("sp_small_in")
    small_upper = core.sem("sp_small_upper")
    small_split = core.sem("sp_small_split")
    small_done = core.sem("sp_small_done")
    fox_taken = core.sem("sp_fox_taken")
    with ExitStack() as ctx:
        ps = ctx.enter_context(nc.psum_tensor("sp_ps", [P, 4, T], F32))
        ps_v = ctx.enter_context(nc.psum_tensor("sp_ps_v", [P, 4, T], F32))
        with nc.Block() as block:

            @block.sync
            def _(sp):
                core.stream(sp, "in2")

            @block.tensor
            def _(pe):
                x = lambda k: core.pair(XN_HI, XN_LO, k)
                pe_gemm(core, pe, 16, KD, x, ps)
                pe_by_token(core, pe, 4, T, x, NT, lambda i, half: ps_v[:, i, :])
                pe.wait_ge(core.banks_free, 4 + e0 + 16)
                pe_by_token(core, pe, 2, 256, x, NT, lambda i, half: ps[:, i, :])
                pe.wait_ge(small_split, 1)
                pe.wait_ge(fox_taken, NT)
                for i in range(NT):
                    for k in range(KD):
                        cols = slice(i * P, (i + 1) * P)
                        mm = product(pe, ps_v[:, 0, i * 32:(i + 1) * 32], (x(k)[0][:, cols], x(k)[1][:, cols]),
                                     (small_hi[:, k * 32:(k + 1) * 32], small_lo[:, k * 32:(k + 1) * 32]), k == 0, k == KD - 1)
                mm.then_inc(small_done, 1)

            @block.scalar
            def _(act):
                act.dma_start(small_w, dram["w_small2"]).then_inc(small_in, 16)
                for n in range(22):
                    core.split_hi(act, g0 + n + 2)
                    act.wait_ge(core.groups_done, g0 + n + 1)
                    if n < 16:
                        scale = HD ** -0.5 if n < 4 or 8 <= n < 12 else 1.0
                        act.activation(by_feature[:, n, :], ps[:, (e0 + n) % 4, :], ACT.Copy, scale=scale)\
                           .then_inc(core.banks_free, 1)
                    if n == 8:
                        act.wait_ge(small_in, 16)
                        act.activation(small_hi, small_w, ACT.Copy).then_inc(small_upper, 1)
                    if n == 19:
                        for i in range(NT):
                            act.activation(fox_value[:, i, :], ps_v[:, i, :], ACT.Copy).then_inc(fox_taken, 1)
                for i in range(NT):
                    act.activation(group_value[:, i, :], ps[:, i, 0:256], ACT.Copy)
                act.wait_ge(small_done, 1)
                act.activation(logits, ps_v[:, 0, 0:NT * 32].rearrange("p (i n) -> p i n", i=NT), ACT.Copy)

            @block.vector
            def _(dve):
                for n in range(22):
                    core.split_lo(dve, g0 + n + 2)
                    if n == 10:
                        dve.wait_ge(small_upper, 1)
                        dve.tensor_tensor(small_lo, small_w, small_hi.bitcast(F32), ALU.subtract).then_inc(small_split, 1)


def forget_stage(core):
    nc, a = core.nc, core.arena
    logits = a[:, 34, 0:NT * 32].rearrange("p (i n) -> p i n", i=NT)
    gates = a[:, 34, 128:128 + NT * 24].rearrange("p (i n) -> p i n", i=NT)
    x = a[:, 34, 256:288].rearrange("p (i n) -> p i n", i=NT)
    soft = a[:, 34, 288:320].rearrange("p (i n) -> p i n", i=NT)
    row = a[0:HEADS, 11, :]
    sums = core.small[:, 0:32].rearrange("p (i n) -> p i n", i=NT)
    shifted, logged, steps = core.sem("fg_shifted"), core.sem("fg_logged"), core.sem("fg_steps")
    soft_ready, summed = core.sem("fg_soft_ready"), core.sem("fg_summed")
    with ExitStack() as ctx:
        ps = ctx.enter_context(nc.psum_tensor("fg_ps", [P, 2, T], F32))
        with nc.Block() as block:

            @block.vector
            def _(dve):
                bias = core.vec[:, VEC_AT["b_forget"]:VEC_AT["b_forget"] + 8].unsqueeze(1).broadcast_to([P, NT, 8])
                dve.tensor_tensor(x, logits[:, :, 0:8], bias, ALU.add).then_inc(shifted, 1)
                dve.wait_ge(shifted, 1)
                dve.wait_ge(logged, 3)
                dve.tensor_scalar(x, x, -1.0, 0.0, ALU.mult, ALU.max).then_inc(steps, 1)
                dve.wait_ge(steps, 1)
                dve.tensor_tensor(soft, soft, x, ALU.add).then_inc(soft_ready, 1)
                dve.wait_ge(summed, 1)
                dve.tensor_scalar(sums, ps[:, 0, 0:32].rearrange("p (i n) -> p i n", i=NT), -1.0, None, ALU.mult)

            @block.scalar
            def _(act):
                act.wait_ge(shifted, 1)
                act.activation(soft, x, ACT.Abs).then_inc(logged, 1)
                act.wait_ge(logged, 1)
                act.activation(soft, soft, ACT.Exp, scale=-1.0).then_inc(logged, 1)
                act.wait_ge(logged, 2)
                act.activation(soft, soft, ACT.Ln, bias=1.0).then_inc(logged, 1)
                act.activation(gates, logits[:, :, 8:32], ACT.Sigmoid)
                act.wait_ge(summed, 1)
                act.activation(row, ps[0:HEADS, 1, :], ACT.Copy)

            @block.tensor
            def _(pe):
                pe.wait_ge(soft_ready, 1)
                for i in range(NT):
                    for j in range(i + 1):
                        pe.matmul(ps[:, 0, i * 8:(i + 1) * 8], core.c("upper" if j == i else "ones"), soft[:, j, :],
                                  start=(j == 0), stop=(j == i))
                for i in range(NT):
                    for j in range(i + 1):
                        mm = pe.matmul(ps[0:HEADS, 1, i * P:(i + 1) * P], soft[:, j, :], core.c("upper" if j == i else "ones"),
                                       start=(j == 0), stop=(j == i))
                mm.then_inc(summed, 1)


def compress_stage(core):
    nc, a, dram = core.nc, core.arena, core.dram
    B = NC_CMP
    shifted = a[:, 49:53, :].rearrange("p (s g) t -> p s g t", s=2)
    pieces = [a[:, lo:lo + 4, :].rearrange("p a t -> p (a t)").rearrange("p (l m) -> p l m", l=16) for lo in (0, 4, 45, 0)]
    w2 = a[:, 53, 256:512].rearrange("p (s f d) -> p s f d", s=2, f=2)
    hidden = a[:, 53, 0:8 * B].rearrange("p (s f n) -> p s f n", s=2, f=2)
    bias = a[:, 53, 8 * B:8 * B + 4].rearrange("p (s f) -> p s f", s=2)
    keys, values = a[:, 54, 0:B], a[0:B, 54, 128:256]
    piece_in = [core.sem(f"cm_piece_in{n}") for n in range(4)]
    w2_in = [core.sem("cm_w2_k_in"), core.sem("cm_w2_v_in")]
    shift_in = [core.sem(f"cm_shift_in{n}") for n in range(4)]
    copied, pos_done, pos_ready = core.sem("cm_copied"), core.sem("cm_pos_done"), core.sem("cm_pos_ready")
    hidden_done, hidden_ready, out_done = core.sem("cm_hidden_done"), core.sem("cm_hidden_ready"), core.sem("cm_out_done")
    with ExitStack() as ctx:
        ps = ctx.enter_context(nc.psum_tensor("cm_ps", [P, 8, T], F32))
        with nc.Block() as block:

            @block.sync
            def _(sp):
                for n in range(3):
                    sp.dma_start(pieces[n], dram["cmp_w1_" + "kv"[n // 2]][:, :, (n % 2) * P:(n % 2 + 1) * P])\
                      .then_inc(piece_in[n], 16)
                for s, name in enumerate("kv"):
                    sp.dma_start(w2[:, s], dram["cmp_w2_" + name]).then_inc(w2_in[s], 16)
                for s in range(2):
                    src = a[:, 24 + s, :]
                    for g in range(2):
                        rows = slice(HD * g, HD * g + HD)
                        sp.dma_start(shifted[HD:P, s, g, 0:T - 1], src[rows, 1:T]).then_inc(shift_in[2 * s + g], 16)
                sp.wait_ge(hidden_done, 1)
                sp.dma_start(pieces[3], dram["cmp_w1_v"][:, :, P:2 * P]).then_inc(piece_in[3], 16)

            @block.gpsimd
            def _(pool):
                for s in range(2):
                    for g in range(2):
                        ins = pool.tensor_copy(shifted[0:HD, s, g, 0:T - 1], a[HD * g:HD * g + HD, 24 + s, 0:T - 1])
                ins.then_inc(copied, 1)

            @block.tensor
            def _(pe):
                pe.wait_ge(copied, 1)
                for n in range(4):
                    s, f = n // 2, n % 2
                    at_pe = VEC_AT["pe_" + "kv"[s]]
                    pe.wait_ge(piece_in[n], 16)
                    for l in range(16):
                        mm = pe.matmul(ps[:, 4 * s + f, 0:1], pieces[n][:, l, :], core.vec[:, at_pe + l:at_pe + l + 1],
                                       start=(l == 0), stop=(l == 15))
                    mm.then_inc(pos_done, 1)
                    if f == 0:
                        pe.wait_ge(shift_in[2 * s], 16)
                        pe.wait_ge(shift_in[2 * s + 1], 16)
                    for l in range(16):
                        mm = pe.matmul(ps[:, 4 * s + 2 + f, 0:2 * B], pieces[n][:, l, :],
                                       shifted[:, s, :, 2 * l:2 * l + 16 * (B - 1) + 1:16], start=(l == 0), stop=(l == 15))
                    mm.then_inc(hidden_done, 1)
                pe.wait_ge(hidden_ready, 4)
                pe.wait_ge(w2_in[0], 16)
                pe.wait_ge(w2_in[1], 16)
                pe.wait_ge(pos_ready, 4)
                for g in range(2):
                    for f in range(2):
                        pe.matmul(ps[HD * g:HD * g + HD, 0, 0:B], w2[:, 0, f, :], hidden[:, 0, f, g * B:(g + 1) * B],
                                  start=(f == 0), stop=(f == 1))
                for g in range(2):
                    for f in range(2):
                        mm = pe.matmul(ps[0:B, 1, g * HD:(g + 1) * HD], hidden[:, 1, f, g * B:(g + 1) * B], w2[:, 1, f, :],
                                       start=(f == 0), stop=(f == 1))
                mm.then_inc(out_done, 1)

            @block.vector
            def _(dve):
                for n in range(4):
                    dve.wait_ge(pos_done, n + 1)
                    dve.tensor_copy(bias[:, n // 2, n % 2:n % 2 + 1], ps[:, 4 * (n // 2) + n % 2, 0:1]).then_inc(pos_ready, 1)
                dve.wait_ge(out_done, 1)
                dve.tensor_copy(keys, ps[:, 0, 0:B])
                dve.tensor_copy(values, ps[0:B, 1, 0:P])

            @block.scalar
            def _(act):
                for n in range(4):
                    act.wait_ge(hidden_done, n + 1)
                    act.wait_ge(pos_ready, n + 1)
                    act.activation(hidden[:, n // 2, n % 2, :], ps[:, 4 * (n // 2) + 2 + n % 2, 0:2 * B], ACT.Silu,
                                   bias=bias[:, n // 2, n % 2:n % 2 + 1]).then_inc(hidden_ready, 1)


def fox_attention_stage(core):
    a = core.arena
    query, key, value = a[:, 12:16, :], a[:, 16:20, :], a[:, 28:32, :]
    head_row = a[0:HEADS, 9:11, :].rearrange("p a t -> p (a t)")
    row, mask = a[0:HEADS, 11, :], a[:, 8, :]
    units = []
    for h in range(HEADS):
        c, rows = h // 2, slice(HD * (h % 2), HD * (h % 2) + HD)
        for i in range(NT):
            n = (i + 1) * P
            cols = slice(i * P, (i + 1) * P)
            scores = [(query[rows, c, cols], key[rows, c, 0:n]), (head_row[:, h * P:(h + 1) * P], row[:, 0:n])]
            vals = [((rows, cols), value[:, j, h * HD:(h + 1) * HD], j) for j in range(i + 1)]
            units.append(Unit(scores, n, vals, add=mask[:, T - n:T], add_query=core.small[:, i * 8 + h:i * 8 + h + 1], group=c))
    attention_stage(core, "fox", units, lambda dve, g, bank: dve.tensor_copy(a[:, g, :], bank))


def sparse_attention_stage(core):
    a = core.arena
    query, select_key, window_key = a[:, 20:24, :], a[:, 26, :], a[:, 27, :]
    group_value = a[:, 32:34, :].rearrange("p a (n t) -> p (a n) t", n=2)
    gates = a[:, 34, 128:128 + NT * 24]
    window = a[:, 35:43, :]
    summary = a[:, 43:45, :].rearrange("p a t -> p (a t)")[:, 0:NT * HEADS * NC_CMP]
    cmp_key, cmp_value = a[:, 54, 0:NC_CMP], a[0:NC_CMP, 54, 128:256]
    units = []
    for h2 in range(HEADS):
        h, c, rows = h2, h2 // 2, slice(HD * (h2 % 2), HD * (h2 % 2) + HD)
        g = h // 4
        q_rows = slice(HD * g, HD * g + HD)
        for i in range(NT):
            n = (i + 1) * P
            cols = slice(i * P, (i + 1) * P)
            q = query[q_rows, h % 4, cols]
            gate = lambda b: gates[:, i * 24 + 3 * h + b:i * 24 + 3 * h + b + 1]
            for b, k in ((1, select_key), (2, window_key)):
                lo = P * (b - 1) + g * HD
                vals = [((rows, cols), group_value[:, j, lo:lo + HD], j) for j in range(i + 1)]
                units.append(Unit([(q, k[q_rows, 0:n])], n, vals, add=window[:, h, T - n:T], gate=gate(b), first=(b == 1),
                                  last=False, group=c))
            add = summary[:, (i * HEADS + h) * NC_CMP:(i * HEADS + h + 1) * NC_CMP]
            units.append(Unit([(q, cmp_key[q_rows, :])], NC_CMP, [((rows, cols), cmp_value[:, g * HD:(g + 1) * HD], 0)], add=add,
                              keep=core.c("cmp_keep", i * NC_CMP, NC_CMP), gate=gate(0), first=False, last=True, group=c))
    attention_stage(core, "nsa", units, lambda dve, g, bank: dve.tensor_copy(a[:, 4 + g, :], bank))


def second_gates_stage(core):
    nc, a = core.nc, core.arena
    opened_gate, part, total = a[:, 44:46, :], a[:, 46, :], a[:, 47:49, :]
    g0 = core.used
    tiles_free = core.sem("g2_tiles_free")
    opened, summed = core.sem("g2_opened"), core.sem("g2_summed")
    branch_done = core.sem("g2_branch_done")
    upper = core.sem("g2_upper")
    with ExitStack() as ctx:
        ps = ctx.enter_context(nc.psum_tensor("g2_ps", [P, 8, T], F32))
        with nc.Block() as block:

            @block.sync
            def _(sp):
                core.stream(sp, "gates2")

            @block.tensor
            def _(pe):
                with pe.Fori(0, KD // 4) as turn:
                    for q in range(4):
                        bank = 4 * (q % 2)
                        pe.wait_ge(tiles_free, turn * 4 + q + 1)
                        for n in range(3):
                            g = g0 + 3 * q + n
                            core.wait_weights(pe, g, turn, 12)
                            for b in range(KD):
                                w = core.weights(g, b * P, (b + 1) * P)
                                if n < 2:
                                    mm = product(pe, ps[:, bank + n, :], w, core.pair(XN_HI, XN_LO, b), b == 0, b == KD - 1)
                                else:
                                    mm = product(pe, ps[:, bank + 2 + b // 4, :], w, core.pair(12, 20, b), b % 4 == 0, b % 4 == 3)
                            mm.then_inc(core.groups_done, 1)
                core.used += 24

            @block.scalar
            def _(act):
                def split(d):
                    act.wait_ge(summed, d + 1)
                    act.activation(core.pair(28, 36, d)[0], total[:, d % 2, :], ACT.Copy).then_inc(upper, 1)

                for d in range(KD):
                    for n in range(3):
                        core.split_hi(act, g0 + 3 * d + n + 2)
                        if n < 2:
                            act.wait_ge(core.groups_done, g0 + 3 * d + n + 1)
                            if d:
                                act.wait_ge(tiles_free, 2 + d)
                            act.activation(opened_gate[:, n, :], ps[:, 4 * (d % 2) + n, :], ACT.Sigmoid).then_inc(opened, 1)
                        elif d:
                            split(d - 1)
                split(KD - 1)

            @block.vector
            def _(dve):
                def lower(d):
                    hi, lo = core.pair(28, 36, d)
                    dve.wait_ge(upper, d + 1)
                    dve.tensor_tensor(lo, total[:, d % 2, :], hi.bitcast(F32), ALU.subtract)

                dve.sem_inc(tiles_free, 2)
                for d in range(KD):
                    for n in range(3):
                        core.split_lo(dve, g0 + 3 * d + n + 2)
                    if d >= 1:
                        lower(d - 1)
                    dve.wait_ge(core.groups_done, g0 + 3 * d + 3)
                    dve.wait_ge(opened, 2 * d + 2)
                    if d:
                        dve.wait_ge(summed, d)
                    dve.tensor_tensor(part, opened_gate[:, 1, :], ps[:, 4 * (d % 2) + 3, :], ALU.mult).then_inc(branch_done, 1)
                    dve.tensor_tensor(total[:, d % 2, :], opened_gate[:, 0, :], ps[:, 4 * (d % 2) + 2, :], ALU.mult)\
                       .then_inc(tiles_free, 1)
                    dve.wait_ge(branch_done, d + 1)
                    dve.wait_ge(tiles_free, 2 + d + 1)
                    dve.tensor_tensor(total[:, d % 2, :], total[:, d % 2, :], part, ALU.add).then_inc(summed, 1)
                lower(KD - 1)


def ff1_stage(core, name, phase):
    nc = core.nc
    lifted_sb, product_sb = core.arena[:, 32:34, :], core.arena[:, 34:36, :]
    g0, e0, count = core.used, core.evacs, PHASES[phase][0]
    lifted, upper = core.sem(name + "_lifted"), core.sem(name + "_upper")
    with ExitStack() as ctx:
        ps = ctx.enter_context(nc.psum_tensor(name + "_ps", [P, 4, T], F32))
        with nc.Block() as block:

            @block.sync
            def _(sp):
                core.stream(sp, phase)

            @block.tensor
            def _(pe):
                pe_gemm(core, pe, count, KD, lambda k: core.pair(XN_HI, XN_LO, k), ps)

            @block.scalar
            def _(act):
                def split(n):
                    act.wait_ge(core.banks_free, 4 + e0 + n + 1)
                    act.activation(core.pair(0, 16, n)[0], product_sb[:, n % 2, :], ACT.Copy).then_inc(upper, 1)

                for n in range(count):
                    core.split_hi(act, g0 + n + 2)
                    if n:
                        split(n - 1)
                split(count - 1)

            @block.vector
            def _(dve):
                def lower(n):
                    hi, lo = core.pair(0, 16, n)
                    dve.wait_ge(upper, n + 1)
                    dve.tensor_tensor(lo, product_sb[:, n % 2, :], hi.bitcast(F32), ALU.subtract)

                for n in range(count):
                    bank = ps[:, (e0 + n) % 4, :]
                    core.split_lo(dve, g0 + n + 2)
                    if n >= 2:
                        lower(n - 2)
                    dve.wait_ge(core.groups_done, g0 + n + 1)
                    dve.tensor_scalar(lifted_sb[:, n % 2, :], bank, 0.0, None, ALU.max).then_inc(lifted, 1)
                    dve.wait_ge(lifted, n + 1)
                    dve.tensor_tensor(product_sb[:, n % 2, :], lifted_sb[:, n % 2, :], bank, ALU.mult).then_inc(core.banks_free, 1)
                lower(count - 2)
                lower(count - 1)


def store_stage(core):
    out_stored = core.sem("out_stored")
    with core.nc.Block() as block:

        @block.sync
        def _(sp):
            sp.dma_start(core.dram["out"], core.arena[:, 0:KD, :]).then_inc(out_stored, 16)
            sp.wait_ge(out_stored, 16)


def norm_h(name, gain, **kw):
    kw = kw or {"split": 1}
    return lambda core: norm_stage(core, name, lambda k: core.h[:, k, :], gain,
                                   **({"split": lambda k: core.pair(XN_HI, XN_LO, k)} if kw == {"split": 1} else
                                      {x: y(core) for x, y in kw.items()}))


def norm_memory(core):
    norm_stage(core, "nmem", lambda k: memory(core)[:, k, :], "norm_mem", split=lambda k: memory_parts(core, k), width=MEM)


def norm_again(core):
    norm_stage(core, "nmix2", lambda k: core.h[:, k, :], "norm_mix", split=lambda k: core.pair(36, 44, k), scratch=55)


def merged_parts(core):
    return lambda k: core.pair(XN_HI, XN_LO, k)


STAGES = [
    setup_stage,
    norm_h("nmix", "norm_mix"),
    proj_stage,
    stick_breaking_stage,
    time_mix_stage,
    time_mix_scale_stage,
    time_mix_chunks_stage,
    time_mix_out_stage,
    norm_again,
    lambda core: split_stage(core, "ys", 12, 0, 12, 24),
    gates_stage,
    lambda core: residual_stage(core, "mix", "mix", merged_parts(core)),
    load_memory_stage,
    norm_memory,
    norm_h("nca", "norm_ca"),
    cross_projections_stage,
    cross_attention_stage,
    lambda core: split_stage(core, "cs", KD, 0, XN_HI, XN_LO),
    lambda core: residual_stage(core, "cawo", "ca", merged_parts(core)),
    norm_h("nffn", "norm_ffn"),
    ffn_up_stage,
    lambda core: residual_stage(core, "down", "down", lambda k: core.pair(0, NF, k), per_tile=2),
    norm_h("nfirst", "norm_final", dst=lambda core: lambda k: core.h[:, k, :]),
    clear_semaphores_stage,
    norm_h("nattn", "g_attn_2"),
    bias_stage,
    second_projections_stage,
    forget_stage,
    compress_stage,
    fox_attention_stage,
    sparse_attention_stage,
    lambda core: split_stage(core, "y2", KD, 0, 12, 20),
    second_gates_stage,
    lambda core: residual_stage(core, "out2", "out2", lambda k: core.pair(28, 36, k)),
    norm_h("nmlp", "g_mlp_2"),
    lambda core: ff1_stage(core, "f1a", "ff1a"),
    lambda core: residual_stage(core, "f2a", "ff2a", lambda k: core.pair(0, 16, k), per_tile=2),
    lambda core: ff1_stage(core, "f1b", "ff1b"),
    lambda core: residual_stage(core, "f2b", "ff2b", lambda k: core.pair(0, 16, k), per_tile=2),
    norm_h("nfinal", "g_final_2", dst=lambda core: lambda k: core.arena[:, k, :]),
    store_stage,
]


def hybrid_decoder_kernel(nc, dram, stages):
    with ExitStack() as ctx:
        core = Core(nc, ctx, dram)
        for stage in stages:
            stage(core)



def _tiles(w):
    k, n = w.shape
    return w.reshape(k // P, P, n // P, P).transpose(2, 1, 0, 3).reshape(n // P, P, k)


def _by_rows(w, per):
    k, n = w.shape
    return w.reshape(k // (per * P), per, P, n).transpose(0, 2, 1, 3).reshape(k // (per * P), P, per * n)


def _columns(v):
    return v.reshape(-1, P).T


def _constants():
    c = {name: np.zeros((P, cols), np.float32) for name, cols in CONSTS}
    i = np.arange(P)
    row, col = i[:, None], i[None, :]
    c["ident"][:] = row == col
    c["ones"][:] = 1.0
    c["head_ones"][:] = row // HD == col // HD
    c["upper"][:] = row <= col
    c["causal4"][:] = np.concatenate([row < col, row <= col, row < col, row <= col], axis=1)
    c["neg_tri"][:] = -1.0 * (row >= col)
    c["neg_ones"][:] = -1.0
    c["neg_diag_t"][:] = np.where(row < col, 0.0, NEG)
    for n in range(7):
        b = 1 << n
        c["level"][:, n * P:(n + 1) * P] = (col // b % 2 == 1) & (row // b == col // b - 1)
    c["flip"][:] = row + col == P - 1
    c["causal_add"][:] = np.where(col <= row, 0.0, NEG)
    for t in range(NT):
        for b in range(NC_CMP):
            ok = 16 * b + 31 <= t * P + i
            c["cmp_add"][:, t * NC_CMP + b] = np.where(ok, 0.0, NEG)
            c["cmp_keep"][:, t * NC_CMP + b] = ok
    return np.concatenate([c[name] for name, _ in CONSTS], axis=1)


def _bucket_rows():
    dist = np.maximum(511 - np.arange(VEC_DIST), 0)
    exact = 16
    nf = np.maximum(dist, exact).astype(np.float32)
    log_b = exact + (np.log(nf / np.float32(exact)) / np.float32(math.log(128 / exact)) * np.float32(32 - exact)).astype(np.int32)
    bucket = np.where(dist < exact, dist, np.minimum(log_b, 31))
    return (np.arange(32)[:, None] == bucket[None, :]).astype(np.float32)


def _layout(i):
    f = lambda name: np.asarray(i[name])[0]
    w_comb, w_in = f("w_comb"), f("w_in_2")
    a = {}
    a["x_t"] = np.asarray(i["x"])[0].T.reshape(KD, P, T).transpose(1, 0, 2)
    a["mem_t"] = np.asarray(i["mem"])[0].T.reshape(KD, P, MEM).transpose(1, 0, 2)
    conv, sb, gate, rwkv = w_comb[:, 0:1536], w_comb[:, 1536:3072], w_comb[:, 3072:6144], w_comb[:, 6144:]
    ct = _tiles(conv)
    order = [x for t in range(4) for x in (4 + t, 8 + t, t)]
    a["w_proj"] = np.concatenate([_tiles(rwkv), ct[order], _tiles(sb[:, 0:1024]), _by_rows(sb[:, 1024:], 2)])
    gt = _tiles(gate).reshape(3, 8, P, 1024)
    bt = np.stack([_tiles(f("branch_proj")[n]) for n in range(3)])
    both = np.concatenate([gt, bt], axis=3)
    a["w_gates"] = both.transpose(1, 2, 0, 3).reshape(8, P, 4, 9 * P).transpose(0, 2, 1, 3).reshape(32, P, 9 * P)
    a["w_mix"] = _tiles(f("w_mix_out"))
    kv = f("ca_wkv")
    a["w_ca"] = np.concatenate([_tiles(kv[:, 0:1024]), _by_rows(kv[:, 1024:], 1), _tiles(f("ca_wq")), _tiles(f("ca_wo"))])
    up = _tiles(f("ffn_up"))
    a["w_up"] = up[[x for t in range(NF) for x in (t, NF + t)]]
    a["w_down"] = _tiles(f("ffn_down")).reshape(8, P, 2, 11 * P).transpose(0, 2, 1, 3).reshape(16, P, 11 * P)
    cuts = np.cumsum((512, 512, 512, 8, 512, 128, 128, 128, 128, 128, 128, 24, 1024, 1024))[:-1]
    fq, fk, fv, fl, nq, kc, vc, ksl, vsl, kwn, vwn, ng, ga, gb = np.split(w_in, cuts, axis=1)
    nq = nq.reshape(D, 2, 4, HD).transpose(0, 2, 1, 3).reshape(D, 512)
    a["w_in2"] = np.concatenate([_tiles(np.concatenate([fq, fk, nq, kc, vc, ksl, kwn], axis=1)), _by_rows(fv, 2),
                                 _by_rows(np.concatenate([vsl, vwn], axis=1), 4)])
    a["w_small2"] = _by_rows(np.concatenate([fl, ng], axis=1), 8)[0]
    bf, bn = _tiles(f("w_br_fox_2")), _tiles(f("w_br_nsa_2"))
    a["w_gates2"] = np.stack([_tiles(ga), _tiles(gb), np.concatenate([bf, bn], axis=2)], axis=1).reshape(24, P, 1024)
    a["w_out2"] = _tiles(f("w_out_2"))
    ff1 = _tiles(f("w_ff1_2"))
    ff2 = _tiles(f("w_ff2_2")).reshape(8, P, 4, 1024).transpose(0, 2, 1, 3)
    for n, half in enumerate("ab"):
        a["w_ff1" + half] = ff1[16 * n:16 * n + 16]
        a["w_ff2" + half] = ff2[:, 2 * n:2 * n + 2].reshape(16, P, 1024)
    a["wa_lora"] = np.concatenate([f("w_lora"), f("a_lora")])
    a["g_lora_t"] = f("g_lora")
    a["table"] = np.asarray(i["rel_bias_table_2"])
    for s in "kv":
        a["cmp_w1_" + s] = f(f"cmp_w1_{s}_2").reshape(16, P, 256).transpose(1, 0, 2)
        a["cmp_w2_" + s] = f(f"cmp_w2_{s}_2").reshape(2, P, HD).transpose(1, 0, 2)
    vec = {
        "norm_mix": i["norm_mix"], "conv_w": i["conv_w"], "mu_rwkv": i["mu_rwkv"], "w0": i["w0"], "a0": i["a0"],
        "k_k": i["k_k"], "k_a": i["k_a"], "r_k": i["r_k"], "lnx_w": i["lnx_w"], "lnx_b": i["lnx_b"],
        "gate_b": i["gate_b"], "norm_ca": i["norm_ca"], "norm_mem": i["norm_mem"], "norm_ffn": i["norm_ffn"],
        "ffn_conv_w": i["ffn_conv_w"], "ffn_conv_b": i["ffn_conv_b"], "norm_final": i["norm_final"],
        "g_attn_2": i["g_attn_2"], "g_mlp_2": i["g_mlp_2"], "g_final_2": i["g_final_2"],
        "pe_k": i["cmp_pe_k_2"], "pe_v": i["cmp_pe_v_2"],
    }
    cols = {name: _columns(np.asarray(v)) for name, v in vec.items()}
    cols["b_forget"] = np.broadcast_to(f("b_forget_2"), (P, 8))
    a["vec"] = np.concatenate([cols[name] for name, _ in VECS], axis=1)
    a["const"] = _constants()
    a["bucket"] = _bucket_rows()
    a["head_row"] = np.repeat(np.eye(HEADS, dtype=np.float32), P, axis=1)
    return {name: np.ascontiguousarray(v) for name, v in a.items()}


def kernel(**inputs):
    import concourse.bacc as bacc
    from concourse.bass_utils import run_bass_kernel_spmd

    arrays = _layout(inputs)
    nc = bacc.Bacc("TRN2", target_bir_lowering=False, num_devices=1)
    dram = {n: nc.dram_tensor(n, a.shape, mybir.dt.from_np(a.dtype), kind="ExternalInput").ap() for n, a in arrays.items()}
    dram["out"] = nc.dram_tensor("out", (P, KD, T), F32, kind="ExternalOutput").ap()
    hybrid_decoder_kernel(nc, dram, STAGES)
    r = run_bass_kernel_spmd(nc, [arrays], core_ids=[0])
    return r.results[0]["out"].transpose(1, 0, 2).reshape(1, D, T).transpose(0, 2, 1)
```

```python
import math
from contextlib import ExitStack

import numpy as np

import concourse.bass as bass
from concourse import mybir

P = 128
T = 512
NT = T // P
D = 1024
KD = D // P
MEM = 256
W = 512
NW = W // P
F = 2816
NF = F // P

HD = 64
HEADS = 8
RING = 4
SLOT = 11 * P
TILES = 71
XN_HI, XN_LO = 55, 63
NC_CMP = (T - 32) // 16 + 1
VEC_DIST = 1024
DECAY = math.exp(-0.5)
RMS_EPS = 1e-6
GN_EPS = 64e-5
NEG = -1e30

ALU = mybir.AluOpType
ACT = mybir.ActivationFunctionType
AX = mybir.AxisListType
F32 = mybir.dt.float32
F32R = mybir.dt.float32r

PHASES = {
    "proj": (38, 8),
    "gates": (32, 9),
    "mix": (8, 8),
    "ca": (32, 8),
    "up": (44, 8),
    "down": (16, 11),
    "in2": (22, 8),
    "gates2": (24, 8),
    "out2": (8, 8),
    "ff1a": (16, 8),
    "ff2a": (16, 8),
    "ff1b": (16, 8),
    "ff2b": (16, 8),
}

VECS = [
    ("norm_mix", 8), ("conv_w", 12), ("mu_rwkv", 14), ("w0", 4), ("a0", 4), ("k_k", 4), ("k_a", 4), ("r_k", 4),
    ("lnx_w", 4), ("lnx_b", 4), ("gate_b", 24), ("norm_ca", 8), ("norm_mem", 8), ("norm_ffn", 8),
    ("ffn_conv_w", 132), ("ffn_conv_b", 44), ("norm_final", 8), ("g_attn_2", 8), ("g_mlp_2", 8), ("g_final_2", 8),
    ("pe_k", 16), ("pe_v", 16), ("b_forget", 8),
]
VEC_AT = {}
_n = 0
for _name, _cols in VECS:
    VEC_AT[_name] = _n
    _n += _cols
N_VEC = _n

CONSTS = [
    ("ident", 128), ("ones", 128), ("head_ones", 128), ("upper", 128), ("causal4", 512), ("neg_tri", 128),
    ("neg_ones", 128), ("neg_diag_t", 128), ("level", 896), ("flip", 128),
    ("causal_add", 128), ("cmp_add", 124), ("cmp_keep", 124),
]
CONST_AT = {}
_n = 0
for _name, _cols in CONSTS:
    CONST_AT[_name] = _n
    _n += _cols
N_CONST = _n


class Core:

    def __init__(self, nc, ctx, dram):
        self.nc, self.dram = nc, dram
        sb = lambda name, shape, dt=F32: ctx.enter_context(nc.sbuf_tensor(name, shape, dt))
        self.vec = sb("vec_sb", [P, N_VEC])
        self.const = sb("const_sb", [P, N_CONST])
        self.small = sb("small", [P, 64])
        self.h = sb("h", [P, KD, T])
        self.raw = sb("weights_raw", [P, 2, SLOT])
        self.w_hi = sb("weights_hi", [P, 2, SLOT], F32R)
        self.w_lo = sb("weights_lo", [P, 2, SLOT], F32R)
        base = nc.sbuf_base
        self.arena = sb("arena", [P, TILES, T])
        self.parts = [nc.alloc_sbuf_tensor_at(f"arena_parts_{i}", [P, min(8, TILES - i), T], F32R, offset=base + i * T * 4)
                      for i in range(0, TILES, 8)]
        self.weights_in = [nc.alloc_semaphore(f"weights_in{s}") for s in range(2)]
        self.hi_ready = nc.alloc_semaphore("weights_hi_ready")
        self.lo_ready = nc.alloc_semaphore("weights_lo_ready")
        self.groups_done = nc.alloc_semaphore("groups_done")
        self.banks_free = nc.alloc_semaphore("banks_free")
        self.stage_sems = []
        self.loaded = 0
        self.used = 0
        self.evacs = 0
        self.order = list(PHASES)
        self.preloaded = {}
        self.cols = [blocks * P for n, blocks in PHASES.values() for _ in range(n)]

    def c(self, name, lo=0, n=None):
        at = CONST_AT[name] + lo
        return self.const[:, at:at + (n if n else dict(CONSTS)[name] - lo)]

    def v(self, name, i):
        return self.vec[:, VEC_AT[name] + i:VEC_AT[name] + i + 1]

    def sem(self, name):
        self.stage_sems.append(self.nc.alloc_semaphore(name))
        return self.stage_sems[-1]

    def pool_dma_sem(self, name):
        return self.nc.alloc_semaphore(name)

    def part(self, tile, lo=0, hi=T):
        return self.parts[tile // 8][:, tile % 8, lo:hi]

    def pair(self, hi, lo, tile):
        return self.part(hi + tile), self.part(lo + tile)

    def load_weights(self, sp, phase, lo, hi):
        src, cols, g0 = self.dram["w_" + phase], PHASES[phase][1] * P, self.loaded

        def load(g, i, at):
            if g >= 2:
                sp.wait_ge(self.lo_ready, g - 1 + i * RING)
            group = src[bass.ds(at + i * RING, 1)] if not isinstance(i, int) else src[at:at + 1]
            sp.dma_start(self.raw[:, g % 2, 0:cols], group.rearrange("a p n -> p (a n)"))\
                .then_inc(self.weights_in[g % 2], 16)

        n = hi - lo
        done = 0
        if g0 == 0:
            done = 2
            for j in range(done):
                load(g0 + j, 0, lo + j)
        turns = (n - done) // RING
        if turns > 1:
            with sp.Fori(0, turns) as i:
                for j in range(RING):
                    load(g0 + done + j, i, lo + done + j)
            done += turns * RING
        for j in range(done, n):
            load(g0 + j, 0, lo + j)
        self.loaded += n

    def stream(self, sp, phase):
        self.load_weights(sp, phase, self.preloaded.pop(phase, 0), PHASES[phase][0])
        at = self.order.index(phase) + 1
        if at < len(self.order):
            self.load_weights(sp, self.order[at], 0, RING)
            self.preloaded[self.order[at]] = RING

    def split_hi(self, act, g):
        if g >= len(self.cols):
            return
        act.wait_ge(self.weights_in[g % 2], 16 * (g // 2 + 1))
        if g >= 2:
            act.wait_ge(self.groups_done, g - 1)
        cols = self.cols[g]
        act.activation(self.w_hi[:, g % 2, 0:cols], self.raw[:, g % 2, 0:cols], ACT.Copy).then_inc(self.hi_ready, 1)

    def split_lo(self, dve, g):
        if g >= len(self.cols):
            return
        dve.wait_ge(self.hi_ready, g + 1)
        cols = self.cols[g]
        dve.tensor_tensor(self.w_lo[:, g % 2, 0:cols], self.raw[:, g % 2, 0:cols], self.w_hi[:, g % 2, 0:cols].bitcast(F32),
                          ALU.subtract).then_inc(self.lo_ready, 1)

    def wait_weights(self, pe, g, i=0, per=RING):
        pe.wait_ge(self.lo_ready, g + 1 + i * per)

    def weights(self, g, lo, hi):
        return self.w_hi[:, g % 2, lo:hi], self.w_lo[:, g % 2, lo:hi]


def product(pe, out, left, right, start, stop):
    pe.matmul(out, left[0], right[0], start=start, stop=False)
    pe.matmul(out, left[0], right[1], start=False, stop=False)
    return pe.matmul(out, left[1], right[0], start=False, stop=stop)


def in_turns(eng, n, per, body):
    turns = n // per
    done = 0
    if turns > 1:
        with eng.Fori(0, turns) as i:
            for j in range(per):
                body(i, j, 0)
        done = turns * per
    for j in range(done, n):
        body(0, j - done, done)


def pe_gemm(core, pe, n, kc, rhs, ps, width=T):
    g0, e0 = core.used, core.evacs

    def step(i, j, done):
        g, e = g0 + done + j, e0 + done + j
        core.wait_weights(pe, g, i)
        pe.wait_ge(core.banks_free, e + 1 + i * RING)
        for k in range(kc):
            mm = product(pe, ps[:, e % 4, 0:width], core.weights(g, k * P, (k + 1) * P), rhs(k), k == 0, k == kc - 1)
        mm.then_inc(core.groups_done, 1)

    in_turns(pe, n, RING, step)
    core.used += n
    core.evacs += n


def pe_by_token(core, pe, groups, width, rhs, tiles, bank):
    per = core.cols[core.used] // width
    for q in range(groups):
        core.wait_weights(pe, core.used)
        for b in range(per):
            k = q * per + b
            x = rhs(k)
            for i in range(tiles):
                for lo in range(0, width, T):
                    n = min(T, width - lo)
                    mm = product(pe, bank(i, lo // T)[:, 0:n], (x[0][:, i * P:(i + 1) * P], x[1][:, i * P:(i + 1) * P]),
                                 core.weights(core.used, b * width + lo, b * width + lo + n), k == 0, k == groups * per - 1)
        mm.then_inc(core.groups_done, 1)
        core.used += 1




def setup_stage(core):
    nc, dram = core.nc, core.dram
    x_in, const_in, vec_in = core.sem("x_in"), core.sem("const_in"), core.sem("vec_in")
    wa_in, g_in = core.sem("wa_lora_in"), core.sem("g_lora_in")
    with nc.Block() as block:

        @block.sync
        def _(sp):
            sp.dma_start(core.h[:], dram["x_t"]).then_inc(x_in, 16)
            sp.dma_start(core.const[:], dram["const"]).then_inc(const_in, 16)
            core.load_weights(sp, "proj", 0, RING)
            core.preloaded["proj"] = RING
            sp.wait_ge(x_in, 16)
            sp.wait_ge(const_in, 16)

        @block.scalar
        def _(act):
            act.dma_start(core.vec[:], dram["vec"]).then_inc(vec_in, 16)
            act.dma_start(core.arena[:, 53, :], dram["wa_lora"]).then_inc(wa_in, 16)
            act.dma_start(core.arena[:, 54, :], dram["g_lora_t"]).then_inc(g_in, 16)
            for g in range(2):
                core.split_hi(act, g)
            act.wait_ge(vec_in, 16)
            act.wait_ge(wa_in, 16)
            act.wait_ge(g_in, 16)

        @block.vector
        def _(dve):
            dve.sem_inc(core.banks_free, 4)
            for g in range(2):
                core.split_lo(dve, g)


def norm_stage(core, name, src, gain, split=None, dst=None, width=T, scratch=40, squares=None):
    nc = core.nc
    squared = core.sem(name + "_squared")
    squared_too = core.sem(name + "_squared_too")
    summed = core.sem(name + "_summed")
    mean_ready = core.sem(name + "_mean_ready")
    rooted = core.sem(name + "_rooted")
    spread = core.sem(name + "_spread")
    steps = core.sem(name + "_steps")
    scaled = core.sem(name + "_scaled")
    upper = core.sem(name + "_upper")
    with ExitStack() as ctx:
        ps = ctx.enter_context(nc.psum_tensor(name + "_ps", [P, 5, T], F32))
        tiles = width // P
        mean, rstd = ps[:, 0:tiles, 0], ps[:, 4, 0:width]
        sq = core.arena[:, scratch:scratch + KD, 0:width]
        inverse = core.small[:, 56:56 + tiles]
        diagonal = core.arena[:, scratch + KD, 0:width]
        with nc.Block() as block:

            @block.scalar
            def _(act):
                if squares is None:
                    for k in range(0, KD, 2):
                        act.activation(sq[:, k, :], src(k), ACT.Square).then_inc(squared, 1)
                act.wait_ge(mean_ready, 1)
                act.activation(inverse, inverse, ACT.Sqrt).then_inc(rooted, 1)
                if split:
                    for k in range(KD):
                        act.wait_ge(scaled, k + 1)
                        act.activation(split(k)[0], sq[:, k, :], ACT.Copy).then_inc(upper, 1)

            @block.tensor
            def _(pe):
                parts = squares or [sq[:, k, :] for k in range(KD)]
                for k, tile in enumerate(parts):
                    if squares is None:
                        pe.wait_ge(squared_too if k % 2 else squared, k // 2 + 1)
                    for i in range(tiles):
                        mm = pe.matmul(ps[:, i, 0:1], tile[:, i * P:(i + 1) * P], core.c("ones", 0, 1), start=(k == 0),
                                       stop=(k == len(parts) - 1))
                mm.then_inc(summed, 1)
                pe.wait_ge(steps, 2)
                pe.matmul(rstd, core.c("ones"), diagonal, start=True, stop=True).then_inc(spread, 1)

            @block.vector
            def _(dve):
                if squares is None:
                    for k in range(1, KD, 2):
                        dve.tensor_tensor(sq[:, k, :], src(k), src(k), ALU.mult).then_inc(squared_too, 1)
                dve.wait_ge(summed, 1)
                dve.tensor_scalar(inverse, mean, 1.0 / D, RMS_EPS, ALU.mult, ALU.add).then_inc(mean_ready, 1)
                dve.wait_ge(rooted, 1)
                dve.reciprocal(inverse, inverse).then_inc(steps, 1)
                dve.wait_ge(steps, 1)
                dve.tensor_tensor(diagonal.rearrange("p (n t) -> p n t", t=P),
                                  core.c("ident").unsqueeze(1).broadcast_to([P, tiles, P]),
                                  inverse.unsqueeze(2).broadcast_to([P, tiles, P]), ALU.mult).then_inc(steps, 1)
                dve.wait_ge(spread, 1)

                def lower(k):
                    dve.wait_ge(upper, k + 1)
                    dve.tensor_tensor(split(k)[1], sq[:, k, :], split(k)[0].bitcast(F32), ALU.subtract)

                for k in range(KD):
                    to = sq[:, k, :] if split else dst(k)
                    dve.scalar_tensor_tensor(to, src(k), core.v(gain, k), rstd, ALU.mult, ALU.mult).then_inc(scaled, 1)
                    if split and k >= 2:
                        lower(k - 2)
                if split:
                    lower(KD - 2)
                    lower(KD - 1)


def proj_stage(core):
    nc = core.nc
    g0, e0 = core.used, core.evacs
    rwkv = core.arena[:, 12:26, :]
    qk = core.arena[:, 26:34, :]
    value = core.arena[:, 34:38, :]
    conv = core.arena[:, 38:50, :]
    diff = core.arena[:, 50:52, :]
    steps = core.sem("proj_steps")
    with ExitStack() as ctx:
        ps = ctx.enter_context(nc.psum_tensor("proj_ps", [P, 4, T], F32))
        ps_v = ctx.enter_context(nc.psum_tensor("proj_ps_v", [P, NT, T], F32))
        with nc.Block() as block:

            @block.sync
            def _(sp):
                core.stream(sp, "proj")

            @block.tensor
            def _(pe):
                x = lambda k: core.pair(XN_HI, XN_LO, k)
                pe_gemm(core, pe, 14, KD, x, ps)
                pe_gemm(core, pe, 12, KD, x, ps)
                pe_gemm(core, pe, 8, KD, x, ps)
                pe_by_token(core, pe, 4, T, x, NT, lambda i, half: ps_v[:, i, :])

            @block.scalar
            def _(act):
                for n in range(38):
                    core.split_hi(act, g0 + n + 2)
                    if n < 34:
                        act.wait_ge(core.groups_done, g0 + n + 1)
                        to = rwkv[:, n, :] if n < 14 else conv[:, n - 14, :] if n < 26 else qk[:, n - 26, :]
                        act.activation(to, ps[:, (e0 + n) % 4, :], ACT.Copy, scale=HD ** -0.5 if 26 <= n < 30 else 1.0)\
                           .then_inc(core.banks_free, 1)
                act.wait_ge(core.groups_done, g0 + 38)
                for i in range(NT):
                    act.activation(value[:, i, :], ps_v[:, i, :], ACT.Copy)

            @block.vector
            def _(dve):
                count = [0]

                def chained(ins):
                    ins.then_inc(steps, 1)
                    count[0] += 1

                def settled():
                    dve.wait_ge(steps, count[0])

                def shift(j):
                    p, d = rwkv[:, j, :], diff[:, j % 2, :]
                    dve.wait_ge(core.banks_free, 4 + e0 + j + 1)
                    chained(dve.tensor_scalar(d[:, 0:1], p[:, 0:1], -1.0, None, ALU.mult))
                    chained(dve.tensor_tensor(d[:, 1:T], p[:, 0:T - 1], p[:, 1:T], ALU.subtract))
                    settled()
                    chained(dve.scalar_tensor_tensor(p, d, core.v("mu_rwkv", j), p, ALU.mult, ALU.add))

                def convolve(j):
                    u, y, b = conv[:, 3 * j, :], conv[:, 3 * j + 1, :], conv[:, 3 * j + 2, :]
                    dve.wait_ge(core.banks_free, 4 + e0 + 14 + 3 * j + 3)
                    chained(dve.tensor_tensor(u, u, y, ALU.mult))
                    settled()
                    chained(dve.tensor_scalar(y, u, core.v("conv_w", 8 + j), None, ALU.mult))
                    settled()
                    chained(dve.scalar_tensor_tensor(y[:, 1:T], u[:, 0:T - 1], core.v("conv_w", 4 + j), y[:, 1:T],
                                                     ALU.mult, ALU.add))
                    settled()
                    chained(dve.scalar_tensor_tensor(y[:, 2:T], u[:, 0:T - 2], core.v("conv_w", j), y[:, 2:T],
                                                     ALU.mult, ALU.add))
                    settled()
                    chained(dve.tensor_tensor(core.arena[:, j, :], y, b, ALU.mult))

                for n in range(38):
                    core.split_lo(dve, g0 + n + 2)
                    if 1 <= n < 15:
                        shift(n - 1)
                    if n >= 17 and (n - 17) % 3 == 0 and (n - 17) // 3 < NW:
                        convolve((n - 17) // 3)


def stick_breaking_stage(core):
    nc = core.nc
    query, key = core.arena[:, 26:30, :], core.arena[:, 30:34, :]
    value = core.arena[:, 34:38, :]
    flat = core.arena[:, 38:53, :].rearrange("p a t -> p (a t)")
    log_buf = [flat[:, b * 1280:(b + 1) * 1280] for b in range(2)]
    soft = [flat[:, 2560 + b * 1280:2560 + (b + 1) * 1280] for b in range(2)]
    att = [flat[:, 5120 + b * 1280:5120 + (b + 1) * 1280] for b in range(2)]
    start = [0, 512, 896, 1152]
    scores_ready = core.sem("sb_scores_ready")
    abs_ready = core.sem("sb_abs_ready")
    exp_ready = core.sem("sb_exp_ready")
    log_ready = core.sem("sb_log_ready")
    soft_part = core.sem("sb_soft_part")
    soft_ready = core.sem("sb_soft_ready")
    weight_ready = core.sem("sb_weight_ready")
    att_ready = core.sem("sb_att_ready")
    out_done = core.sem("sb_out_done")
    out_taken = core.sem("sb_out_taken")
    with ExitStack() as ctx:
        ps = ctx.enter_context(nc.psum_tensor("sb_ps", [P, 6, T], F32))
        ps_out = ctx.enter_context(nc.psum_tensor("sb_ps_out", [P, 2, T], F32))

        def tile(h, j):
            bank, lo = (j, 0) if j < 3 else (2, 256)
            return ps[:, 3 * (h % 2) + bank, lo:lo + T - j * P]

        def parts(h, buf):
            return [(ps[:, 3 * (h % 2) + m, 0:n], buf[h % 2][:, lo:lo + n]) for m, lo, n in ((0, 0, 512), (1, 512, 384), (2, 896, 384))]

        with nc.Block() as block:

            @block.tensor
            def _(pe):
                def scores(h):
                    c, off = h // 2, HD * (h % 2)
                    if h >= 2:
                        pe.wait_ge(att_ready, h - 1)
                    for j in range(NT):
                        mm = pe.matmul(tile(h, j), key[off:off + HD, c, j * P:(j + 1) * P], query[off:off + HD, c, j * P:T],
                                       start=(j < 3), stop=False, skip_group_check=True)
                    mm.then_inc(scores_ready, 1)

                def weights(h):
                    pe.wait_ge(soft_ready, h + 1)
                    for j in range(NT):
                        pe.matmul(tile(h, j)[:, 0:P], core.c("ident"), core.c("neg_diag_t"), start=False, stop=False,
                                  skip_group_check=True)
                        for m in range(j, NT):
                            mm = pe.matmul(tile(h, j)[:, (m - j) * P:T - j * P], core.c("neg_tri" if m == j else "neg_ones"),
                                           soft[h % 2][:, start[m]:start[m] + T - m * P], start=False, stop=(m == NT - 1),
                                           skip_group_check=True)
                    mm.then_inc(weight_ready, 1)

                def output(h):
                    c, off = h // 2, HD * (h % 2)
                    pe.wait_ge(att_ready, h + 1)
                    if c >= 2:
                        pe.wait_ge(out_taken, c - 1)
                    for j in range(NT):
                        mm = pe.matmul(ps_out[off:off + HD, c % 2, j * P:T], value[:, j, h * HD:(h + 1) * HD],
                                       att[h % 2][:, start[j]:start[j] + T - j * P], start=(j == 0), stop=(j == NT - 1),
                                       skip_group_check=True)
                    mm.then_inc(out_done, 1)

                scores(0)
                for h in range(HEADS):
                    if h + 1 < HEADS:
                        scores(h + 1)
                    weights(h)
                    if h >= 1:
                        output(h - 1)
                output(HEADS - 1)

            @block.scalar
            def _(act):
                def logs(h):
                    act.wait_ge(scores_ready, h + 1)
                    if h >= 2:
                        act.wait_ge(soft_part, h - 1)
                    for banks, cols in parts(h, log_buf):
                        ins = act.activation(cols, banks, ACT.Abs)
                    ins.then_inc(abs_ready, 1)
                    act.wait_ge(abs_ready, h + 1)
                    act.activation(log_buf[h % 2], log_buf[h % 2], ACT.Exp, scale=-1.0).then_inc(exp_ready, 1)
                    act.wait_ge(exp_ready, h + 1)
                    act.activation(log_buf[h % 2], log_buf[h % 2], ACT.Ln, bias=1.0).then_inc(log_ready, 1)

                def weights(h):
                    act.wait_ge(weight_ready, h + 1)
                    if h >= 2:
                        act.wait_ge(out_done, h - 1)
                    for i, (banks, cols) in enumerate(parts(h, att)):
                        ins = act.activation(cols, banks, ACT.Exp)
                    ins.then_inc(att_ready, 1)

                logs(0)
                for h in range(HEADS):
                    if h + 1 < HEADS:
                        logs(h + 1)
                    weights(h)

            @block.vector
            def _(dve):
                def softplus(h):
                    dve.wait_ge(log_ready, h + 1)
                    if h >= 2:
                        dve.wait_ge(weight_ready, h - 1)
                    for (banks, cols), (_, logs) in zip(parts(h, soft), parts(h, log_buf)):
                        ins = dve.scalar_tensor_tensor(cols, banks, 0.0, logs, ALU.max, ALU.add)
                    ins.then_inc(soft_part, 1)
                    dve.wait_ge(soft_part, h + 1)
                    for j in range(NT):
                        diag = soft[h % 2][:, start[j]:start[j] + P]
                        ins = dve.tensor_tensor(diag, diag, core.c("causal4", 0, P), ALU.mult)
                    ins.then_inc(soft_ready, 1)

                def take(c):
                    dve.wait_ge(out_done, 2 * c + 2)
                    dve.tensor_copy(core.arena[:, 4 + c, :], ps_out[:, c % 2, :]).then_inc(out_taken, 1)

                for h in range(HEADS):
                    softplus(h)
                    if h >= 2 and h % 2 == 0:
                        take(h // 2 - 1)
                take(NW - 1)


def clear_semaphores_stage(core):
    with core.nc.Block() as block:

        @block.sync
        def _(sp):
            for sem in core.stage_sems:
                sp.sem_clear(sem)

    for sem in core.stage_sems:
        core.nc.release_semaphore(sem)
    core.stage_sems = []


def time_mix_stage(core):
    nc, a = core.nc, core.arena
    r, k, v = a[:, 12:16, :], a[:, 16:20, :], a[:, 20:24, :]
    wa, xg, lora, g_lora = a[:, 24, :], a[:, 25, :], a[:, 53, :], a[:, 54, :]
    kk, bonus, key = a[:, 26:30, :], a[:, 30:34, :], a[:, 34:38, :]
    decay, rate, gate, sums = a[:, 38:42, :], a[:, 42:46, :], a[:, 46:50, :], a[:, 50:54, :]
    restart = a[:, 58, :]
    norm, rk = a[:, 61:65, :], a[:, 65:69, :]
    mid = core.small[:, 0:16]
    inner = core.sem("tm_inner")
    lora_out = core.sem("tm_lora_out")
    lora_taken = core.sem("tm_lora_taken")
    square = core.sem("tm_square")
    bonus_in = core.sem("tm_bonus_in")
    norm_sum = core.sem("tm_norm_sum")
    bonus_sum = core.sem("tm_bonus_sum")
    norm_taken = core.sem("tm_norm_taken")
    rooted = core.sem("tm_rooted")
    steps = core.sem("tm_steps")
    ready = core.sem("tm_restart")
    with ExitStack() as ctx:
        ps = ctx.enter_context(nc.psum_tensor("tm_ps", [P, 8, T], F32))
        with nc.Block() as block:

            @block.gpsimd
            def _(pool):
                pool.memset(restart, 1.0).then_inc(ready, 1)
                pool.wait_ge(ready, 1)
                pool.memset(restart[:, 0:T:P], 0.0).then_inc(ready, 1)

            @block.scalar
            def _(act):
                act.activation(wa[0:HD, :], wa[0:HD, :], ACT.Tanh).then_inc(inner, 1)
                act.activation(xg, xg, ACT.Sigmoid).then_inc(inner, 1)
                for c in range(NW):
                    act.wait_ge(lora_out, c + 1)
                    act.activation(decay[:, c, :], ps[:, 4 * (c % 2), :], ACT.Sigmoid, bias=core.v("w0", c))
                    act.activation(rate[:, c, :], ps[:, 4 * (c % 2) + 1, :], ACT.Sigmoid, bias=core.v("a0", c))
                    act.activation(gate[:, c, :], ps[:, 4 * (c % 2) + 2, :], ACT.Copy).then_inc(lora_taken, 1)
                for c in range(NW):
                    act.wait_ge(norm_taken, c + 1)
                    act.activation(norm[:, c, :], norm[:, c, :], ACT.Sqrt).then_inc(rooted, 1)

            @block.tensor
            def _(pe):
                pe.wait_ge(inner, 2)
                for c in range(NW):
                    if c >= 2:
                        pe.wait_ge(lora_taken, c - 1)
                    cols = slice(c * P, (c + 1) * P)
                    pe.matmul(ps[:, 4 * (c % 2), :], lora[0:HD, cols], wa[0:HD, :], start=True, stop=True)
                    pe.matmul(ps[:, 4 * (c % 2) + 1, :], lora[HD:P, cols], wa[HD:P, :], start=True, stop=True)
                    pe.matmul(ps[:, 4 * (c % 2) + 2, :], g_lora[:, cols], xg, start=True, stop=True).then_inc(lora_out, 1)
                for c in range(NW):
                    pe.wait_ge(square, c + 1)
                    if c >= 2:
                        pe.wait_ge(norm_taken, c - 1)
                    pe.matmul(ps[:, 4 * (c % 2) + 3, :], core.c("head_ones"), bonus[:, c, :], start=True, stop=True)\
                      .then_inc(norm_sum, 1)
                pe.wait_ge(lora_taken, NW)
                for c in range(NW):
                    pe.wait_ge(bonus_in, c + 1)
                    pe.matmul(ps[:, (0, 1, 4, 5)[c], :], core.c("head_ones"), rk[:, c, :], start=True, stop=True)\
                      .then_inc(bonus_sum, 1)

            @block.vector
            def _(dve):
                n = 0
                for c in range(NW):
                    dve.tensor_scalar(kk[:, c, :], k[:, c, :], core.v("k_k", c), None, ALU.mult).then_inc(steps, 1)
                    n += 1
                    dve.wait_ge(steps, n)
                    dve.tensor_tensor(bonus[:, c, :], kk[:, c, :], kk[:, c, :], ALU.mult).then_inc(square, 1)
                for c in range(NW):
                    dve.tensor_scalar(rk[:, c, :], r[:, c, :], core.v("r_k", c), None, ALU.mult).then_inc(steps, 1)
                    n += 1
                for c in range(NW):
                    dve.wait_ge(norm_sum, c + 1)
                    dve.tensor_scalar(norm[:, c, :], ps[:, 4 * (c % 2) + 3, :], 1e-24, None, ALU.max).then_inc(norm_taken, 1)
                for c in range(NW):
                    dve.wait_ge(lora_taken, c + 1)
                    dve.tensor_scalar(key[:, c, :], rate[:, c, :], -1.0, core.v("k_a", c), ALU.add, ALU.mult).then_inc(steps, 1)
                    n += 1
                    dve.wait_ge(steps, n)
                    dve.scalar_tensor_tensor(key[:, c, :], key[:, c, :], 1.0, k[:, c, :], ALU.add, ALU.mult).then_inc(steps, 1)
                    n += 1
                    dve.wait_ge(steps, n)
                    dve.tensor_tensor(rk[:, c, :], rk[:, c, :], key[:, c, :], ALU.mult).then_inc(bonus_in, 1)
                dve.wait_ge(ready, 2)
                for c in range(NW):
                    dve.tensor_tensor_scan(sums[:, c, :], restart, decay[:, c, :], 0.0, ALU.mult, ALU.add).then_inc(steps, 1)
                n += NW
                dve.wait_ge(steps, n)
                for c in range(NW):
                    dve.tensor_copy(mid[:, 4 * c:4 * c + 4], sums[:, c, P // 2 - 1:T:P]).then_inc(steps, 1)
                n += NW
                dve.wait_ge(steps, n)
                for c in range(NW):
                    s3 = sums[:, c, :].rearrange("p (n t) -> p n t", t=P)
                    dve.tensor_tensor(s3, s3, mid[:, 4 * c:4 * c + 4].unsqueeze(2).broadcast_to([P, NT, P]), ALU.subtract)\
                       .then_inc(steps, 1)
                n += NW
                dve.wait_ge(steps, n)
                for c in range(NW):
                    dve.tensor_tensor(decay[:, c, :], sums[:, c, :], decay[:, c, :], ALU.subtract).then_inc(steps, 1)
                n += NW
                for c in range(NW):
                    dve.wait_ge(rooted, c + 1)
                    dve.reciprocal(norm[:, c, :], norm[:, c, :]).then_inc(steps, 1)
                    n += 1
                    dve.wait_ge(steps, n)
                    dve.tensor_tensor(kk[:, c, :], kk[:, c, :], norm[:, c, :], ALU.mult)
                for c in range(NW):
                    dve.wait_ge(bonus_sum, c + 1)
                    dve.tensor_tensor(bonus[:, c, :], ps[:, (0, 1, 4, 5)[c], :], v[:, c, :], ALU.mult)


def time_mix_scale_stage(core):
    nc, a = core.nc, core.arena
    r, k_out, v, v_tok = a[:, 12:16, :], a[:, 16:20, :], a[:, 20:24, :], a[:, 12:16, :]
    kk, key, kk_tok, key_tok = a[:, 26:30, :], a[:, 34:38, :], a[:, 34:38, :], a[:, 26:30, :]
    before, rate, sums, upto = a[:, 38:42, :], a[:, 42:46, :], a[:, 50:54, :], a[:, 54:58, :]
    pair = a[:, 61:69, :].rearrange("p (c n) (m q t) -> p c (n m) q t", n=2, q=2, t=P)
    upto_ready = core.sem("ts_upto_ready")
    before_ready = core.sem("ts_before_ready")
    away_ready = core.sem("ts_away_ready")
    steps = core.sem("ts_steps")
    r_used = core.sem("ts_r_used")
    k_made = core.sem("ts_k_made")
    b_made = core.sem("ts_b_made")
    turned = core.sem("ts_turned")
    placed = core.sem("ts_placed")
    chunks = lambda x: x.rearrange("p (n t) -> p n t", t=P)
    with ExitStack() as ctx:
        ps = ctx.enter_context(nc.psum_tensor("ts_ps", [P, 8, T], F32))
        with nc.Block() as block:

            @block.scalar
            def _(act):
                for c in range(NW):
                    act.activation(upto[:, c, :], sums[:, c, :], ACT.Exp, scale=-DECAY).then_inc(upto_ready, 1)
                    act.activation(before[:, c, :], before[:, c, :], ACT.Exp, scale=-DECAY).then_inc(before_ready, 1)
                    act.wait_ge(upto_ready, c + 1)
                    act.activation(sums[:, c, :], sums[:, c, :], ACT.Exp, scale=DECAY).then_inc(away_ready, 1)
                act.activation(core.small[:, 16:32], core.small[:, 0:16], ACT.Exp, scale=-DECAY)
                for n in range(12):
                    act.wait_ge(turned, n + 1)
                    if n < 4:
                        act.wait_ge(r_used, NW)
                    else:
                        act.wait_ge(b_made, NW)
                    out = (v_tok, key_tok, kk_tok)[n // 4]
                    act.activation(out[:, n % 4, :], ps[:, n % 8, :], ACT.Copy).then_inc(placed, 1)

            @block.vector
            def _(dve):
                for c in range(NW):
                    dve.wait_ge(upto_ready, c + 1)
                    dve.tensor_tensor(pair[:, c, :, 1, :], chunks(r[:, c, :]), chunks(upto[:, c, :]), ALU.mult).then_inc(r_used, 1)
                for c in range(NW):
                    dve.wait_ge(before_ready, c + 1)
                    dve.tensor_tensor(pair[:, c, :, 0, :], chunks(kk[:, c, :]), chunks(before[:, c, :]), ALU.mult)
                    dve.wait_ge(away_ready, c + 1)
                    dve.tensor_tensor(k_out[:, c, :], key[:, c, :], sums[:, c, :], ALU.mult).then_inc(k_made, 1)
                    dve.tensor_tensor(rate[:, c, :], rate[:, c, :], kk[:, c, :], ALU.mult).then_inc(steps, 1)
                    dve.wait_ge(steps, c + 1)
                    dve.tensor_tensor(rate[:, c, :], rate[:, c, :], sums[:, c, :], ALU.mult).then_inc(b_made, 1)
                for c in range(NW):
                    dve.tensor_copy(core.small[:, 32 + 4 * c:36 + 4 * c], upto[:, c, P - 1:T:P])

            @block.tensor
            def _(pe):
                for n in range(12):
                    src = (v, k_out, rate)[n // 4]
                    if n == 4:
                        pe.wait_ge(k_made, NW)
                    if n == 8:
                        pe.wait_ge(b_made, NW)
                    if n >= 8:
                        pe.wait_ge(placed, n - 7)
                    for c in range(NW):
                        mm = pe.transpose(ps[:, n % 8, c * P:(c + 1) * P], src[:, c, (n % 4) * P:(n % 4 + 1) * P], core.c("ident"))
                    mm.then_inc(turned, 1)


def time_mix_chunks_stage(core):
    nc, a = core.nc, core.arena
    v_tok, key_tok, b_tok = a[:, 12:16, :], a[:, 26:30, :], a[:, 34:38, :]
    k_out, b_out = a[:, 16:20, :], a[:, 42:46, :]
    pair = a[:, 61:69, :].rearrange("p (c n) (m q t) -> p c (n m) q t", n=2, q=2, t=P)
    gram = a[:, 50:58, :]
    inv, inv_t = a[:, 38:40, :], a[:, 40:42, :]
    level = [a[:, 20:22, :], a[:, 22:24, :]]
    prod = a[:, 24:26, :]
    state = a[:, 58, 0:256]
    x_sb, sa = a[:, 59, :], a[:, 60, :]
    out = a[:, 8:12, :]
    from_start, to_end = core.small[:, 16:32], core.small[:, 32:48]
    LEVELS = 7
    gram_done = core.sem("tc_gram_done")
    gram_ready = core.sem("tc_gram_ready")
    level_ready = core.sem("tc_level_ready")
    prod_done = core.sem("tc_prod_done")
    prod_ready = core.sem("tc_prod_ready")
    step_done = core.sem("tc_step_done")
    step_ready = core.sem("tc_step_ready")
    x_done, x_ready = core.sem("tc_x_done"), core.sem("tc_x_ready")
    sa_done, sa_ready = core.sem("tc_sa_done"), core.sem("tc_sa_ready")
    end_done, out_ready = core.sem("tc_end_done"), core.sem("tc_out_ready")
    state_sum, state_ready = core.sem("tc_state_sum"), core.sem("tc_state_ready")
    heads = lambda x: x.rearrange("p a (m t) -> p (a m) t", t=P)
    with ExitStack() as ctx:
        ps = ctx.enter_context(nc.psum_tensor("tc_ps", [P, 8, T], F32))
        with nc.Block() as block:

            @block.tensor
            def _(pe):
                def grams(ch):
                    for h in range(HEADS):
                        c, rows, u = h // 2, slice(HD * (h % 2), HD * (h % 2) + HD), ch * HEADS + h
                        if u >= 2:
                            pe.wait_ge(gram_ready, u - 1)
                        qr = pair[rows, c, ch, :, :].rearrange("p q t -> p (q t)")
                        cols = slice(ch * P, (ch + 1) * P)
                        pe.matmul(ps[:, h % 2, 0:256], b_out[rows, c, cols], qr, start=True, stop=True)
                        pe.matmul(ps[:, h % 2, 256:512], k_out[rows, c, cols], qr, start=True, stop=True)\
                          .then_inc(gram_done, 1)

                def inverse(ch):
                    for n in range(LEVELS):
                        pe.wait_ge(level_ready, ch * LEVELS + n + 1)
                        if n == 0:
                            if ch:
                                pe.wait_ge(out_ready, ch)
                                pe.wait_ge(state_ready, ch)
                            for half in range(2):
                                for m in range(4):
                                    mm = pe.matmul(ps[:, 4 + half, m * P:(m + 1) * P],
                                                   heads(level[ch * LEVELS % 2])[:, 4 * half + m, :], core.c("ident"),
                                                   start=True, stop=True)
                                mm.then_inc(step_done, 1)
                            continue
                        for half in range(2):
                            u = (ch * LEVELS + n) * 2 + half
                            if u >= 2:
                                pe.wait_ge(step_ready, u - 1)
                            for m in range(4):
                                h = 4 * half + m
                                mm = pe.matmul(ps[:, 2 + half, m * P:(m + 1) * P], heads(level[(ch * LEVELS + n) % 2])[:, h, :],
                                               heads(inv)[:, h, :], start=True, stop=True)
                            mm.then_inc(prod_done, 1)
                        for half in range(2):
                            pe.wait_ge(prod_ready, (ch * (LEVELS - 1) + n - 1) * 2 + half + 1)
                            for m in range(4):
                                h = 4 * half + m
                                if n < LEVELS - 1:
                                    pe.matmul(ps[:, 4 + half, m * P:(m + 1) * P], heads(inv_t)[:, h, :], heads(prod)[:, h, :],
                                              start=True, stop=True)
                                mm = pe.matmul(ps[:, 6 + half, m * P:(m + 1) * P], heads(prod)[:, h, :], heads(inv_t)[:, h, :],
                                               start=True, stop=True)
                            mm.then_inc(step_done, 1)

                def recur(ch):
                    if ch:
                        pe.wait_ge(state_ready, ch)
                    pe.wait_ge(step_ready, (ch + 1) * LEVELS * 2)
                    pe.wait_ge(gram_ready, (ch + 1) * HEADS)
                    for h in range(HEADS):
                        c, rows, cols = h // 2, slice(HD * (h % 2), HD * (h % 2) + HD), slice(h * HD, (h + 1) * HD)
                        x_ps = ps[:, 4 * (h % 2), c * HD:(c + 1) * HD]
                        if ch:
                            pe.matmul(x_ps, pair[rows, c, ch, 0, :], state[rows, c * HD:(c + 1) * HD],
                                      start=True, stop=False)
                        mm = pe.matmul(x_ps, gram[:, h, 256:384], v_tok[:, ch, cols], start=(ch == 0), stop=True)
                    mm.then_inc(x_done, 1)
                    pe.wait_ge(x_ready, ch + 1)
                    for h in range(HEADS):
                        cols = slice(h * HD, (h + 1) * HD)
                        mm = pe.matmul(ps[:, 1, cols], heads(inv_t)[:, h, :], x_sb[:, cols], start=True, stop=True)
                    mm.then_inc(sa_done, 1)
                    pe.wait_ge(sa_ready, ch + 1)
                    for h in range(HEADS):
                        c, rows, cols = h // 2, slice(HD * (h % 2), HD * (h % 2) + HD), slice(h * HD, (h + 1) * HD)
                        o, s = ps[rows, 2, c * P:(c + 1) * P], ps[rows, 3, c * HD:(c + 1) * HD]
                        if ch < NT - 1:
                            pe.matmul(s, key_tok[:, ch, cols], v_tok[:, ch, cols], start=True, stop=False)
                            pe.matmul(s, b_tok[:, ch, cols], sa[:, cols], start=False, stop=True)
                        if ch:
                            pe.matmul(o, state[rows, c * HD:(c + 1) * HD], pair[rows, c, ch, 1, :], start=True, stop=False)
                        pe.matmul(o, v_tok[:, ch, cols], gram[:, h, 384:512], start=(ch == 0), stop=False)
                        mm = pe.matmul(o, sa[:, cols], gram[:, h, 128:256], start=False, stop=True)
                    mm.then_inc(end_done, 1)

                for ch in range(NT):
                    grams(ch)
                    inverse(ch)
                    recur(ch)

            @block.gpsimd
            def _(pool):
                for ch in range(NT):
                    pool.wait_ge(gram_ready, (ch + 1) * HEADS)
                    for n in range(LEVELS):
                        g = ch * LEVELS + n
                        if g >= 2:
                            pool.wait_ge(step_ready, 2 * (g - 1))
                        pool.tensor_tensor(heads(level[g % 2]), gram[:, :, 0:P],
                                           core.c("level", n * P, P).unsqueeze(1).broadcast_to([P, HEADS, P]), ALU.mult)\
                            .then_inc(level_ready, 1)

            @block.scalar
            def _(act):
                for ch in range(NT):
                    for n in range(LEVELS - 1):
                        for half in range(2):
                            act.wait_ge(prod_done, (ch * (LEVELS - 1) + n) * 2 + half + 1)
                            act.activation(prod[:, half, :], ps[:, 2 + half, :], ACT.Copy).then_inc(prod_ready, 1)
                    act.wait_ge(x_done, ch + 1)
                    for odd in range(2):
                        ins = act.activation(x_sb.rearrange("p (c n v) -> p c n v", n=2, v=HD)[:, :, odd, :],
                                             ps[:, 4 * odd, 0:256].rearrange("p (c v) -> p c v", v=HD), ACT.Copy)
                    ins.then_inc(x_ready, 1)
                    act.wait_ge(end_done, ch + 1)
                    act.activation(out[:, :, ch * P:(ch + 1) * P], ps[:, 2, :].rearrange("p (c t) -> p c t", t=P), ACT.Copy)\
                       .then_inc(out_ready, 1)

            @block.vector
            def _(dve):
                for ch in range(NT):
                    if ch:
                        dve.wait_ge(end_done, ch)
                        dve.wait_ge(level_ready, ch * LEVELS)
                    for h in range(HEADS):
                        dve.wait_ge(gram_done, ch * HEADS + h + 1)
                        dve.tensor_tensor(gram[:, h, :], ps[:, h % 2, :], core.c("causal4"), ALU.mult).then_inc(gram_ready, 1)
                    dve.wait_ge(level_ready, ch * LEVELS + 1)
                    ident = core.c("ident").unsqueeze(1).broadcast_to([P, 4, P])
                    for half in range(2):
                        own = slice(4 * half, 4 * half + 4)
                        dve.wait_ge(step_done, ch * LEVELS * 2 + half + 1)
                        dve.tensor_tensor(heads(inv)[:, own, :], ident, ps[:, 4 + half, :].rearrange("p (m t) -> p m t", t=P),
                                          ALU.subtract)
                        dve.tensor_tensor(heads(inv_t)[:, own, :], ident, heads(level[ch * LEVELS % 2])[:, own, :], ALU.subtract)\
                           .then_inc(step_ready, 1)
                    for n in range(1, LEVELS):
                        for half in range(2):
                            u = (ch * LEVELS + n) * 2 + half
                            dve.wait_ge(step_done, u + 1)
                            dve.wait_ge(step_ready, u - 1)
                            if n < LEVELS - 1:
                                dve.tensor_tensor(inv[:, half, :], inv[:, half, :], ps[:, 4 + half, :], ALU.subtract)
                            dve.tensor_tensor(inv_t[:, half, :], inv_t[:, half, :], ps[:, 6 + half, :], ALU.subtract)\
                               .then_inc(step_ready, 1)
                    dve.wait_ge(sa_done, ch + 1)
                    dve.tensor_scalar(sa, ps[:, 1, :], -1.0, None, ALU.mult).then_inc(sa_ready, 1)
                    if ch < NT - 1:
                        dve.wait_ge(end_done, ch + 1)
                        if ch:
                            dve.tensor_tensor(state, state, ps[:, 3, 0:256], ALU.add).then_inc(state_sum, 1)
                        else:
                            dve.tensor_copy(state, ps[:, 3, 0:256]).then_inc(state_sum, 1)
                        dve.wait_ge(state_sum, ch + 1)
                        for c in range(NW):
                            part = state[:, c * HD:(c + 1) * HD]
                            ins = dve.tensor_scalar(part, part, to_end[:, 4 * c + ch:4 * c + ch + 1],
                                                    from_start[:, 4 * c + ch + 1:4 * c + ch + 2], ALU.mult, ALU.mult)
                        ins.then_inc(state_ready, 1)


def time_mix_out_stage(core):
    nc, a = core.nc, core.arena
    out, bonus, gate = a[:, 8:12, :], a[:, 30:34, :], a[:, 46:50, :]
    square, rstd = a[:, 50:54, :], a[:, 54:58, :]
    mean_done, centred = core.sem("to_mean_done"), core.sem("to_centred")
    squared, var_done = core.sem("to_squared"), core.sem("to_var_done")
    steps, var_ready, rooted = core.sem("to_steps"), core.sem("to_var_ready"), core.sem("to_rooted")
    with ExitStack() as ctx:
        ps = ctx.enter_context(nc.psum_tensor("to_ps", [P, 8, T], F32))
        with nc.Block() as block:

            @block.tensor
            def _(pe):
                for c in range(NW):
                    pe.matmul(ps[:, c, :], core.c("head_ones"), out[:, c, :], start=True, stop=True).then_inc(mean_done, 1)
                for c in range(NW):
                    pe.wait_ge(squared, c + 1)
                    pe.matmul(ps[:, 4 + c, :], core.c("head_ones"), square[:, c, :], start=True, stop=True).then_inc(var_done, 1)

            @block.scalar
            def _(act):
                for c in range(NW):
                    act.wait_ge(centred, c + 1)
                    act.activation(square[:, c, :], out[:, c, :], ACT.Square).then_inc(squared, 1)
                for c in range(NW):
                    act.wait_ge(var_ready, c + 1)
                    act.activation(rstd[:, c, :], rstd[:, c, :], ACT.Sqrt).then_inc(rooted, 1)

            @block.vector
            def _(dve):
                for c in range(NW):
                    dve.wait_ge(mean_done, c + 1)
                    dve.scalar_tensor_tensor(out[:, c, :], ps[:, c, :], -1.0 / HD, out[:, c, :], ALU.mult, ALU.add)\
                       .then_inc(centred, 1)
                for c in range(NW):
                    dve.wait_ge(var_done, c + 1)
                    dve.tensor_scalar(rstd[:, c, :], ps[:, 4 + c, :], 1.0 / HD, GN_EPS, ALU.mult, ALU.add).then_inc(var_ready, 1)
                n = 0
                for c in range(NW):
                    dve.tensor_scalar(bonus[:, c, :], bonus[:, c, :], core.v("lnx_b", c), None, ALU.add).then_inc(steps, 1)
                n += NW
                dve.wait_ge(steps, n)
                for c in range(NW):
                    dve.wait_ge(rooted, c + 1)
                    dve.reciprocal(rstd[:, c, :], rstd[:, c, :]).then_inc(steps, 1)
                    n += 1
                    dve.wait_ge(steps, n)
                    dve.scalar_tensor_tensor(out[:, c, :], out[:, c, :], core.v("lnx_w", c), rstd[:, c, :], ALU.mult, ALU.mult)\
                       .then_inc(steps, 1)
                    n += 1
                    dve.wait_ge(steps, n)
                    dve.tensor_tensor(out[:, c, :], out[:, c, :], bonus[:, c, :], ALU.add).then_inc(steps, 1)
                    n += 1
                    dve.wait_ge(steps, n)
                    dve.tensor_tensor(out[:, c, :], out[:, c, :], gate[:, c, :], ALU.mult)


def pe_gemm_deep(core, pe, n, per_tile, blocks, rhs, ps):
    g0, e0 = core.used, core.evacs
    assert 2 * per_tile % RING == 0 and n % 2 == 0

    def step(i, j, done):
        e = e0 + done + j
        pe.wait_ge(core.banks_free, e + 3 + i * 2)
        for q in range(per_tile):
            g = g0 + (done + j) * per_tile + q
            core.wait_weights(pe, g, i, 2 * per_tile)
            for b in range(blocks):
                k = q * blocks + b
                mm = product(pe, ps[:, e % 2, :], core.weights(g, b * P, (b + 1) * P), rhs(k), k == 0,
                             k == per_tile * blocks - 1)
            mm.then_inc(core.groups_done, 1)

    in_turns(pe, n, 2, step)
    core.used += n * per_tile
    core.evacs += n


def split_stage(core, name, n, src, hi, lo):
    upper = core.sem(name + "_upper")
    with core.nc.Block() as block:

        @block.scalar
        def _(act):
            for k in range(n):
                act.activation(core.part(hi + k), core.arena[:, src + k, :], ACT.Copy).then_inc(upper, 1)

        @block.vector
        def _(dve):
            for k in range(n):
                dve.wait_ge(upper, k + 1)
                dve.tensor_tensor(core.part(lo + k), core.arena[:, src + k, :],
                                  core.part(hi + k).bitcast(F32), ALU.subtract)


def gates_stage(core):
    nc, a = core.nc, core.arena
    open_gate = a[:, 0:3, :]
    part = a[:, 3:5, :]
    total = a[:, 5:7, :]
    g0 = core.used
    pairs_free = core.sem("gt_pairs_free")
    opened = core.sem("gt_opened")
    summed = core.sem("gt_summed")
    upper = core.sem("gt_upper")
    with ExitStack() as ctx:
        ps = ctx.enter_context(nc.psum_tensor("gt_ps", [P, 6, T], F32))
        with nc.Block() as block:

            @block.sync
            def _(sp):
                core.stream(sp, "gates")

            @block.tensor
            def _(pe):
                with pe.Fori(0, KD) as d:
                    for m in range(36):
                        n, k = m // 12, m % 12
                        if k == 0:
                            pe.wait_ge(pairs_free, d * 3 + n + 1)
                        g = g0 + m // 9
                        if m % 9 == 0:
                            core.wait_weights(pe, g, d)
                        w = core.weights(g, (m % 9) * P, (m % 9 + 1) * P)
                        if k < KD:
                            mm = product(pe, ps[:, 2 * n, :], w, core.pair(36, 44, k), k == 0, k == KD - 1)
                        else:
                            mm = product(pe, ps[:, 2 * n + 1, :], w, core.pair(12, 24, 4 * n + k - KD), k == KD, k == 11)
                        if m % 9 == 8:
                            mm.then_inc(core.groups_done, 1)
                core.used += 32

            @block.scalar
            def _(act):
                for d in range(KD):
                    for m in range(4):
                        core.split_hi(act, g0 + 4 * d + m + 2)
                        if m:
                            n = m - 1
                            act.wait_ge(core.groups_done, g0 + 4 * d + m + 1)
                            if d:
                                act.wait_ge(pairs_free, 3 + 3 * (d - 1) + n + 1)
                            act.activation(open_gate[:, n, :], ps[:, 2 * n, :], ACT.Sigmoid, bias=core.v("gate_b", 8 * n + d))\
                               .then_inc(opened, 1)
                        elif d:
                            act.wait_ge(summed, 2 * d)
                            act.activation(core.pair(XN_HI, XN_LO, d - 1)[0], total[:, (d - 1) % 2, :], ACT.Copy).then_inc(upper, 1)
                act.wait_ge(summed, 2 * KD)
                act.activation(core.pair(XN_HI, XN_LO, KD - 1)[0], total[:, (KD - 1) % 2, :], ACT.Copy).then_inc(upper, 1)

            @block.vector
            def _(dve):
                def lower(d):
                    hi, lo = core.pair(XN_HI, XN_LO, d)
                    dve.wait_ge(upper, d + 1)
                    dve.tensor_tensor(lo, total[:, d % 2, :], hi.bitcast(F32), ALU.subtract)

                dve.sem_inc(pairs_free, 3)
                for d in range(KD):
                    for m in range(4):
                        core.split_lo(dve, g0 + 4 * d + m + 2)
                        if m == 0:
                            if d:
                                lower(d - 1)
                            continue
                        n = m - 1
                        dve.wait_ge(opened, 3 * d + n + 1)
                        to = total[:, d % 2, :] if n == 0 else part[:, n - 1, :]
                        dve.tensor_tensor(to, open_gate[:, n, :], ps[:, 2 * n + 1, :], ALU.mult).then_inc(pairs_free, 1)
                        if n:
                            dve.wait_ge(pairs_free, 3 + 3 * d + n + 1)
                            if n == 2:
                                dve.wait_ge(summed, 2 * d + 1)
                            dve.tensor_tensor(total[:, d % 2, :], total[:, d % 2, :], to, ALU.add).then_inc(summed, 1)
                lower(KD - 1)


def residual_stage(core, name, phase, rhs, per_tile=1, squares=None, beside=None):
    nc = core.nc
    beside = beside and beside(core)
    squared, added = core.sem(name + "_squared"), core.sem(name + "_squares_added")
    g0, e0 = core.used, core.evacs
    with ExitStack() as ctx:
        ps = ctx.enter_context(nc.psum_tensor(name + "_ps", [P, 4, T], F32))
        if beside:
            beside.ps = ctx.enter_context(nc.psum_tensor(name + "_beside_ps", [P, 4, T], F32))
        with nc.Block() as block:

            @block.sync
            def _(sp):
                core.stream(sp, phase)

            if beside:

                @block.gpsimd
                def _(pool):
                    beside.gpsimd(pool)

            @block.tensor
            def _(pe):
                if per_tile == 1:
                    pe_gemm(core, pe, KD, KD, rhs, ps)
                    return
                for half in range(2):
                    pe_gemm_deep(core, pe, KD // 2, per_tile, PHASES[phase][1], rhs, ps)
                    if beside:
                        beside.tensor(pe, half)

            @block.scalar
            def _(act):
                def square(d):
                    act.wait_ge(core.banks_free, 4 + e0 + d + 1)
                    if d >= 3:
                        act.wait_ge(added, d - 2)
                    to = squares[min(d, 1 + (d + 1) % 2)]
                    act.activation(to, core.h[:, d, :], ACT.Square).then_inc(squared, 1)

                for n in range(KD * per_tile):
                    core.split_hi(act, g0 + n + 2)
                    if beside and n == KD * per_tile // 2 - 1:
                        beside.scalar(act)
                    if squares and n and n % per_tile == 0:
                        square(n // per_tile - 1)
                if squares:
                    square(KD - 1)

            @block.vector
            def _(dve):
                def add_squares(d):
                    dve.wait_ge(squared, d + 1)
                    if d >= 2:
                        dve.wait_ge(added, d - 1)
                    dve.tensor_tensor(squares[0], squares[0], squares[1 + (d + 1) % 2], ALU.add).then_inc(added, 1)

                banks = 4 if per_tile == 1 else 2
                for n in range(KD * per_tile):
                    core.split_lo(dve, g0 + n + 2)
                    if (n + 1) % per_tile == 0:
                        d = n // per_tile
                        dve.wait_ge(core.groups_done, g0 + n + 1)
                        dve.tensor_tensor(core.h[:, d, :], core.h[:, d, :], ps[:, (e0 + d) % banks, :], ALU.add)\
                           .then_inc(core.banks_free, 1)
                        if squares and d >= 2:
                            add_squares(d - 1)
                if beside:
                    beside.vector(dve)


class LoadMemory:

    def __init__(self, core):
        self.core, self.mem_in = core, core.pool_dma_sem("mem_in")

    def gpsimd(self, pool):
        pool.dma_start(memory(self.core), self.core.dram["mem_t"]).then_inc(self.mem_in, 16)
        pool.wait_ge(self.mem_in, 16)

    def scalar(self, act):
        pass

    def vector(self, dve):
        pass


def memory(core):
    return core.arena[:, 12:16, :].rearrange("p a (n t) -> p (a n) t", n=2)


def memory_parts(core, k):
    halves = lambda tile: core.part(tile + k // 2, (k % 2) * MEM, (k % 2 + 1) * MEM)
    return halves(32), halves(36)


def cross_projections_stage(core):
    nc, a = core.nc, core.arena
    keys = a[:, 16:20, :].rearrange("p a (n t) -> p (a n) t", n=2)
    values = a[:, 20:24, :]
    queries = a[:, 24:32, :]
    g0, e0 = core.used, core.evacs
    with ExitStack() as ctx:
        ps = ctx.enter_context(nc.psum_tensor("cp_ps", [P, 4, T], F32))
        ps_v = ctx.enter_context(nc.psum_tensor("cp_ps_v", [P, 4, T], F32))
        with nc.Block() as block:

            @block.sync
            def _(sp):
                core.load_weights(sp, "ca", RING, 24)
                core.load_weights(sp, "ca", 24, 24 + RING)
                core.preloaded["ca"] = 24 + RING

            @block.tensor
            def _(pe):
                pe_gemm(core, pe, 8, KD, lambda k: memory_parts(core, k), ps, MEM)
                pe_by_token(core, pe, KD, 2 * T, lambda k: memory_parts(core, k), 2, lambda i, half: ps_v[:, 2 * i + half, :])
                pe_gemm(core, pe, 8, KD, lambda k: core.pair(XN_HI, XN_LO, k), ps)

            @block.scalar
            def _(act):
                for n in range(24):
                    core.split_hi(act, g0 + n + 2)
                    act.wait_ge(core.groups_done, g0 + n + 1)
                    if n < 8:
                        act.activation(keys[:, n, :], ps[:, (e0 + n) % 4, 0:MEM], ACT.Copy).then_inc(core.banks_free, 1)
                    elif n >= 16:
                        act.activation(queries[:, n - 16, :], ps[:, (e0 + n - 8) % 4, :], ACT.Copy, scale=1.0 / 16)\
                           .then_inc(core.banks_free, 1)
                    if n == 15:
                        for m in range(4):
                            act.activation(values[:, m, :], ps_v[:, m, :], ACT.Copy)

            @block.vector
            def _(dve):
                for n in range(24):
                    core.split_lo(dve, g0 + n + 2)


class Unit:

    def __init__(self, scores, n, values, add=None, add_query=None, keep=None, gate=None, first=True, last=True, group=0):
        self.scores, self.n, self.values = scores, n, values
        self.add, self.add_query, self.keep, self.gate = add, add_query, keep, gate
        self.first, self.last, self.group = first, last, group


def attention_stage(core, name, units, take):
    nc, a = core.nc, core.arena
    score_sb, turned_sb, stats = a[:, 35:39, :], a[:, 39:41, :], a[:, 41, :]
    count = len(units)
    scores_done = core.sem(name + "_scores_done")
    biased = core.sem(name + "_biased")
    max_ready = core.sem(name + "_max_ready")
    exp_ready = core.sem(name + "_exp_ready")
    inverse = core.sem(name + "_inverse")
    prob_ready = core.sem(name + "_prob_ready")
    turned = core.sem(name + "_turned")
    turned_ready = core.sem(name + "_turned_ready")
    out_done = core.sem(name + "_out_done")
    taken = core.sem(name + "_taken")
    groups = units[-1].group + 1
    last_of = {g: max(i for i, x in enumerate(units) if x.group == g) for g in range(groups)}
    stat = lambda u, n: stats[:, 4 * (u % 4) + n:4 * (u % 4) + n + 1]
    with ExitStack() as ctx:
        ps = ctx.enter_context(nc.psum_tensor(name + "_ps", [P, 8, T], F32))
        with nc.Block() as block:

            @block.tensor
            def _(pe):
                def scores(u):
                    x = units[u]
                    if u >= 4:
                        pe.wait_ge(exp_ready, u - 3)
                    for n, (lhs, rhs) in enumerate(x.scores):
                        mm = pe.matmul(ps[:, u % 4, 0:x.n], lhs, rhs, start=(n == 0), stop=(n == len(x.scores) - 1))
                    mm.then_inc(scores_done, 1)

                def turn(u):
                    x = units[u]
                    pe.wait_ge(prob_ready, u + 1)
                    if u >= 2:
                        pe.wait_ge(turned_ready, u - 1)
                    for lo in range(0, x.n, P):
                        n = min(P, x.n - lo)
                        mm = pe.transpose(ps[0:n, 4 + u % 2, lo:lo + P], score_sb[:, u % 4, lo:lo + n], core.c("ident"))
                    mm.then_inc(turned, 1)

                def output(u):
                    x = units[u]
                    pe.wait_ge(turned_ready, u + 1)
                    if x.group >= 2:
                        pe.wait_ge(taken, x.group - 1)
                    blocks = (x.n + P - 1) // P
                    for out, lhs, blk in x.values:
                        n = min(P, x.n - blk * P)
                        mm = pe.matmul(ps[out[0], 6 + x.group % 2, out[1]], lhs, turned_sb[0:n, u % 2, blk * P:(blk + 1) * P],
                                       start=(x.first and blk == 0), stop=(x.last and blk == blocks - 1), skip_group_check=True)
                    mm.then_inc(out_done, 1)

                for u in range(min(3, count)):
                    scores(u)
                for u in range(count):
                    if u + 3 < count:
                        scores(u + 3)
                    turn(u)
                    if u:
                        output(u - 1)
                output(count - 1)

            @block.scalar
            def _(act):
                def exps(u):
                    x = units[u]
                    act.wait_ge(max_ready, u + 1)
                    src = ps[:, u % 4, 0:x.n] if x.add is None else score_sb[:, u % 4, 0:x.n]
                    if x.add is None and u >= 4:
                        act.wait_ge(turned, u - 3)
                    act.activation(score_sb[:, u % 4, 0:x.n], src, ACT.Exp, bias=stat(u, 0), accum_out=stat(u, 1))\
                       .then_inc(exp_ready, 1)

                def place(u):
                    x = units[u]
                    act.wait_ge(turned, u + 1)
                    if u >= 2:
                        act.wait_ge(out_done, u - 1)
                    rows = min(P, x.n)
                    width = (x.n + P - 1) // P * P
                    act.activation(turned_sb[0:rows, u % 2, 0:width], ps[0:rows, 4 + u % 2, 0:width], ACT.Copy)\
                       .then_inc(turned_ready, 1)

                exps(0)
                for u in range(count):
                    if u + 1 < count:
                        exps(u + 1)
                    place(u)

            @block.vector
            def _(dve):
                def maxima(u):
                    x = units[u]
                    dve.wait_ge(scores_done, u + 1)
                    src = ps[:, u % 4, 0:x.n]
                    if x.add is not None:
                        if u >= 4:
                            dve.wait_ge(turned, u - 3)
                        dst = score_sb[:, u % 4, 0:x.n]
                        if x.add_query is not None:
                            dve.scalar_tensor_tensor(dst, src, x.add_query, x.add, ALU.add, ALU.add).then_inc(biased, 1)
                        else:
                            dve.tensor_tensor(dst, src, x.add, ALU.add).then_inc(biased, 1)
                        dve.wait_ge(biased, u + 1)
                        src = dst
                    elif u >= 4:
                        dve.wait_ge(exp_ready, u - 3)
                    dve.tensor_reduce(stat(u, 0), src, AX.X, ALU.max, negate=True).then_inc(max_ready, 1)

                def normalize(u):
                    x = units[u]
                    dve.wait_ge(exp_ready, u + 1)
                    dve.reciprocal(stat(u, 2), stat(u, 1)).then_inc(inverse, 1)
                    dve.wait_ge(inverse, u + 1)
                    p = score_sb[:, u % 4, 0:x.n]
                    if x.keep is not None:
                        dve.scalar_tensor_tensor(p, p, stat(u, 2), x.keep, ALU.mult, ALU.mult).then_inc(kept, 1)
                        kept_n[0] += 1
                        dve.wait_ge(kept, kept_n[0])
                        dve.tensor_scalar(p, p, x.gate, None, ALU.mult).then_inc(prob_ready, 1)
                    elif x.gate is not None:
                        dve.tensor_scalar(p, p, stat(u, 2), x.gate, ALU.mult, ALU.mult).then_inc(prob_ready, 1)
                    else:
                        dve.tensor_scalar(p, p, stat(u, 2), None, ALU.mult).then_inc(prob_ready, 1)

                kept, kept_n = (core.sem(name + "_kept") if any(x.keep is not None for x in units) else None), [0]
                for u in range(min(2, count)):
                    maxima(u)
                nxt = 0
                for u in range(count):
                    if u + 2 < count:
                        maxima(u + 2)
                    normalize(u)
                    if nxt < groups and last_of[nxt] <= u - 2:
                        dve.wait_ge(out_done, last_of[nxt] + 1)
                        take(dve, nxt, ps[:, 6 + nxt % 2, :]).then_inc(taken, 1)
                        nxt += 1
                for g in range(nxt, groups):
                    dve.wait_ge(out_done, last_of[g] + 1)
                    take(dve, g, ps[:, 6 + g % 2, :]).then_inc(taken, 1)


def cross_attention_stage(core):
    a = core.arena
    keys = a[:, 16:20, :].rearrange("p a (n t) -> p (a n) t", n=2)
    values = a[:, 20:24, :].rearrange("p (i n) t -> p i (n t)", n=2)
    queries = a[:, 24:32, :]
    units = []
    for h in range(4):
        for pair in range(2):
            for i in (2 * pair, 2 * pair + 1):
                cols = slice(i * P, (i + 1) * P)
                scores = [(queries[:, 2 * h + f, cols], keys[:, 2 * h + f, :]) for f in range(2)]
                vals = []
                for f in range(2):
                    for blk in range(2):
                        lo = f * 2 * P + (i % 2) * P
                        vals.append(((slice(0, P), slice(lo, lo + P)),
                                     values[:, blk, h * 256 + f * P:h * 256 + (f + 1) * P], blk))
                units.append(Unit(scores, MEM, vals, group=2 * h + pair))

    def take(dve, g, bank):
        h, pair = g // 2, g % 2
        return dve.tensor_copy(a[:, 2 * h:2 * h + 2, pair * 256:pair * 256 + 256], bank.rearrange("p (f t) -> p f t", f=2))

    attention_stage(core, "ca", units, take)


def ffn_up_stage(core):
    nc, a = core.nc, core.arena
    taps, hidden = a[:, 44:48, :], a[:, 48:50, :]
    g0, e0 = core.used, core.evacs
    now = core.sem("fu_now")
    steps = core.sem("fu_steps")
    gated = core.sem("fu_gated")
    made = core.sem("fu_made")
    upper = core.sem("fu_upper")
    lower_done = core.sem("fu_lower_done")
    with ExitStack() as ctx:
        ps = ctx.enter_context(nc.psum_tensor("fu_ps", [P, 4, T], F32))
        with nc.Block() as block:

            @block.sync
            def _(sp):
                core.stream(sp, "up")

            @block.tensor
            def _(pe):
                pe_gemm(core, pe, 2 * NF, KD, lambda k: core.pair(XN_HI, XN_LO, k), ps)

            which = lambda n: n // 2 + NF * (n % 2)

            @block.scalar
            def _(act):
                def split(j):
                    act.wait_ge(made, j + 1)
                    act.activation(core.pair(0, NF, j)[0], hidden[:, j % 2, :], ACT.Copy).then_inc(upper, 1)

                for n in range(2 * NF):
                    core.split_hi(act, g0 + n + 2)
                    if n % 2 and n >= 3:
                        split(n // 2 - 1)
                    act.wait_ge(core.groups_done, g0 + n + 1)
                    if n >= 4:
                        act.wait_ge(made, n // 2 - 1)
                    act.activation(taps[:, n % 4, :], ps[:, (e0 + n) % 4, :], ACT.Identity, scale=core.v("ffn_conv_w", 88 + which(n)),
                                   bias=core.v("ffn_conv_b", which(n))).then_inc(now, 1)
                    if n % 2:
                        act.wait_ge(core.banks_free, 4 + e0 + n)
                        act.activation(taps[:, (n - 1) % 4, :], taps[:, (n - 1) % 4, :], ACT.Silu).then_inc(gated, 1)
                split(NF - 1)

            @block.vector
            def _(dve):
                def lower(j):
                    hi, lo = core.pair(0, NF, j)
                    dve.wait_ge(upper, j + 1)
                    dve.tensor_tensor(lo, hidden[:, j % 2, :], hi.bitcast(F32), ALU.subtract).then_inc(lower_done, 1)

                for n in range(2 * NF):
                    core.split_lo(dve, g0 + n + 2)
                    if n % 2 == 0 and n >= 4:
                        lower(n // 2 - 2)
                    y, x = taps[:, n % 4, :], ps[:, (e0 + n) % 4, :]
                    dve.wait_ge(now, n + 1)
                    dve.scalar_tensor_tensor(y[:, 1:T], x[:, 0:T - 1], core.v("ffn_conv_w", 44 + which(n)), y[:, 1:T],
                                             ALU.mult, ALU.add).then_inc(steps, 1)
                    dve.wait_ge(steps, n + 1)
                    dve.scalar_tensor_tensor(y[:, 2:T], x[:, 0:T - 2], core.v("ffn_conv_w", which(n)), y[:, 2:T],
                                             ALU.mult, ALU.add).then_inc(core.banks_free, 1)
                    if n % 2:
                        dve.wait_ge(core.banks_free, 4 + e0 + n + 1)
                        dve.wait_ge(gated, n // 2 + 1)
                        dve.tensor_tensor(hidden[:, n // 2 % 2, :], taps[:, (n - 1) % 4, :], y, ALU.mult).then_inc(made, 1)
                lower(NF - 2)
                lower(NF - 1)


def second_window(core):
    return core.arena[:, 44:52, :]


def second_summary(core):
    return core.arena[:, 52:54, :].rearrange("p a t -> p (a t)")[:, 0:NT * HEADS * NC_CMP]


class RelativeBias:

    SPREAD = 896

    def __init__(self, core):
        a, sem = core.arena, core.sem
        self.core = core
        self.bucket = a[0:32, 54:56, :].rearrange("p a t -> p (a t)")
        self.table = core.small[0:32, 48:56]
        self.row = a[0:HEADS, 44:46, :].rearrange("p a t -> p (a t)")
        self.spread = a[:, 54:68, :].rearrange("p a t -> p (a t)").rearrange("p (h y) -> p h y", h=HEADS)
        self.scratch = core.nc.dram_tensor("bias_rows", (HEADS * VEC_DIST,), F32)
        self.bucket_in, self.table_in = core.pool_dma_sem("bi_bucket_in"), core.pool_dma_sem("bi_table_in")
        self.row_out, self.spread_in = core.pool_dma_sem("bi_row_out"), core.pool_dma_sem("bi_spread_in")
        self.row_done, self.row_ready = sem("bi_row_done"), sem("bi_row_ready")
        self.flipped, self.taken = sem("bi_flipped"), sem("bi_taken")

    def gpsimd(self, pool):
        dram = self.core.dram
        pool.dma_start(self.bucket, dram["bucket"]).then_inc(self.bucket_in, 16)
        pool.dma_start(self.table, dram["table"]).then_inc(self.table_in, 16)
        pool.wait_ge(self.row_ready, 2)
        pool.dma_start(self.scratch.ap().rearrange("(h y) -> h y", h=HEADS), self.row).then_inc(self.row_out, 16)
        pool.wait_ge(self.row_out, 16)
        pool.dma_start(self.spread, bass.AP(self.scratch, 0, [[1, P], [VEC_DIST, HEADS], [1, self.SPREAD]]))\
            .then_inc(self.spread_in, 16)

    def tensor(self, pe, half):
        ps = self.ps
        if half == 0:
            pe.wait_ge(self.bucket_in, 16)
            pe.wait_ge(self.table_in, 16)
            for n in range(2):
                pe.matmul(ps[0:HEADS, n, :], self.table, self.bucket[:, n * T:(n + 1) * T], start=True, stop=True)\
                  .then_inc(self.row_done, 1)
            return
        flip = self.core.c("flip")
        pe.wait_ge(self.spread_in, 16)
        for h in range(HEADS):
            if h >= 4:
                pe.wait_ge(self.taken, h - 3)
            pe.matmul(ps[:, h % 4, :], flip, self.spread[:, h, 0:T], start=True, stop=True).then_inc(self.flipped, 1)
        per = HEADS * NC_CMP
        for i in range(NT):
            lo = 415 - i * P
            pe.wait_ge(self.taken, HEADS - 3 + i // 2)
            pe.matmul(ps[:, i // 2, (i % 2) * per:(i % 2 + 1) * per], flip,
                      self.spread[:, :, lo:lo + 16 * (NC_CMP - 1) + 1:16], start=True, stop=True).then_inc(self.flipped, 1)

    def scalar(self, act):
        for n in range(2):
            act.wait_ge(self.row_done, n + 1)
            act.activation(self.row[:, n * T:(n + 1) * T], self.ps[0:HEADS, n, :], ACT.Copy).then_inc(self.row_ready, 1)

    def vector(self, dve):
        core, ps = self.core, self.ps
        window, summary = second_window(core), second_summary(core)
        dve.wait_ge(self.spread_in, 16)
        for h in range(HEADS):
            dve.wait_ge(self.flipped, h + 1)
            dve.tensor_copy(window[:, h, 0:T - P], ps[:, h % 4, 0:T - P])
            dve.tensor_tensor(window[:, h, T - P:T], ps[:, h % 4, T - P:T], core.c("causal_add"), ALU.add).then_inc(self.taken, 1)
        half = NT * HEADS * NC_CMP // 2
        for n in range(2):
            dve.wait_ge(self.flipped, HEADS + 2 * n + 2)
            view = lambda x: x.rearrange("p (i h b) -> p i h b", i=2, h=HEADS)
            mask_add = core.c("cmp_add", 2 * n * NC_CMP, 2 * NC_CMP).rearrange("p (i b) -> p i b", i=2)
            dve.tensor_tensor(view(summary[:, n * half:(n + 1) * half]), view(ps[:, n, 0:half]),
                              mask_add.unsqueeze(2).broadcast_to([P, 2, HEADS, NC_CMP]), ALU.add)


def second_projections_stage(core):
    nc, a, dram = core.nc, core.arena, core.dram
    by_feature = a[:, 12:28, :]
    fox_value = a[:, 28:32, :]
    group_value = a[:, 32:34, :].rearrange("p a (n t) -> p (a n) t", n=2)
    logits = a[:, 34, 0:NT * 32].rearrange("p (i n) -> p i n", i=NT)
    small_w, small_hi, small_lo = a[:, 11, 0:KD * 32], core.part(54, 0, KD * 32), core.part(54, KD * 32, 2 * KD * 32)
    g0, e0 = core.used, core.evacs
    mask = a[:, 8, :]
    head_in, piece_in, w2_in = core.pool_dma_sem("sp_head_in"), core.pool_dma_sem("sp_piece_in"), core.pool_dma_sem("sp_w2_in")
    cleared = core.sem("sp_mask_cleared")
    small_in = core.sem("sp_small_in")
    small_upper = core.sem("sp_small_upper")
    small_split = core.sem("sp_small_split")
    small_done = core.sem("sp_small_done")
    fox_taken = core.sem("sp_fox_taken")
    with ExitStack() as ctx:
        ps = ctx.enter_context(nc.psum_tensor("sp_ps", [P, 4, T], F32))
        ps_v = ctx.enter_context(nc.psum_tensor("sp_ps_v", [P, 4, T], F32))
        with nc.Block() as block:

            @block.sync
            def _(sp):
                core.stream(sp, "in2")

            @block.gpsimd
            def _(pool):
                pieces, w2 = compress_weights(core)
                for n in range(3):
                    pool.dma_start(pieces[n], dram["cmp_w1_" + "kv"[n // 2]][:, :, (n % 2) * P:(n % 2 + 1) * P])\
                        .then_inc(piece_in, 16)
                for s, name in enumerate("kv"):
                    pool.dma_start(w2[:, s], dram["cmp_w2_" + name]).then_inc(w2_in, 16)
                pool.dma_start(a[0:HEADS, 9:11, :].rearrange("p a t -> p (a t)"), dram["head_row"]).then_inc(head_in, 16)
                pool.memset(mask, 0.0).then_inc(cleared, 1)
                pool.wait_ge(cleared, 1)
                pool.tensor_copy(mask[:, T - P:T], core.c("causal_add"))
                pool.wait_ge(piece_in, 48)
                pool.wait_ge(w2_in, 32)
                pool.wait_ge(head_in, 16)

            @block.tensor
            def _(pe):
                x = lambda k: core.pair(XN_HI, XN_LO, k)
                pe_gemm(core, pe, 16, KD, x, ps)
                pe_by_token(core, pe, 4, T, x, NT, lambda i, half: ps_v[:, i, :])
                pe.wait_ge(core.banks_free, 4 + e0 + 16)
                pe_by_token(core, pe, 2, 256, x, NT, lambda i, half: ps[:, i, :])
                pe.wait_ge(small_split, 1)
                pe.wait_ge(fox_taken, NT)
                for i in range(NT):
                    for k in range(KD):
                        cols = slice(i * P, (i + 1) * P)
                        mm = product(pe, ps_v[:, 0, i * 32:(i + 1) * 32], (x(k)[0][:, cols], x(k)[1][:, cols]),
                                     (small_hi[:, k * 32:(k + 1) * 32], small_lo[:, k * 32:(k + 1) * 32]), k == 0, k == KD - 1)
                mm.then_inc(small_done, 1)

            @block.scalar
            def _(act):
                act.dma_start(small_w, dram["w_small2"]).then_inc(small_in, 16)
                for n in range(22):
                    core.split_hi(act, g0 + n + 2)
                    act.wait_ge(core.groups_done, g0 + n + 1)
                    if n < 16:
                        scale = HD ** -0.5 if n < 4 or 8 <= n < 12 else 1.0
                        act.activation(by_feature[:, n, :], ps[:, (e0 + n) % 4, :], ACT.Copy, scale=scale)\
                           .then_inc(core.banks_free, 1)
                    if n == 8:
                        act.wait_ge(small_in, 16)
                        act.activation(small_hi, small_w, ACT.Copy).then_inc(small_upper, 1)
                    if n == 19:
                        for i in range(NT):
                            act.activation(fox_value[:, i, :], ps_v[:, i, :], ACT.Copy).then_inc(fox_taken, 1)
                for i in range(NT):
                    act.activation(group_value[:, i, :], ps[:, i, 0:256], ACT.Copy)
                act.wait_ge(small_done, 1)
                act.activation(logits, ps_v[:, 0, 0:NT * 32].rearrange("p (i n) -> p i n", i=NT), ACT.Copy)

            @block.vector
            def _(dve):
                for n in range(22):
                    core.split_lo(dve, g0 + n + 2)
                    if n == 10:
                        dve.wait_ge(small_upper, 1)
                        dve.tensor_tensor(small_lo, small_w, small_hi.bitcast(F32), ALU.subtract).then_inc(small_split, 1)


def forget_stage(core):
    nc, a = core.nc, core.arena
    logits = a[:, 34, 0:NT * 32].rearrange("p (i n) -> p i n", i=NT)
    gates = a[:, 34, 128:128 + NT * 24].rearrange("p (i n) -> p i n", i=NT)
    x = a[:, 34, 256:288].rearrange("p (i n) -> p i n", i=NT)
    soft = a[:, 34, 288:320].rearrange("p (i n) -> p i n", i=NT)
    row = a[0:HEADS, 11, :]
    sums = core.small[:, 0:32].rearrange("p (i n) -> p i n", i=NT)
    shifted, logged, steps = core.sem("fg_shifted"), core.sem("fg_logged"), core.sem("fg_steps")
    soft_ready, summed = core.sem("fg_soft_ready"), core.sem("fg_summed")
    with ExitStack() as ctx:
        ps = ctx.enter_context(nc.psum_tensor("fg_ps", [P, 2, T], F32))
        with nc.Block() as block:

            @block.vector
            def _(dve):
                bias = core.vec[:, VEC_AT["b_forget"]:VEC_AT["b_forget"] + 8].unsqueeze(1).broadcast_to([P, NT, 8])
                dve.tensor_tensor(x, logits[:, :, 0:8], bias, ALU.add).then_inc(shifted, 1)
                dve.wait_ge(shifted, 1)
                dve.wait_ge(logged, 3)
                dve.tensor_scalar(x, x, -1.0, 0.0, ALU.mult, ALU.max).then_inc(steps, 1)
                dve.wait_ge(steps, 1)
                dve.tensor_tensor(soft, soft, x, ALU.add).then_inc(soft_ready, 1)
                dve.wait_ge(summed, 1)
                dve.tensor_scalar(sums, ps[:, 0, 0:32].rearrange("p (i n) -> p i n", i=NT), -1.0, None, ALU.mult)

            @block.scalar
            def _(act):
                act.wait_ge(shifted, 1)
                act.activation(soft, x, ACT.Abs).then_inc(logged, 1)
                act.wait_ge(logged, 1)
                act.activation(soft, soft, ACT.Exp, scale=-1.0).then_inc(logged, 1)
                act.wait_ge(logged, 2)
                act.activation(soft, soft, ACT.Ln, bias=1.0).then_inc(logged, 1)
                act.activation(gates, logits[:, :, 8:32], ACT.Sigmoid)
                act.wait_ge(summed, 1)
                act.activation(row, ps[0:HEADS, 1, :], ACT.Copy)

            @block.tensor
            def _(pe):
                pe.wait_ge(soft_ready, 1)
                for i in range(NT):
                    for j in range(i + 1):
                        pe.matmul(ps[:, 0, i * 8:(i + 1) * 8], core.c("upper" if j == i else "ones"), soft[:, j, :],
                                  start=(j == 0), stop=(j == i))
                for i in range(NT):
                    for j in range(i + 1):
                        mm = pe.matmul(ps[0:HEADS, 1, i * P:(i + 1) * P], soft[:, j, :], core.c("upper" if j == i else "ones"),
                                       start=(j == 0), stop=(j == i))
                mm.then_inc(summed, 1)


def compress_weights(core):
    a = core.arena
    pieces = [a[:, lo:lo + 4, :].rearrange("p a t -> p (a t)").rearrange("p (l m) -> p l m", l=16) for lo in (0, 4, 39, 0)]
    return pieces, a[:, 43, 256:512].rearrange("p (s f d) -> p s f d", s=2, f=2)


def compress_stage(core):
    nc, a, dram = core.nc, core.arena, core.dram
    B = NC_CMP
    blocks = a[:, 35:39, :].rearrange("p a t -> p (a t)")[:, 0:2 * 16 * (2 * B + 1)].rearrange("p (s l n) -> p s l n", s=2, l=16)
    of_group = lambda x, s, g: blocks[x, s, :, g * B:(g + 1) * B]
    by_block = lambda x: bass.AP(x.tensor, x.offset, [list(x.ap[0]), [2, 16], [16, B]])
    pieces, w2 = compress_weights(core)
    hidden = a[:, 43, 0:8 * B].rearrange("p (s f n) -> p s f n", s=2, f=2)
    bias = a[:, 43, 8 * B:8 * B + 4].rearrange("p (s f) -> p s f", s=2)
    keys, values = a[:, 54, 0:B], a[0:B, 54, 128:256]
    last_in = core.sem("cm_last_in")
    moved, placed, copied_k = core.sem("cm_moved"), core.sem("cm_placed"), core.sem("cm_copied_k")
    copied, pos_ready = core.sem("cm_copied"), core.sem("cm_pos_ready")
    hidden_done, hidden_ready, out_done = core.sem("cm_hidden_done"), core.sem("cm_hidden_ready"), core.sem("cm_out_done")
    with ExitStack() as ctx:
        ps = ctx.enter_context(nc.psum_tensor("cm_ps", [P, 8, T], F32))
        with nc.Block() as block:

            @block.sync
            def _(sp):
                sp.wait_ge(hidden_done, 1)
                sp.dma_start(pieces[3], dram["cmp_w1_v"][:, :, P:2 * P]).then_inc(last_in, 16)

            @block.gpsimd
            def _(pool):
                for g in range(2):
                    ins = pool.tensor_copy(of_group(slice(0, HD), 1, g), by_block(a[HD * g:HD * g + HD, 25, 0:T - 1]))
                ins.then_inc(copied, 1)

            @block.tensor
            def _(pe):
                for s in range(2):
                    for g in range(2):
                        pe.matmul(ps[HD:P, 4 * s + 2 + g, 0:T - 1], core.c("ident", HD * g, HD), a[:, 24 + s, 1:T],
                                  start=True, stop=True).then_inc(moved, 1)
                for n in range(4):
                    s, f = n // 2, n % 2
                    if n == 3:
                        pe.wait_ge(last_in, 16)
                    if f == 0:
                        pe.wait_ge(placed, 2 * s + 2)
                        pe.wait_ge(copied if s else copied_k, 1)
                    for l in range(16):
                        mm = pe.matmul(ps[:, 4 * s + 2 + f, 0:2 * B + 1], pieces[n][:, l, :], blocks[:, s, l, :],
                                       start=(l == 0), stop=(l == 15))
                    mm.then_inc(hidden_done, 1)
                pe.wait_ge(hidden_ready, 4)
                pe.wait_ge(pos_ready, 4)
                for g in range(2):
                    for f in range(2):
                        pe.matmul(ps[HD * g:HD * g + HD, 0, 0:B], w2[:, 0, f, :], hidden[:, 0, f, g * B:(g + 1) * B],
                                  start=(f == 0), stop=(f == 1))
                for g in range(2):
                    for f in range(2):
                        mm = pe.matmul(ps[0:B, 1, g * HD:(g + 1) * HD], hidden[:, 1, f, g * B:(g + 1) * B], w2[:, 1, f, :],
                                       start=(f == 0), stop=(f == 1))
                mm.then_inc(out_done, 1)

            @block.vector
            def _(dve):
                for g in range(2):
                    dve.tensor_copy(of_group(slice(0, HD), 0, g), by_block(a[HD * g:HD * g + HD, 24, 0:T - 1]))
                for s in range(2):
                    at_pe = VEC_AT["pe_" + "kv"[s]]
                    ins = dve.tensor_copy(blocks[:, s, :, 2 * B], core.vec[:, at_pe:at_pe + 16])
                ins.then_inc(copied_k, 1)
                for n in range(4):
                    dve.wait_ge(hidden_done, n + 1)
                    dve.tensor_copy(bias[:, n // 2, n % 2:n % 2 + 1], ps[:, 4 * (n // 2) + 2 + n % 2, 2 * B:2 * B + 1]).then_inc(pos_ready, 1)
                dve.wait_ge(out_done, 1)
                dve.tensor_copy(keys, ps[:, 0, 0:B])
                dve.tensor_copy(values, ps[0:B, 1, 0:P])

            @block.scalar
            def _(act):
                for n in range(4):
                    act.wait_ge(moved, n + 1)
                    act.activation(of_group(slice(HD, P), n // 2, n % 2), by_block(ps[HD:P, 4 * (n // 2) + 2 + n % 2, 0:T - 1]), ACT.Copy)\
                       .then_inc(placed, 1)
                for n in range(4):
                    act.wait_ge(pos_ready, n + 1)
                    act.activation(hidden[:, n // 2, n % 2, :], ps[:, 4 * (n // 2) + 2 + n % 2, 0:2 * B], ACT.Silu,
                                   bias=bias[:, n // 2, n % 2:n % 2 + 1]).then_inc(hidden_ready, 1)


def fox_attention_stage(core):
    a = core.arena
    query, key, value = a[:, 12:16, :], a[:, 16:20, :], a[:, 28:32, :]
    head_row = a[0:HEADS, 9:11, :].rearrange("p a t -> p (a t)")
    row, mask = a[0:HEADS, 11, :], a[:, 8, :]
    units = []
    for h in range(HEADS):
        c, rows = h // 2, slice(HD * (h % 2), HD * (h % 2) + HD)
        for i in range(NT):
            n = (i + 1) * P
            cols = slice(i * P, (i + 1) * P)
            scores = [(query[rows, c, cols], key[rows, c, 0:n]), (head_row[:, h * P:(h + 1) * P], row[:, 0:n])]
            vals = [((rows, cols), value[:, j, h * HD:(h + 1) * HD], j) for j in range(i + 1)]
            units.append(Unit(scores, n, vals, add=mask[:, T - n:T], add_query=core.small[:, i * 8 + h:i * 8 + h + 1], group=c))
    attention_stage(core, "fox", units, lambda dve, g, bank: dve.tensor_copy(a[:, g, :], bank))


def sparse_attention_stage(core):
    a = core.arena
    query, select_key, window_key = a[:, 20:24, :], a[:, 26, :], a[:, 27, :]
    group_value = a[:, 32:34, :].rearrange("p a (n t) -> p (a n) t", n=2)
    gates = a[:, 34, 128:128 + NT * 24]
    window, summary = second_window(core), second_summary(core)
    cmp_key, cmp_value = a[:, 54, 0:NC_CMP], a[0:NC_CMP, 54, 128:256]
    units = []
    for h2 in range(HEADS):
        h, c, rows = h2, h2 // 2, slice(HD * (h2 % 2), HD * (h2 % 2) + HD)
        g = h // 4
        q_rows = slice(HD * g, HD * g + HD)
        for i in range(NT):
            n = (i + 1) * P
            cols = slice(i * P, (i + 1) * P)
            q = query[q_rows, h % 4, cols]
            gate = lambda b: gates[:, i * 24 + 3 * h + b:i * 24 + 3 * h + b + 1]
            for b, k in ((1, select_key), (2, window_key)):
                lo = P * (b - 1) + g * HD
                vals = [((rows, cols), group_value[:, j, lo:lo + HD], j) for j in range(i + 1)]
                units.append(Unit([(q, k[q_rows, 0:n])], n, vals, add=window[:, h, T - n:T], gate=gate(b), first=(b == 1),
                                  last=False, group=c))
            add = summary[:, (i * HEADS + h) * NC_CMP:(i * HEADS + h + 1) * NC_CMP]
            units.append(Unit([(q, cmp_key[q_rows, :])], NC_CMP, [((rows, cols), cmp_value[:, g * HD:(g + 1) * HD], 0)], add=add,
                              keep=core.c("cmp_keep", i * NC_CMP, NC_CMP), gate=gate(0), first=False, last=True, group=c))
    attention_stage(core, "nsa", units, lambda dve, g, bank: dve.tensor_copy(a[:, 4 + g, :], bank))


def second_gates_stage(core):
    nc, a = core.nc, core.arena
    opened_gate, part, total = a[:, 44:46, :], a[:, 46, :], a[:, 47:49, :]
    g0 = core.used
    tiles_free = core.sem("g2_tiles_free")
    opened, summed = core.sem("g2_opened"), core.sem("g2_summed")
    branch_done = core.sem("g2_branch_done")
    upper = core.sem("g2_upper")
    with ExitStack() as ctx:
        ps = ctx.enter_context(nc.psum_tensor("g2_ps", [P, 8, T], F32))
        with nc.Block() as block:

            @block.sync
            def _(sp):
                core.stream(sp, "gates2")

            @block.tensor
            def _(pe):
                with pe.Fori(0, KD // 4) as turn:
                    for q in range(4):
                        bank = 4 * (q % 2)
                        pe.wait_ge(tiles_free, turn * 4 + q + 1)
                        for n in range(3):
                            g = g0 + 3 * q + n
                            core.wait_weights(pe, g, turn, 12)
                            for b in range(KD):
                                w = core.weights(g, b * P, (b + 1) * P)
                                if n < 2:
                                    mm = product(pe, ps[:, bank + n, :], w, core.pair(XN_HI, XN_LO, b), b == 0, b == KD - 1)
                                else:
                                    mm = product(pe, ps[:, bank + 2 + b // 4, :], w, core.pair(12, 20, b), b % 4 == 0, b % 4 == 3)
                            mm.then_inc(core.groups_done, 1)
                core.used += 24

            @block.scalar
            def _(act):
                def split(d):
                    act.wait_ge(summed, d + 1)
                    act.activation(core.pair(28, 36, d)[0], total[:, d % 2, :], ACT.Copy).then_inc(upper, 1)

                for d in range(KD):
                    for n in range(3):
                        core.split_hi(act, g0 + 3 * d + n + 2)
                        if n < 2:
                            act.wait_ge(core.groups_done, g0 + 3 * d + n + 1)
                            if d:
                                act.wait_ge(tiles_free, 2 + d)
                            act.activation(opened_gate[:, n, :], ps[:, 4 * (d % 2) + n, :], ACT.Sigmoid).then_inc(opened, 1)
                        elif d:
                            split(d - 1)
                split(KD - 1)

            @block.vector
            def _(dve):
                def lower(d):
                    hi, lo = core.pair(28, 36, d)
                    dve.wait_ge(upper, d + 1)
                    dve.tensor_tensor(lo, total[:, d % 2, :], hi.bitcast(F32), ALU.subtract)

                dve.sem_inc(tiles_free, 2)
                for d in range(KD):
                    for n in range(3):
                        core.split_lo(dve, g0 + 3 * d + n + 2)
                    if d >= 1:
                        lower(d - 1)
                    dve.wait_ge(core.groups_done, g0 + 3 * d + 3)
                    dve.wait_ge(opened, 2 * d + 2)
                    if d:
                        dve.wait_ge(summed, d)
                    dve.tensor_tensor(part, opened_gate[:, 1, :], ps[:, 4 * (d % 2) + 3, :], ALU.mult).then_inc(branch_done, 1)
                    dve.tensor_tensor(total[:, d % 2, :], opened_gate[:, 0, :], ps[:, 4 * (d % 2) + 2, :], ALU.mult)\
                       .then_inc(tiles_free, 1)
                    dve.wait_ge(branch_done, d + 1)
                    dve.wait_ge(tiles_free, 2 + d + 1)
                    dve.tensor_tensor(total[:, d % 2, :], total[:, d % 2, :], part, ALU.add).then_inc(summed, 1)
                lower(KD - 1)


def ff1_stage(core, name, phase):
    nc = core.nc
    lifted_sb, product_sb = core.arena[:, 32:34, :], core.arena[:, 34:36, :]
    g0, e0, count = core.used, core.evacs, PHASES[phase][0]
    lifted, upper = core.sem(name + "_lifted"), core.sem(name + "_upper")
    with ExitStack() as ctx:
        ps = ctx.enter_context(nc.psum_tensor(name + "_ps", [P, 4, T], F32))
        with nc.Block() as block:

            @block.sync
            def _(sp):
                core.stream(sp, phase)

            @block.tensor
            def _(pe):
                pe_gemm(core, pe, count, KD, lambda k: core.pair(XN_HI, XN_LO, k), ps)

            @block.scalar
            def _(act):
                def split(n):
                    act.wait_ge(core.banks_free, 4 + e0 + n + 1)
                    act.activation(core.pair(0, 16, n)[0], product_sb[:, n % 2, :], ACT.Copy).then_inc(upper, 1)

                for n in range(count):
                    core.split_hi(act, g0 + n + 2)
                    if n:
                        split(n - 1)
                split(count - 1)

            @block.vector
            def _(dve):
                def lower(n):
                    hi, lo = core.pair(0, 16, n)
                    dve.wait_ge(upper, n + 1)
                    dve.tensor_tensor(lo, product_sb[:, n % 2, :], hi.bitcast(F32), ALU.subtract)

                for n in range(count):
                    bank = ps[:, (e0 + n) % 4, :]
                    core.split_lo(dve, g0 + n + 2)
                    if n >= 2:
                        lower(n - 2)
                    dve.wait_ge(core.groups_done, g0 + n + 1)
                    dve.tensor_scalar(lifted_sb[:, n % 2, :], bank, 0.0, None, ALU.max).then_inc(lifted, 1)
                    dve.wait_ge(lifted, n + 1)
                    dve.tensor_tensor(product_sb[:, n % 2, :], lifted_sb[:, n % 2, :], bank, ALU.mult).then_inc(core.banks_free, 1)
                lower(count - 2)
                lower(count - 1)


def store_stage(core):
    out_stored = core.sem("out_stored")
    with core.nc.Block() as block:

        @block.sync
        def _(sp):
            sp.dma_start(core.dram["out"], core.arena[:, 0:KD, :]).then_inc(out_stored, 16)
            sp.wait_ge(out_stored, 16)


def norm_h(name, gain, scratch=40):
    return lambda core: norm_stage(core, name, lambda k: core.h[:, k, :], gain, split=lambda k: core.pair(XN_HI, XN_LO, k),
                                   scratch=scratch)


def norm_memory(core):
    norm_stage(core, "nmem", lambda k: memory(core)[:, k, :], "norm_mem", split=lambda k: memory_parts(core, k), width=MEM)


def norm_again(core):
    norm_stage(core, "nmix2", lambda k: core.h[:, k, :], "norm_mix", split=lambda k: core.pair(36, 44, k), scratch=55)


def squares_of(at):
    return lambda core: [core.arena[:, at + n, :] for n in range(3)]


def norm_summed(name, gain, at, split=True, dst=None, scratch=40):
    return lambda core: norm_stage(core, name, lambda k: core.h[:, k, :], gain,
                                   split=(lambda k: core.pair(XN_HI, XN_LO, k)) if split else None,
                                   dst=dst and dst(core), squares=squares_of(at)(core)[:2], scratch=scratch)


def merged_parts(core):
    return lambda k: core.pair(XN_HI, XN_LO, k)


STAGES = [
    setup_stage,
    norm_h("nmix", "norm_mix"),
    proj_stage,
    stick_breaking_stage,
    time_mix_stage,
    time_mix_scale_stage,
    time_mix_chunks_stage,
    time_mix_out_stage,
    norm_again,
    lambda core: split_stage(core, "ys", 12, 0, 12, 24),
    gates_stage,
    lambda core: residual_stage(core, "mix", "mix", merged_parts(core), squares=squares_of(50)(core), beside=LoadMemory),
    norm_memory,
    norm_summed("nca", "norm_ca", 50),
    cross_projections_stage,
    cross_attention_stage,
    lambda core: split_stage(core, "cs", KD, 0, XN_HI, XN_LO),
    lambda core: residual_stage(core, "cawo", "ca", merged_parts(core), squares=squares_of(50)(core)),
    norm_summed("nffn", "norm_ffn", 50),
    ffn_up_stage,
    lambda core: residual_stage(core, "down", "down", lambda k: core.pair(0, NF, k), per_tile=2,
                                squares=squares_of(68)(core), beside=RelativeBias),
    norm_summed("nfirst", "norm_final", 68, split=False, scratch=0, dst=lambda core: lambda k: core.h[:, k, :]),
    clear_semaphores_stage,
    norm_h("nattn", "g_attn_2", scratch=0),
    second_projections_stage,
    forget_stage,
    compress_stage,
    fox_attention_stage,
    sparse_attention_stage,
    lambda core: split_stage(core, "y2", KD, 0, 12, 20),
    second_gates_stage,
    lambda core: residual_stage(core, "out2", "out2", lambda k: core.pair(28, 36, k), squares=squares_of(50)(core)),
    norm_summed("nmlp", "g_mlp_2", 50),
    lambda core: ff1_stage(core, "f1a", "ff1a"),
    lambda core: residual_stage(core, "f2a", "ff2a", lambda k: core.pair(0, 16, k), per_tile=2),
    lambda core: ff1_stage(core, "f1b", "ff1b"),
    lambda core: residual_stage(core, "f2b", "ff2b", lambda k: core.pair(0, 16, k), per_tile=2,
                                squares=squares_of(50)(core)),
    norm_summed("nfinal", "g_final_2", 50, split=False, dst=lambda core: lambda k: core.arena[:, k, :]),
    store_stage,
]


def hybrid_decoder_kernel(nc, dram, stages):
    with ExitStack() as ctx:
        core = Core(nc, ctx, dram)
        for stage in stages:
            stage(core)



def _tiles(w):
    k, n = w.shape
    return w.reshape(k // P, P, n // P, P).transpose(2, 1, 0, 3).reshape(n // P, P, k)


def _by_rows(w, per):
    k, n = w.shape
    return w.reshape(k // (per * P), per, P, n).transpose(0, 2, 1, 3).reshape(k // (per * P), P, per * n)


def _columns(v):
    return v.reshape(-1, P).T


def _constants():
    c = {name: np.zeros((P, cols), np.float32) for name, cols in CONSTS}
    i = np.arange(P)
    row, col = i[:, None], i[None, :]
    c["ident"][:] = row == col
    c["ones"][:] = 1.0
    c["head_ones"][:] = row // HD == col // HD
    c["upper"][:] = row <= col
    c["causal4"][:] = np.concatenate([row < col, row <= col, row < col, row <= col], axis=1)
    c["neg_tri"][:] = -1.0 * (row >= col)
    c["neg_ones"][:] = -1.0
    c["neg_diag_t"][:] = np.where(row < col, 0.0, NEG)
    for n in range(7):
        b = 1 << n
        c["level"][:, n * P:(n + 1) * P] = (col // b % 2 == 1) & (row // b == col // b - 1)
    c["flip"][:] = row + col == P - 1
    c["causal_add"][:] = np.where(col <= row, 0.0, NEG)
    for t in range(NT):
        for b in range(NC_CMP):
            ok = 16 * b + 31 <= t * P + i
            c["cmp_add"][:, t * NC_CMP + b] = np.where(ok, 0.0, NEG)
            c["cmp_keep"][:, t * NC_CMP + b] = ok
    return np.concatenate([c[name] for name, _ in CONSTS], axis=1)


def _bucket_rows():
    dist = np.maximum(511 - np.arange(VEC_DIST), 0)
    exact = 16
    nf = np.maximum(dist, exact).astype(np.float32)
    log_b = exact + (np.log(nf / np.float32(exact)) / np.float32(math.log(128 / exact)) * np.float32(32 - exact)).astype(np.int32)
    bucket = np.where(dist < exact, dist, np.minimum(log_b, 31))
    return (np.arange(32)[:, None] == bucket[None, :]).astype(np.float32)


def _layout(i):
    f = lambda name: np.asarray(i[name])[0]
    w_comb, w_in = f("w_comb"), f("w_in_2")
    a = {}
    a["x_t"] = np.asarray(i["x"])[0].T.reshape(KD, P, T).transpose(1, 0, 2)
    a["mem_t"] = np.asarray(i["mem"])[0].T.reshape(KD, P, MEM).transpose(1, 0, 2)
    conv, sb, gate, rwkv = w_comb[:, 0:1536], w_comb[:, 1536:3072], w_comb[:, 3072:6144], w_comb[:, 6144:]
    ct = _tiles(conv)
    order = [x for t in range(4) for x in (4 + t, 8 + t, t)]
    a["w_proj"] = np.concatenate([_tiles(rwkv), ct[order], _tiles(sb[:, 0:1024]), _by_rows(sb[:, 1024:], 2)])
    gt = _tiles(gate).reshape(3, 8, P, 1024)
    bt = np.stack([_tiles(f("branch_proj")[n]) for n in range(3)])
    both = np.concatenate([gt, bt], axis=3)
    a["w_gates"] = both.transpose(1, 2, 0, 3).reshape(8, P, 4, 9 * P).transpose(0, 2, 1, 3).reshape(32, P, 9 * P)
    a["w_mix"] = _tiles(f("w_mix_out"))
    kv = f("ca_wkv")
    a["w_ca"] = np.concatenate([_tiles(kv[:, 0:1024]), _by_rows(kv[:, 1024:], 1), _tiles(f("ca_wq")), _tiles(f("ca_wo"))])
    up = _tiles(f("ffn_up"))
    a["w_up"] = up[[x for t in range(NF) for x in (t, NF + t)]]
    a["w_down"] = _tiles(f("ffn_down")).reshape(8, P, 2, 11 * P).transpose(0, 2, 1, 3).reshape(16, P, 11 * P)
    cuts = np.cumsum((512, 512, 512, 8, 512, 128, 128, 128, 128, 128, 128, 24, 1024, 1024))[:-1]
    fq, fk, fv, fl, nq, kc, vc, ksl, vsl, kwn, vwn, ng, ga, gb = np.split(w_in, cuts, axis=1)
    nq = nq.reshape(D, 2, 4, HD).transpose(0, 2, 1, 3).reshape(D, 512)
    a["w_in2"] = np.concatenate([_tiles(np.concatenate([fq, fk, nq, kc, vc, ksl, kwn], axis=1)), _by_rows(fv, 2),
                                 _by_rows(np.concatenate([vsl, vwn], axis=1), 4)])
    a["w_small2"] = _by_rows(np.concatenate([fl, ng], axis=1), 8)[0]
    bf, bn = _tiles(f("w_br_fox_2")), _tiles(f("w_br_nsa_2"))
    a["w_gates2"] = np.stack([_tiles(ga), _tiles(gb), np.concatenate([bf, bn], axis=2)], axis=1).reshape(24, P, 1024)
    a["w_out2"] = _tiles(f("w_out_2"))
    ff1 = _tiles(f("w_ff1_2"))
    ff2 = _tiles(f("w_ff2_2")).reshape(8, P, 4, 1024).transpose(0, 2, 1, 3)
    for n, half in enumerate("ab"):
        a["w_ff1" + half] = ff1[16 * n:16 * n + 16]
        a["w_ff2" + half] = ff2[:, 2 * n:2 * n + 2].reshape(16, P, 1024)
    a["wa_lora"] = np.concatenate([f("w_lora"), f("a_lora")])
    a["g_lora_t"] = f("g_lora")
    a["table"] = np.asarray(i["rel_bias_table_2"])
    for s in "kv":
        a["cmp_w1_" + s] = f(f"cmp_w1_{s}_2").reshape(16, P, 256).transpose(1, 0, 2)
        a["cmp_w2_" + s] = f(f"cmp_w2_{s}_2").reshape(2, P, HD).transpose(1, 0, 2)
    vec = {
        "norm_mix": i["norm_mix"], "conv_w": i["conv_w"], "mu_rwkv": i["mu_rwkv"], "w0": i["w0"], "a0": i["a0"],
        "k_k": i["k_k"], "k_a": i["k_a"], "r_k": i["r_k"], "lnx_w": i["lnx_w"], "lnx_b": i["lnx_b"],
        "gate_b": i["gate_b"], "norm_ca": i["norm_ca"], "norm_mem": i["norm_mem"], "norm_ffn": i["norm_ffn"],
        "ffn_conv_w": i["ffn_conv_w"], "ffn_conv_b": i["ffn_conv_b"], "norm_final": i["norm_final"],
        "g_attn_2": i["g_attn_2"], "g_mlp_2": i["g_mlp_2"], "g_final_2": i["g_final_2"],
        "pe_k": i["cmp_pe_k_2"], "pe_v": i["cmp_pe_v_2"],
    }
    cols = {name: _columns(np.asarray(v)) for name, v in vec.items()}
    cols["b_forget"] = np.broadcast_to(f("b_forget_2"), (P, 8))
    a["vec"] = np.concatenate([cols[name] for name, _ in VECS], axis=1)
    a["const"] = _constants()
    a["bucket"] = _bucket_rows()
    a["head_row"] = np.repeat(np.eye(HEADS, dtype=np.float32), P, axis=1)
    return {name: np.ascontiguousarray(v) for name, v in a.items()}


def kernel(**inputs):
    import concourse.bacc as bacc
    from concourse.bass_utils import run_bass_kernel_spmd

    arrays = _layout(inputs)
    nc = bacc.Bacc("TRN2", target_bir_lowering=False, num_devices=1)
    dram = {n: nc.dram_tensor(n, a.shape, mybir.dt.from_np(a.dtype), kind="ExternalInput").ap() for n, a in arrays.items()}
    dram["out"] = nc.dram_tensor("out", (P, KD, T), F32, kind="ExternalOutput").ap()
    hybrid_decoder_kernel(nc, dram, STAGES)
    r = run_bass_kernel_spmd(nc, [arrays], core_ids=[0])
    return r.results[0]["out"].transpose(1, 0, 2).reshape(1, D, T).transpose(0, 2, 1)
```
